# Optimizing a Trainium2 kernel written in Bass

```python
import math
import jax
import jax.numpy as jnp
from jax import lax
import numpy as np

D_MODEL = 1024
BATCH = 1
SEQ = 256
DEPTH = 1

HEAD_DIM = 64
Q_BLOCK = 128
N_BRANCH = 4
BRANCH_WIDTH = 256

MOBA_HEADS = 4
MOBA_BLOCK = 256
MOBA_TOPK = 3

DIFF_HEADS = 4
DIFF_QK_DIM = 32
DIFF_V_DIM = 2 * DIFF_QK_DIM

SB_HEADS = 4

SWA_Q_HEADS = 4
SWA_KV_HEADS = 2
SWA_WINDOW = 128

REL_BUCKETS = 32
REL_MAX_DIST = 128
N_BIAS_HEADS = MOBA_HEADS + DIFF_HEADS + SWA_Q_HEADS

N_GROUPS = 4
EXPERTS_PER_GROUP = 8
N_EXPERTS = N_GROUPS * EXPERTS_PER_GROUP
EXPERT_TOPK = 2
D_EXPERT = 512
MOE_BLOCK = 128

NORM_EPS = 1e-6

MOBA_COLS = 3 * MOBA_HEADS * HEAD_DIM
DIFF_COLS = DIFF_HEADS * (4 * DIFF_QK_DIM + DIFF_V_DIM)
SB_COLS = 3 * SB_HEADS * HEAD_DIM
SWA_COLS = (SWA_Q_HEADS + 2 * SWA_KV_HEADS) * HEAD_DIM
IN_COLS = MOBA_COLS + DIFF_COLS + SB_COLS + SWA_COLS

kernel_name = "hybrid_gated_moba_diff_stickbreak_swa_hmoe"

def rmsnorm(x, g):
    x32 = x.astype(jnp.float32)
    y = x32 * lax.rsqrt(jnp.mean(x32 * x32, axis=-1, keepdims=True) + NORM_EPS)
    return (y * g.astype(jnp.float32)).astype(x.dtype)

def rel_bucket(dist):
    n = jnp.maximum(dist, 0)
    max_exact = REL_BUCKETS // 2
    nf = jnp.maximum(n, 1).astype(jnp.float32)
    large = max_exact + (jnp.log(nf / max_exact) / math.log(REL_MAX_DIST / max_exact)
                         * (REL_BUCKETS - max_exact)).astype(jnp.int32)
    large = jnp.minimum(large, REL_BUCKETS - 1)
    return jnp.where(n < max_exact, n, large)

def head_bias(tab, dist):
    return jnp.take(tab, rel_bucket(dist), axis=1).astype(jnp.float32)

def moba_attention(q, k, v, tab):
    B, S, H, d = q.shape
    nb = -(-S // MOBA_BLOCK)
    pad = nb * MOBA_BLOCK - S
    q = q.transpose(0, 2, 1, 3)
    k = jnp.pad(k.transpose(0, 2, 1, 3), ((0, 0), (0, 0), (0, pad), (0, 0)))
    v = jnp.pad(v.transpose(0, 2, 1, 3), ((0, 0), (0, 0), (0, pad), (0, 0)))
    kblk = k.reshape(B, H, nb, MOBA_BLOCK, d)
    vblk = v.reshape(B, H, nb, MOBA_BLOCK, d)
    kmean = jnp.mean(kblk.astype(jnp.float32), axis=3).astype(k.dtype)
    topk = min(MOBA_TOPK, nb)
    scale = d ** -0.5
    bi = jnp.arange(B)[:, None, None, None]
    hi = jnp.arange(H)[None, :, None, None]
    in_blk = jnp.arange(MOBA_BLOCK)

    def chunk(c):
        t0 = c * Q_BLOCK
        qc = lax.dynamic_slice_in_dim(q, t0, Q_BLOCK, axis=2)
        tpos = t0 + jnp.arange(Q_BLOCK)
        own = t0 // MOBA_BLOCK
        gate = jnp.einsum('bhqd,bhnd->bhqn', qc, kmean).astype(jnp.float32)
        gate = jnp.where(jnp.arange(nb) < own, gate, -jnp.inf)
        gval, gidx = lax.top_k(gate, topk)
        ks = kblk[bi, hi, gidx]
        vs = vblk[bi, hi, gidx]
        s_sel = jnp.einsum('bhqd,bhqjkd->bhqjk', qc, ks).astype(jnp.float32) * scale
        kpos = gidx[..., None] * MOBA_BLOCK + in_blk
        s_sel = s_sel + tab[hi[..., None], rel_bucket(tpos[:, None, None] - kpos)].astype(jnp.float32)
        s_sel = jnp.where(jnp.isfinite(gval)[..., None], s_sel, -jnp.inf)
        ko = lax.dynamic_slice_in_dim(k, own * MOBA_BLOCK, MOBA_BLOCK, axis=2)
        vo = lax.dynamic_slice_in_dim(v, own * MOBA_BLOCK, MOBA_BLOCK, axis=2)
        dist = tpos[:, None] - (own * MOBA_BLOCK + in_blk)[None, :]
        s_own = jnp.einsum('bhqd,bhkd->bhqk', qc, ko).astype(jnp.float32) * scale + head_bias(tab, dist)[None]
        s_own = jnp.where(dist >= 0, s_own, -jnp.inf)
        logits = jnp.concatenate([s_sel.reshape(B, H, Q_BLOCK, topk * MOBA_BLOCK), s_own], axis=-1)
        p = jax.nn.softmax(logits, axis=-1).astype(v.dtype)
        p_sel = p[..., :topk * MOBA_BLOCK].reshape(B, H, Q_BLOCK, topk, MOBA_BLOCK)
        p_own = p[..., topk * MOBA_BLOCK:]
        return (jnp.einsum('bhqjk,bhqjkd->bhqd', p_sel, vs)
                + jnp.einsum('bhqk,bhkd->bhqd', p_own, vo))

    out = lax.map(chunk, jnp.arange(S // Q_BLOCK))
    return out.transpose(1, 0, 3, 2, 4).reshape(B, S, H * d)

def diff_attention(q1, q2, k1, k2, v, lam, lam_init, subln_g, tab):
    B, S, H, dq = q1.shape
    dv = v.shape[-1]
    scale = dq ** -0.5
    kpos = jnp.arange(S)

    def chunk(c):
        t0 = c * Q_BLOCK
        dist = (t0 + jnp.arange(Q_BLOCK))[:, None] - kpos[None, :]
        causal = dist >= 0
        bias = head_bias(tab, dist)

        def probs(qa, ka):
            qc = lax.dynamic_slice_in_dim(qa, t0, Q_BLOCK, axis=1)
            s = jnp.einsum('bqhd,bkhd->bhqk', qc, ka).astype(jnp.float32) * scale + bias
            return jax.nn.softmax(jnp.where(causal, s, -jnp.inf), axis=-1)

        a = probs(q1, k1) - lam * probs(q2, k2)
        return jnp.einsum('bhqk,bkhd->bqhd', a.astype(v.dtype), v)

    out = lax.map(chunk, jnp.arange(S // Q_BLOCK))
    out = out.transpose(1, 0, 2, 3, 4).reshape(B, S, H, dv)
    out = rmsnorm(out, subln_g) * (1.0 - lam_init)
    return out.reshape(B, S, H * dv)

def stick_breaking_attention(q, k, v):
    B, S, H, d = q.shape
    scale = d ** -0.5
    kpos = jnp.arange(S)

    def chunk(c):
        t0 = c * Q_BLOCK
        qc = lax.dynamic_slice_in_dim(q, t0, Q_BLOCK, axis=1)
        strict = (t0 + jnp.arange(Q_BLOCK))[:, None] > kpos[None, :]
        z = jnp.einsum('bqhd,bkhd->bhqk', qc, k).astype(jnp.float32) * scale
        log_keep = jnp.where(strict, jax.nn.log_sigmoid(-z), 0.0)
        later = lax.cumsum(log_keep, axis=3, reverse=True) - log_keep
        w = jnp.where(strict, jnp.exp(jax.nn.log_sigmoid(z) + later), 0.0)
        return jnp.einsum('bhqk,bkhd->bqhd', w.astype(v.dtype), v)

    out = lax.map(chunk, jnp.arange(S // Q_BLOCK))
    return out.transpose(1, 0, 2, 3, 4).reshape(B, S, H * d)

def sliding_window_attention(q, k, v, sinks, tab):
    B, S, Hq, d = q.shape
    Hkv = k.shape[2]
    G = Hq // Hkv
    nb = S // Q_BLOCK
    qb = q.reshape(B, nb, Q_BLOCK, Hkv, G, d)

    def band(t):
        tb = t.reshape(B, nb, Q_BLOCK, Hkv, d)
        prev = jnp.pad(tb[:, :-1], ((0, 0), (1, 0), (0, 0), (0, 0), (0, 0)))
        return jnp.concatenate([prev, tb], axis=2)

    kb, vb = band(k), band(v)
    s = jnp.einsum('bnqkgd,bnskd->bnkgqs', qb, kb).astype(jnp.float32) * d ** -0.5
    qi = jnp.arange(Q_BLOCK)[:, None]
    sj = jnp.arange(2 * Q_BLOCK)[None, :]
    dist = qi + Q_BLOCK - sj
    in_win = (dist >= 0) & (dist < SWA_WINDOW)
    key_abs = jnp.arange(nb)[:, None, None] * Q_BLOCK + sj[None] - Q_BLOCK
    valid = in_win[None] & (key_abs >= 0)
    s = s + head_bias(tab, dist).reshape(Hkv, G, Q_BLOCK, 2 * Q_BLOCK)[None, None]
    s = jnp.where(valid[None, :, None, None], s, -jnp.inf)
    sink = sinks.astype(jnp.float32).reshape(1, 1, Hkv, G, 1, 1)
    m = jnp.maximum(jnp.max(s, axis=-1, keepdims=True), sink)
    e = jnp.exp(s - m)
    p = e / (jnp.sum(e, axis=-1, keepdims=True) + jnp.exp(sink - m))
    o = jnp.einsum('bnkgqs,bnskd->bnqkgd', p.astype(v.dtype), vb)
    return o.reshape(B, S, Hq * d)

def hierarchical_moe(h, w_rg, b_rg, w_re, b_re, w1, w3, w2):
    B, S, D = h.shape
    xf = h.reshape(-1, D)
    N = xf.shape[0]
    g_logits = (xf @ w_rg).astype(jnp.float32) + b_rg.astype(jnp.float32)
    g_prob = jax.nn.softmax(g_logits, axis=-1)
    grp = jnp.argmax(g_logits, axis=-1)
    p_grp = jnp.take_along_axis(g_prob, grp[:, None], axis=1)
    e_logits = ((xf @ w_re).astype(jnp.float32) + b_re.astype(jnp.float32)).reshape(N, N_GROUPS, EXPERTS_PER_GROUP)
    e_logits = jnp.take_along_axis(e_logits, grp[:, None, None], axis=1)[:, 0]
    top_val, top_idx = lax.top_k(e_logits, EXPERT_TOPK)
    gate = p_grp * jax.nn.softmax(top_val, axis=-1)
    expert = grp[:, None] * EXPERTS_PER_GROUP + top_idx

    A = N * EXPERT_TOPK
    eid = expert.reshape(-1)
    order = jnp.argsort(eid)
    eid_s = eid[order]
    tok_s = order // EXPERT_TOPK
    gate_s = gate.reshape(-1)[order]
    counts = jnp.bincount(eid, length=N_EXPERTS)
    padded = (counts + MOE_BLOCK - 1) // MOE_BLOCK * MOE_BLOCK
    pad_end = jnp.cumsum(padded)
    pad_start = pad_end - padded
    start = jnp.cumsum(counts) - counts
    dest = pad_start[eid_s] + jnp.arange(A) - start[eid_s]
    R = ((A + MOE_BLOCK - 1) // MOE_BLOCK + N_EXPERTS) * MOE_BLOCK
    nblk = R // MOE_BLOCK
    xbuf = jnp.zeros((R, D), xf.dtype).at[dest].set(xf[tok_s])
    blk_expert = jnp.minimum(jnp.searchsorted(pad_end, jnp.arange(nblk) * MOE_BLOCK, side='right'), N_EXPERTS - 1)

    def expert_block(args):
        xb, e = args
        return (jax.nn.silu(xb @ w1[e]) * (xb @ w3[e])) @ w2[e]

    ybuf = lax.map(expert_block, (xbuf.reshape(nblk, MOE_BLOCK, D), blk_expert)).reshape(R, D)
    y = ybuf[dest] * gate_s[:, None].astype(ybuf.dtype)
    out = jnp.zeros((N, D), h.dtype).at[tok_s].add(y)
    return out.reshape(B, S, D)

def setup_inputs(seed: int = 0) -> dict:
    key = jax.random.key(seed)
    ks = jax.random.split(key, 24)

    def nrm(k, shape, scale):
        return jax.random.normal(k, shape, jnp.float32) * scale

    return {
        "x": nrm(ks[0], (BATCH, SEQ, D_MODEL), 1.0),
        "rel_bias": nrm(ks[1], (REL_BUCKETS, N_BIAS_HEADS), 0.5),
        "g_mix": 1.0 + nrm(ks[2], (DEPTH, D_MODEL), 0.02),
        "w_in": nrm(ks[3], (DEPTH, D_MODEL, IN_COLS), D_MODEL ** -0.5),
        "diff_lq1": nrm(ks[4], (DEPTH, DIFF_QK_DIM), 0.1),
        "diff_lk1": nrm(ks[5], (DEPTH, DIFF_QK_DIM), 0.1),
        "diff_lq2": nrm(ks[6], (DEPTH, DIFF_QK_DIM), 0.1),
        "diff_lk2": nrm(ks[7], (DEPTH, DIFF_QK_DIM), 0.1),
        "diff_subln": 1.0 + nrm(ks[8], (DEPTH, DIFF_V_DIM), 0.02),
        "swa_sinks": nrm(ks[9], (DEPTH, SWA_Q_HEADS), 1.0),
        "w_gate": nrm(ks[10], (DEPTH, N_BRANCH, D_MODEL, D_MODEL), D_MODEL ** -0.5),
        "w_br": nrm(ks[11], (DEPTH, N_BRANCH, BRANCH_WIDTH, D_MODEL), BRANCH_WIDTH ** -0.5),
        "w_o": nrm(ks[12], (DEPTH, D_MODEL, D_MODEL), D_MODEL ** -0.5),
        "g_ffn": 1.0 + nrm(ks[13], (DEPTH, D_MODEL), 0.02),
        "w_route_group": nrm(ks[14], (DEPTH, D_MODEL, N_GROUPS), D_MODEL ** -0.5),
        "b_route_group": nrm(ks[15], (DEPTH, N_GROUPS), 0.01),
        "w_route_expert": nrm(ks[16], (DEPTH, D_MODEL, N_EXPERTS), D_MODEL ** -0.5),
        "b_route_expert": nrm(ks[17], (DEPTH, N_EXPERTS), 0.01),
        "w1": nrm(ks[18], (DEPTH, N_EXPERTS, D_MODEL, D_EXPERT), D_MODEL ** -0.5),
        "w3": nrm(ks[19], (DEPTH, N_EXPERTS, D_MODEL, D_EXPERT), D_MODEL ** -0.5),
        "w2": nrm(ks[20], (DEPTH, N_EXPERTS, D_EXPERT, D_MODEL), D_EXPERT ** -0.5),
        "g_final": 1.0 + nrm(ks[21], (D_MODEL,), 0.02),
    }

def reference(x, rel_bias, g_mix, w_in, diff_lq1, diff_lk1, diff_lq2, diff_lk2, diff_subln,
              swa_sinks, w_gate, w_br, w_o, g_ffn, w_route_group, b_route_group,
              w_route_expert, b_route_expert, w1, w3, w2, g_final):
    B, S, _ = x.shape
    tab = rel_bias.T
    tab_moba = tab[:MOBA_HEADS]
    tab_diff = tab[MOBA_HEADS:MOBA_HEADS + DIFF_HEADS]
    tab_swa = tab[MOBA_HEADS + DIFF_HEADS:]
    dq = DIFF_HEADS * DIFF_QK_DIM
    for l in range(DEPTH):
        h = rmsnorm(x, g_mix[l])
        proj = h @ w_in[l]
        pa, pb, pc, pd = jnp.split(proj, [MOBA_COLS, MOBA_COLS + DIFF_COLS,
                                          MOBA_COLS + DIFF_COLS + SB_COLS], axis=-1)
        qa, ka, va = [t.reshape(B, S, MOBA_HEADS, HEAD_DIM) for t in jnp.split(pa, 3, axis=-1)]
        o_a = moba_attention(qa, ka, va, tab_moba)
        q1, q2, k1, k2, vb = jnp.split(pb, [dq, 2 * dq, 3 * dq, 4 * dq], axis=-1)
        q1, q2, k1, k2 = [t.reshape(B, S, DIFF_HEADS, DIFF_QK_DIM) for t in (q1, q2, k1, k2)]
        vb = vb.reshape(B, S, DIFF_HEADS, DIFF_V_DIM)
        lam_init = 0.8 - 0.6 * math.exp(-0.3 * l)
        lam = (jnp.exp(jnp.sum(diff_lq1[l].astype(jnp.float32) * diff_lk1[l].astype(jnp.float32)))
               - jnp.exp(jnp.sum(diff_lq2[l].astype(jnp.float32) * diff_lk2[l].astype(jnp.float32)))
               + lam_init)
        o_b = diff_attention(q1, q2, k1, k2, vb, lam, lam_init, diff_subln[l], tab_diff)
        qc, kc, vc = [t.reshape(B, S, SB_HEADS, HEAD_DIM) for t in jnp.split(pc, 3, axis=-1)]
        o_c = stick_breaking_attention(qc, kc, vc)
        qd, kd, vd = jnp.split(pd, [SWA_Q_HEADS * HEAD_DIM, (SWA_Q_HEADS + SWA_KV_HEADS) * HEAD_DIM], axis=-1)
        o_d = sliding_window_attention(qd.reshape(B, S, SWA_Q_HEADS, HEAD_DIM),
                                       kd.reshape(B, S, SWA_KV_HEADS, HEAD_DIM),
                                       vd.reshape(B, S, SWA_KV_HEADS, HEAD_DIM),
                                       swa_sinks[l], tab_swa)
        branches = (o_a, o_b, o_c, o_d)
        merged = jax.nn.sigmoid(h @ w_gate[l, 0]) * (branches[0] @ w_br[l, 0])
        for i in range(1, N_BRANCH):
            merged = merged + jax.nn.sigmoid(h @ w_gate[l, i]) * (branches[i] @ w_br[l, i])
        x = x + merged @ w_o[l]
        x = x + hierarchical_moe(rmsnorm(x, g_ffn[l]), w_route_group[l], b_route_group[l],
                                 w_route_expert[l], b_route_expert[l], w1[l], w3[l], w2[l])
    return rmsnorm(x, g_final)


_drawn_inputs = setup_inputs


def setup_inputs(seed=0):
    import zlib

    import numpy as np

    out = dict(_drawn_inputs(seed))
    spreads = {}
    factors = {'diff_subln': 9.782,
     'swa_sinks': 45.652,
     'b_route_group': 64.0,
     'b_route_expert': 4.767,
     'g_final': 7.523,
     'g_ffn': 3.242}
    for name, (base, spread) in spreads.items():
        noise = np.random.default_rng([zlib.crc32(name.encode()), seed]).standard_normal(out[name].shape)
        drawn = base * np.exp(spread * noise) if base else spread * noise
        out[name] = jnp.asarray(drawn.astype(out[name].dtype))
    for name, factor in factors.items():
        out[name] = (out[name] * factor).astype(out[name].dtype)
    return out
```

```python
from contextlib import ExitStack

import concourse.bass as bass
from concourse import mybir

F32 = mybir.dt.float32
I32 = mybir.dt.int32
ALU = mybir.AluOpType
ACT = mybir.ActivationFunctionType
AX = mybir.AxisListType.X

P = 128
TOK = 256
NT = TOK // P
D = 1024
KD = D // P
HD = 64
EPS = 1e-6
BANK = 512
NEG = 1.0e30

C_ID, C_GE, C_LT, C_ONE, C_SLOT, C_IOTA, C_DIAG = 0, 128, 256, 384, 512, 576, 608
C_EPS, C_UNIT, C_W = 992, 993, 994

CAP = 64
NG, EPG = 4, 8
NE = NG * EPG
DE = 512
CE = DE // P
PAIRS = NE // 2
BLOCKS = TOK // CAP

UNIT = 4096
RING, RING1 = 9, 7
PAIR_UNITS = 6
PEEL = 2
STEP = 3
LOOPS = 4

MAP = 3 * P
TILE_COLS = [(0, P), (P, MAP)]

A_, B_, C_BR, D_ = range(4)
QK = dict(Aq=0, Ak=2, Bq1=4, Bq2=5, Bk1=6, Bk2=7, Cq=8, Ck=10, Dq=12, Dk=14)
V_AT = [0, 256, 512, 768]
LAM_INIT = 0.2


def projection_blocks():
    s64, s32 = HD ** -0.5, 32 ** -0.5
    out = []
    out += [(0, 128 * i, "T", i, (-s64 if i < 2 else 1.0)) for i in range(4)]
    out += [(1, 0, "V", (A_, t), 1.0) for t in range(NT)]
    out += [(1, 256, "T", 4, -s32), (1, 384, "T", 5, -s32)]
    out += [(2, 0, "T", 6, 1.0), (2, 128, "T", 7, 1.0)]
    out += [(2, 256, "V", (B_, t), 1.0) for t in range(NT)]
    out += [(3, 128 * i, "T", 8 + i, (s64 if i < 2 else 1.0)) for i in range(4)]
    out += [(4, 0, "V", (C_BR, t), 1.0) for t in range(NT)]
    out += [(4, 256, "T", 12, -s64), (4, 384, "T", 13, -s64)]
    out += [(5, 0, "K", 14, 1.0), (5, 64, "K", 15, 1.0), (5, 128, "W", None, 1.0)]
    return out


def hybrid_decoder_layer(nc, a, out):
    blocks = projection_blocks()
    ends = [max(i for i, b in enumerate(blocks) if b[0] == u) + 1 for u in range(6)]

    stream = [("in", u, 0) for u in range(6)] + [("gate", 0, 0), ("gate", 0, 1)]
    for b in range(1, 4):
        stream += [("gate", b, 0), ("br", b - 1, 0), ("gate", b, 1)]
    stream += [("br", 3, 0), ("wo", 0, 0), ("wo", 1, 0)]
    slot_uses = [sum(u % RING1 == s for u in range(len(stream))) for s in range(RING)]
    slot_uses[7] = slot_uses[8] = 0
    where = {x: u for u, x in enumerate(stream)}
    FIRST = len(stream) % RING1

    with ExitStack() as ctx:
        at = [16512]

        def place(name, shape, dt=F32, offset=None):
            size = 4
            for n in shape[1:]:
                size *= n
            if offset is None:
                offset = at[0]
                at[0] += (size + 31) // 32 * 32
            return nc.alloc_sbuf_tensor_at(name, list(shape), dt, offset=offset)

        sem = lambda name: ctx.enter_context(nc.semaphore(name))
        bank = [ctx.enter_context(nc.psum_tensor(f"bank{i}", [P, BANK], F32)) for i in range(8)]

        cst = place("cst", [P, C_W])
        x = place("x", [P, NT, D])
        hk = place("hk", [P, NT, KD, P])
        hT = place("hT", [P, KD, TOK])
        merged = hk[:].rearrange("p t k q -> p t (k q)")
        wr = place("wr", [P, KD, NG + NE])
        rbias = place("rbias", [P, NG + NE])
        gmix = place("gmix", [P, KD])
        gffn = place("gffn", [P, KD])
        sub = place("sub", [P, HD])
        sinks = place("sinks", [P, 4])
        nsink = place("nsink", [P, 4])
        lqk = place("lqk", [P, 2, 2, 32])
        lam = place("lam", [P, 8])
        ss = place("ss", [P, 2])
        rs = place("rs", [P, 2])
        nm = place("nm", [P, 2, 2, 2])
        lsum = place("lsum", [P, 2, 2, 2])
        esink = place("esink", [P, 2])
        shared = at[0]
        ring_at = 229344 - RING * UNIT * 4
        units = [place(f"unit{s}", [P, UNIT], offset=ring_at + 4 * UNIT * ((s + 2) % RING)) for s in range(RING)]

        vv = place("vv", [P, NT, 896])
        sig = place("sig", [P, 2, NT, D])
        o = place("o", [P, 2, NT, 256])
        oT = place("oT", [P, 2, TOK])
        pT = place("pT", [P, MAP])
        tmp = place("tmp", [P, BANK])
        assert at[0] <= ring_at, (at[0], ring_at)
        relb = place("relb", [32, 12], offset=shared + 7168)
        onehot = place("onehot", [32, MAP], offset=shared + 7168 + 64)
        bmask = place("bmask", [12, MAP], offset=shared + 7168 + 64 + 1536)
        dvec = place("dvec", [12, MAP], offset=shared + 7168 + 64 + 3072)
        at[0] = ring_at
        qk = place("qk", [P, 16, TOK])
        bias = place("bias", [P, 12, TOK])
        prob = place("prob", [P, 2, MAP])
        assert at[0] <= ring_at + 8 * UNIT

        at[0] = shared
        xT = place("xT", [P, KD, P])
        sg = place("sg", [P, DE])
        hid = place("hid", [P, CE, P])
        hidT = place("hidT", [P, CE, P])
        y = place("y", [P, D])
        pick = place("pick", [P, NT, P])
        pickw = place("pickw", [P, NT, P])
        pickT = place("pickT", [P, NT, P])
        lg = place("lg", [P, NT, NG + NE])
        ge = place("ge", [P, NT, NG])
        eg = place("eg", [P, NT, NG])
        cg = place("cg", [P, NT, NG])
        ohg = place("ohg", [P, NT, NG])
        em = place("em", [P, NT, NE])
        ce = place("ce", [P, NT, NE])
        oh1 = place("oh1", [P, NT, NE])
        oh2 = place("oh2", [P, NT, NE])
        asg = place("asg", [P, NT, NE])
        gate = place("gate", [P, NT, NE])
        slot = place("slot", [P, NT, NE])
        m = place("m", [P, 10, NT])
        most = place("most", [P, 1])
        flag = place("flag", [P, 1], I32)
        gfin = place("gfin", [P, D])
        assert at[0] <= ring_at

        dram_vec = nc.dram_tensor("dram_vec", (12, MAP), F32, kind="Internal").ap()

        ident = cst[:, C_ID:C_ID + P]
        at_or_after = cst[:, C_GE:C_GE + P]
        before = cst[:, C_LT:C_LT + P]
        ones = cst[:, C_ONE:C_ONE + P]
        slot_no = cst[:, C_SLOT:C_SLOT + CAP]
        eps = cst[:, C_EPS:C_EPS + 1]
        unit1 = cst[:, C_UNIT:C_UNIT + 1]

        names = """cst small wr late scratch biasT hk tr1 dvp dvec lamx lame proj projA projD scores sread norm probs
            ptps dd pt gate gexp sig pv oev bsq brms ob oTps oTs br mrg mTps mTA mTD wo h2ps h2T lg_ps eg sums e2 asg
            pos flag fx stored chain_a chain_d rms hk2"""
        s = {n: sem("s_" + n) for n in names.split()}
        s_x = [sem(f"s_rows{t}") for t in range(NT)]
        s_unit = [sem(f"s_unit{i}") for i in range(RING)]

        def moe_sems(tag):
            ns = "P Pw gat xT A B sg hid hTp STp hT ST Y y0 y1 comb".split()
            return {n: sem(f"s_{tag}_{n}") for n in ns}

        main, over = moe_sems("moe"), moe_sems("over")
        s_over_unit = [sem(f"s_over_unit{i}") for i in range(PAIR_UNITS)]
        s_over_slot = sem("s_over_slot")

        def arrived(eng, unit):
            eng.wait_ge(s_unit[unit % RING1], 16 * (unit // RING1 + 1))

        def slot_of(n):
            return (n + FIRST) % RING

        def unit_value(n, i=0):
            k = slot_of(n)
            first = (k - FIRST) % RING
            return i * (16 * PAIR_UNITS * STEP // RING) + 16 * (slot_uses[k] + (n - first) // RING + 1)

        def free_of(n, i=0):
            p, r = divmod(n, PAIR_UNITS)
            p = i * STEP + p
            return ((main["A"], p + 1), (main["B"], p + 1), (main["Y"], 2 * p + 2))[r // 2]

        def expert_source(r, expert):
            w = (a["w1"], a["w3"], a["w2"])[r // 2]
            e = expert + r % 2
            rows = CE if r >= 4 else KD
            return w[0, bass.ds(e, 1)].rearrange("e (p k) n -> p (e k) n", p=P, k=rows)

        def unit_view(k, r):
            return units[k][:].rearrange("p (k n) -> p k n", k=(CE if r >= 4 else KD))

        block = ctx.enter_context(nc.Block())

        @block.sync
        def _(sp):
            for t in range(NT):
                sp.dma_start(x[:, t, :], a["x"][0, t * P:(t + 1) * P, :]).then_inc(s_x[t], 16)
            sp.dma_start(cst[:], a["constants"]).then_inc(s["cst"], 16)
            sp.dma_start(gmix[:], a["g_mix"][0].rearrange("(p k) -> p k", k=KD)).then_inc(s["small"], 16)
            sp.dma_start(relb[:], a["rel_bias"]).then_inc(s["small"], 16)
            sp.dma_start(onehot[:], a["bucket_onehot"]).then_inc(s["small"], 16)
            sp.dma_start(bmask[:], a["bias_mask"]).then_inc(s["small"], 16)
            for i, n in enumerate(("diff_lq1", "diff_lk1", "diff_lq2", "diff_lk2")):
                sp.dma_start(lqk[:, i // 2, i % 2, :], a[n][0].partition_broadcast(P)).then_inc(s["small"], 16)
            sp.dma_start(sub[:], a["diff_subln"][0].partition_broadcast(P)).then_inc(s["small"], 16)
            sp.dma_start(sinks[:], a["swa_sinks"][0].partition_broadcast(P)).then_inc(s["small"], 16)

            def released(u):
                kind, i, n = stream[u]
                if kind == "in":
                    sp.wait_ge(s["proj"], ends[i])
                elif kind == "gate":
                    sp.wait_ge(s["gate"], 4 * i + 2 * n + 2)
                elif kind == "br":
                    sp.wait_ge(s["br"], 4 * i + 4)
                else:
                    sp.wait_ge(s["wo"], 3 + i)

            w_in = a["w_in"][0].rearrange("(p k) n -> p k n", k=KD)
            w_o = a["w_o"][0].rearrange("(p k) n -> p k n", k=KD)
            for u, (kind, i, n) in enumerate(stream):
                if u >= RING1:
                    released(u - RING1)
                dst = units[u % RING1]
                if kind == "in":
                    wide = min(BANK, 2816 - BANK * i)
                    src = w_in[:, :, BANK * i:BANK * i + wide]
                    dst = dst[:].rearrange("p (k n) -> p k n", k=KD)[:, :, 0:wide]
                elif kind == "gate":
                    src = a["w_gate"][0, i].rearrange("(p k) n -> p k n", k=KD)[:, :, BANK * n:BANK * (n + 1)]
                    dst = dst[:].rearrange("p (k n) -> p k n", k=KD)
                elif kind == "br":
                    src = a["w_br"][0, i].rearrange("(c p) n -> p c n", p=P)
                    dst = dst[:, 0:2 * D].rearrange("p (c n) -> p c n", c=2)
                else:
                    src = w_o[:, :, BANK * i:BANK * (i + 1)]
                    dst = dst[:].rearrange("p (k n) -> p k n", k=KD)
                sp.dma_start(dst, src).then_inc(s_unit[u % RING1], 16)

            def load_expert_unit(n, i=0, loop=False):
                if n < RING and not loop:
                    k = slot_of(n)
                    if k < RING1:
                        released(max(u for u in range(len(stream)) if u % RING1 == k))
                    else:
                        sp.wait_ge(s["pv"], 16)
                else:
                    sp.wait_ge(*free_of(n - RING, i))
                p, r = divmod(n, PAIR_UNITS)
                sp.dma_start(unit_view(slot_of(n), r), expert_source(r, (i * STEP + p) * 2)).then_inc(s_unit[slot_of(n)], 16)

            head = 2 * PAIR_UNITS
            for n in range(head):
                load_expert_unit(n)
            span = STEP * PAIR_UNITS
            with sp.Fori(0, LOOPS) as i:
                for n in range(head, head + span):
                    load_expert_unit(n, i, loop=True)
            for n in range(head + LOOPS * span, PAIRS * PAIR_UNITS):
                load_expert_unit(n)

            sp.wait_ge(s["flag"], 1)
            crowded = sp.value_load(flag[0:1, 0:1])
            with sp.If(crowded > CAP):
                sp.wait_ge(main["Y"], 2 * PAIRS)
                with sp.Fori(0, BLOCKS - 1) as b:
                    with sp.Fori(0, PAIRS) as p:
                        sp.wait_ge(over["comb"], b * PAIRS + p + 1)
                        for r in range(PAIR_UNITS):
                            sp.dma_start(unit_view(r, r), expert_source(r, p * 2)).then_inc(s_over_unit[r], 16)
                sp.wait_ge(over["comb"], (BLOCKS - 1) * PAIRS + 1)

            sp.wait_ge(main["comb"], PAIRS)
            for t in range(NT):
                sp.wait_ge(s["fx"], t + 1)
                sp.dma_start(out[0, t * P:(t + 1) * P, :], x[:, t, :]).then_inc(s["stored"], 16)
            sp.wait_ge(s["stored"], 16 * NT)

        @block.gpsimd
        def _(pool):
            pool.wait_ge(s["dvec"], 1)
            pool.dma_start(dram_vec, dvec[:]).then_inc(s["scratch"], 16)
            pool.wait_ge(s["scratch"], 16)
            pool.dma_start(bias[:], bass.AP(dram_vec.tensor, 0, [[1, P], [MAP, 12], [1, TOK]])).then_inc(s["biasT"], 16)
            pool.wait_ge(s["hk2"], NT)
            pool.dma_start(gfin[:], a["g_final"].partition_broadcast(P)).then_inc(s["late"], 16)

        @block.scalar
        def _(act):
            chain = [0]

            def link(ins):
                chain[0] += 1
                ins.then_inc(s["chain_a"], 1)
                act.wait_ge(s["chain_a"], chain[0])

            act.dma_start(gffn[:], a["g_ffn"][0].rearrange("(p k) -> p k", k=KD)).then_inc(s["wr"], 16)
            act.dma_start(wr[:, :, 0:NG], a["w_route_group"][0].rearrange("(p k) n -> p k n", k=KD)).then_inc(s["wr"], 16)
            act.dma_start(wr[:, :, NG:], a["w_route_expert"][0].rearrange("(p k) n -> p k n", k=KD)).then_inc(s["wr"], 16)
            act.dma_start(rbias[:, 0:NG], a["b_route_group"][0].partition_broadcast(P)).then_inc(s["wr"], 16)
            act.dma_start(rbias[:, NG:], a["b_route_expert"][0].partition_broadcast(P)).then_inc(s["wr"], 16)

            def root(n, src, scale, dst, done):
                act.wait_ge(s["sums"], n)
                nc.scalar.activation(dst, src, ACT.Sqrt, bias=eps, scale=scale).then_inc(done, 1)

            act.wait_ge(s["cst"], 16)
            for t in range(NT):
                root(t + 1, ss[:, t:t + 1], 1.0 / D, rs[:, t:t + 1], s["rms"])
            act.wait_ge(s["lamx"], 1)
            nc.scalar.activation(lam[:, 2:4], lam[:, 0:2], ACT.Exp).then_inc(s["lame"], 1)

            def block_out(i):
                unit, col, kind, to, scale = blocks[i]
                src = bank[i % 8][:, 0:TOK]
                if kind in "TK":
                    return qk[:, to, :], src, scale
                if kind == "V":
                    return vv[:, to[1], V_AT[to[0]]:V_AT[to[0]] + 256], src, scale
                return vv[:, :, V_AT[3]:V_AT[3] + P], src.rearrange("p (t n) -> p t n", t=NT), scale

            for i in range(0, len(blocks), 2):
                act.wait_ge(s["proj"], i + 1)
                dst, src, scale = block_out(i)
                nc.scalar.activation(dst, src, ACT.Copy, scale=scale).then_inc(s["projA"], 1)

            for st in range(16):
                b, h = divmod(st, 4)
                par = st % 2
                if b in (A_, D_):
                    if b == A_:
                        act.wait_ge(s["sread"], st + 1)
                    else:
                        act.wait_ge(s["norm"], h + 1)
                    if b == D_:
                        for t in range(NT):
                            nc.scalar.activation(esink[:, t:t + 1], sinks[:, h:h + 1], ACT.Exp,
                                                 bias=nm[:, par, 0, t:t + 1])
                    for t, (c0, c1) in enumerate(TILE_COLS):
                        last = nc.scalar.activation(prob[:, 0, c0:c1], prob[:, 0, c0:c1], ACT.Exp, scale=-1.0,
                                                    bias=nm[:, par, 0, t:t + 1], accum_out=lsum[:, par, 0, t:t + 1])
                    last.then_inc(s["probs"], 1)
                elif b == B_:
                    act.wait_ge(s["sread"], st + 1)
                    for mp in range(2):
                        for t, (c0, c1) in enumerate(TILE_COLS):
                            last = nc.scalar.activation(prob[:, mp, c0:c1], prob[:, mp, c0:c1], ACT.Exp, scale=-1.0,
                                                        bias=nm[:, par, mp, t:t + 1],
                                                        accum_out=lsum[:, par, mp, t:t + 1])
                    last.then_inc(s["dvp"], 1)
                else:
                    act.wait_ge(s["sread"], st + 1)
                    act.wait_ge(s["ptps"], st)
                    link(nc.scalar.activation(prob[:, 1, :], prob[:, 0, :], ACT.Abs))
                    link(nc.scalar.activation(prob[:, 1, :], prob[:, 1, :], ACT.Exp, scale=-1.0))
                    nc.scalar.activation(prob[:, 1, :], prob[:, 1, :], ACT.Ln, bias=unit1).then_inc(s["dvp"], 1)
                if st >= 1:
                    act.wait_ge(s["pv"], st)
                if b == C_BR:
                    act.wait_ge(s["dd"], h + 1)
                    nc.scalar.activation(pT[:], prob[:, 0, :], ACT.Exp).then_inc(s["pt"], 1)
                else:
                    act.wait_ge(s["ptps"], st + 1)
                    nc.scalar.activation(pT[:], bank[2][:, 0:MAP], ACT.Copy).then_inc(s["pt"], 1)
                n, t = divmod(h, 2)
                act.wait_ge(s["gate"], st + 1)
                if b >= 2:
                    act.wait_ge(s["mrg"], 4 * (b - 1))
                nc.scalar.activation(sig[:, b % 2, t, n * BANK:(n + 1) * BANK], bank[4 + par][:], ACT.Exp,
                                     scale=-1.0).then_inc(s["gexp"], 1)
                if h == 3 and b == B_:
                    act.wait_ge(s["bsq"], 1)
                    nc.scalar.activation(lsum[:].rearrange("p a b t -> p (a b t)"), lsum[:].rearrange("p a b t -> p (a b t)"),
                                         ACT.Sqrt, bias=eps, scale=1.0 / HD).then_inc(s["brms"], 1)

            for j in range(0, 4, 2):
                act.wait_ge(s["mTps"], j + 1)
                nc.scalar.activation(hT[:, 2 * j:2 * j + 2, :].rearrange("p k t -> p (k t)"), bank[j][:],
                                     ACT.Copy).then_inc(s["mTA"], 1)
            for t in range(NT):
                root(NT + t + 1, ss[:, t:t + 1], 1.0 / D, rs[:, t:t + 1], s["rms"])
            act.wait_ge(s["eg"], 1)
            nc.scalar.activation(eg[:], ge[:], ACT.Exp).then_inc(s["e2"], 1)
            act.wait_ge(s["eg"], 2)
            nc.scalar.activation(m[:, 6, :], m[:, 5, :], ACT.Exp).then_inc(s["e2"], 1)

            def experts(z, p, first=False):
                act.wait_ge(z["A"], p + 1)
                if not first:
                    act.wait_ge(z["hid"], p)
                nc.scalar.activation(sg[:], bank[4][:], ACT.Silu).then_inc(z["sg"], 1)
                act.wait_ge(z["hTp"], p + 1)
                if not first:
                    act.wait_ge(z["Y"], 2 * p)
                nc.scalar.activation(hidT[:].rearrange("p c q -> p (c q)"), bank[4][:], ACT.Copy).then_inc(z["hT"], 1)
                act.wait_ge(z["Y"], 2 * p + 1)
                if not first:
                    act.wait_ge(z["comb"], p)
                nc.scalar.activation(y[:, 0:BANK], bank[6][:], ACT.Copy).then_inc(z["y0"], 1)

            experts(main, 0, first=True)
            experts(main, 1)
            with act.Fori(0, LOOPS) as i:
                for j in range(STEP):
                    experts(main, i * STEP + PEEL + j)
            for p in range(PEEL + LOOPS * STEP, PAIRS):
                experts(main, p)

            act.wait_ge(s["flag"], 1)
            crowded = act.value_load(flag[0:1, 0:1])
            with act.If(crowded > CAP):
                with act.Fori(0, BLOCKS - 1) as b:
                    with act.Fori(0, PAIRS) as p:
                        q = b * PAIRS + p
                        act.wait_ge(over["comb"], q + 1)
                        experts(over, q, first=True)
                act.wait_ge(over["comb"], (BLOCKS - 1) * PAIRS + 1)
            for t in range(NT):
                root(2 * NT + t + 1, ss[:, t:t + 1], 1.0 / D, rs[:, t:t + 1], s["rms"])

        @block.vector
        def _(dve):
            chain = [0]

            def link(ins):
                chain[0] += 1
                ins.then_inc(s["chain_d"], 1)
                dve.wait_ge(s["chain_d"], chain[0])

            def squares(t, junk):
                nc.vector.tensor_tensor_reduce(out=junk, in0=x[:, t, :], in1=x[:, t, :], scale=1.0, scalar=0.0,
                                               op0=ALU.mult, op1=ALU.add, accum_out=ss[:, t:t + 1]).then_inc(s["sums"], 1)

            def normalise(t, n, done):
                dve.wait_ge(s["rms"], n)
                link(nc.vector.reciprocal(rs[:, t:t + 1], rs[:, t:t + 1]))
                nc.vector.tensor_scalar(hk[:, t, :, :], x[:, t, :].rearrange("p (q k) -> p k q", k=KD),
                                        rs[:, t:t + 1], None, ALU.mult).then_inc(done, 1)

            def scaled(dst, src, g, done):
                nc.vector.tensor_tensor(dst, src, g.unsqueeze(2).broadcast_to([P, 2, TOK]), ALU.mult).then_inc(done, 1)

            for t in range(NT):
                dve.wait_ge(s_x[t], 16)
                squares(t, hk[:, t].rearrange("p k q -> p (k q)"))
            for t in range(NT):
                normalise(t, t + 1, s["hk"])

            dve.wait_ge(s["small"], 16 * 10)
            dve.wait_ge(s["tr1"], 1)
            nc.vector.tensor_tensor(dvec[:], bank[7][0:12, 0:MAP], bmask[:], ALU.add).then_inc(s["dvec"], 1)
            for j in range(4):
                dve.wait_ge(s["tr1"], j + 2)
                scaled(hT[:, 2 * j:2 * j + 2, :], bank[j][:].rearrange("p (k t) -> p k t", k=2),
                       gmix[:, 2 * j:2 * j + 2], s["hk"])
            link(nc.vector.tensor_tensor(lqk[:, :, 0, :], lqk[:, :, 0, :], lqk[:, :, 1, :], ALU.mult))
            nc.vector.tensor_reduce(lam[:, 0:2], lqk[:, :, 0, :], AX, ALU.add).then_inc(s["lamx"], 1)
            link(nc.vector.tensor_scalar(sub[:], sub[:], 1.0 - LAM_INIT, None, ALU.mult))
            link(nc.vector.tensor_scalar(nsink[:], sinks[:], -1.0, None, ALU.mult))
            dve.wait_ge(s["lame"], 1)
            link(nc.vector.tensor_tensor(lam[:, 4:5], lam[:, 3:4], lam[:, 2:3], ALU.subtract))
            link(nc.vector.tensor_scalar(lam[:, 5:6], lam[:, 4:5], -LAM_INIT, None, ALU.add))
            neg_lam = lam[:, 5:6]

            def block_out(i):
                unit, col, kind, to, scale = blocks[i]
                src = bank[i % 8][:, 0:TOK]
                if kind in "TK":
                    return qk[:, to, :], src, scale
                if kind == "V":
                    return vv[:, to[1], V_AT[to[0]]:V_AT[to[0]] + 256], src, scale
                return vv[:, :, V_AT[3]:V_AT[3] + P], src.rearrange("p (t n) -> p t n", t=NT), scale

            for i in range(1, len(blocks), 2):
                dve.wait_ge(s["proj"], i + 1)
                dst, src, scale = block_out(i)
                nc.vector.tensor_scalar(dst, src, scale, None, ALU.mult).then_inc(s["projD"], 1)

            dve.wait_ge(s["biasT"], 16)

            def biased(par, mp, src, table):
                for t, (c0, c1) in enumerate(TILE_COLS):
                    keys = bias[:, table, 127::-1] if t == 0 else bias[:, table, 255::-1]
                    last = nc.vector.tensor_tensor_reduce(out=prob[:, mp, c0:c1], in0=src[:, c0:c1], in1=keys,
                                                          scale=1.0, scalar=4.0 * NEG, op0=ALU.add, op1=ALU.min,
                                                          accum_out=nm[:, par, mp, t:t + 1])
                return last

            def transposed_out(b):
                dve.wait_ge(s["oTps"], b + 1)
                if b >= 1:
                    dve.wait_ge(s["br"], 4 * b)
                nc.vector.tensor_copy(oT[:].rearrange("p c t -> p (c t)"), bank[7][:]).then_inc(s["oTs"], 1)

            def merge(b, j):
                t, n = divmod(j, 2)
                dve.wait_ge(s["br"], 4 * b + j + 1)
                dve.wait_ge(s["sig"], 4 * b + 4)
                cols = slice(n * BANK, (n + 1) * BANK)
                if b == 0:
                    nc.vector.tensor_tensor(merged[:, t, cols], bank[6 + j % 2][:], sig[:, b % 2, t, cols],
                                            ALU.mult).then_inc(s["mrg"], 1)
                else:
                    dve.wait_ge(s["mrg"], 4 * b + j)
                    link(nc.vector.tensor_tensor(tmp[:], bank[6 + j % 2][:], sig[:, b % 2, t, cols], ALU.mult))
                    nc.vector.tensor_tensor(merged[:, t, cols], merged[:, t, cols], tmp[:], ALU.add).then_inc(s["mrg"], 1)

            for st in range(16):
                b, h = divmod(st, 4)
                par = st % 2
                dve.wait_ge(s["scores"], st + 1)
                if st >= 1:
                    dve.wait_ge(s["pt"], st)
                if b in (A_, D_):
                    table = h if b == A_ else 8 + h
                    biased(par, 0, bank[par], table).then_inc(s["sread"], 1)
                    if b == D_:
                        dve.wait_ge(s["sread"], st + 1)
                        nc.vector.tensor_scalar(nm[:, par, 0, :], nm[:, par, 0, :], nsink[:, h:h + 1], None,
                                                ALU.min).then_inc(s["norm"], 1)
                elif b == B_:
                    biased(par, 0, bank[0], 4 + h)
                    biased(par, 1, bank[1], 4 + h).then_inc(s["sread"], 1)
                    dve.wait_ge(s["dvp"], h + 1)
                    link(nc.vector.reciprocal(lsum[:, par, :, :], lsum[:, par, :, :]))
                    link(nc.vector.tensor_scalar(lsum[:, par, 1, :], lsum[:, par, 1, :], neg_lam, None, ALU.mult))
                    for t, (c0, c1) in enumerate(TILE_COLS):
                        link(nc.vector.tensor_scalar(prob[:, 1, c0:c1], prob[:, 1, c0:c1], lsum[:, par, 1, t:t + 1],
                                                     None, ALU.mult))
                    for t, (c0, c1) in enumerate(TILE_COLS):
                        last = nc.vector.scalar_tensor_tensor(out=prob[:, 0, c0:c1], in0=prob[:, 0, c0:c1],
                                                              scalar=lsum[:, par, 0, t:t + 1], in1=prob[:, 1, c0:c1],
                                                              op0=ALU.mult, op1=ALU.add)
                    last.then_inc(s["probs"], 1)
                else:
                    nc.vector.tensor_tensor(prob[:, 0, :], bank[par][:, 0:MAP], cst[:, C_DIAG:C_DIAG + MAP],
                                            ALU.add).then_inc(s["sread"], 1)
                    dve.wait_ge(s["dvp"], 4 + h + 1)
                    nc.vector.scalar_tensor_tensor(out=prob[:, 1, :], in0=prob[:, 0, :], scalar=0.0,
                                                   in1=prob[:, 1, :], op0=ALU.max, op1=ALU.add).then_inc(s["probs"], 1)
                    dve.wait_ge(s["ptps"], st + 1)
                    nc.vector.tensor_tensor(prob[:, 0, :], prob[:, 0, :], bank[2][:, 0:MAP],
                                            ALU.subtract).then_inc(s["dd"], 1)
                n, t = divmod(h, 2)
                chunk = sig[:, b % 2, t, n * BANK:(n + 1) * BANK]
                dve.wait_ge(s["gexp"], st + 1)
                link(nc.vector.tensor_scalar(chunk, chunk, 1.0, None, ALU.add))
                nc.vector.reciprocal(chunk, chunk).then_inc(s["sig"], 1)
                if b in (A_, D_):
                    dve.wait_ge(s["probs"], st + 1)
                    if b == D_:
                        link(nc.vector.tensor_tensor(lsum[:, par, 0, :], lsum[:, par, 0, :], esink[:], ALU.add))
                    link(nc.vector.reciprocal(lsum[:, par, 0, :], lsum[:, par, 0, :]))
                    dve.wait_ge(s["pv"], st + 1)
                    for t in range(NT):
                        last = nc.vector.tensor_scalar(o[:, b % 2, t, h * HD:(h + 1) * HD],
                                                       bank[3][:, t * HD:(t + 1) * HD], lsum[:, par, 0, t:t + 1],
                                                       None, ALU.mult)
                else:
                    dve.wait_ge(s["pv"], st + 1)
                    last = nc.vector.tensor_copy(o[:, b % 2, :, h * HD:(h + 1) * HD],
                                                 bank[3][:, 0:P].rearrange("p (t d) -> p t d", t=NT))
                last.then_inc(s["oev"], 1)
                if b == B_ and h == 3:
                    heads = o[:, B_ % 2].rearrange("p t (h d) -> p (t h) d", d=HD)
                    dve.wait_ge(s["oev"], st + 1)
                    sq = tmp[:].rearrange("p (g d) -> p g d", d=HD)
                    rms = lsum[:].rearrange("p a b t -> p (a b t)")
                    link(nc.vector.tensor_tensor(sq, heads, heads, ALU.mult))
                    nc.vector.tensor_reduce(rms, sq, AX, ALU.add).then_inc(s["bsq"], 1)
                    dve.wait_ge(s["brms"], 1)
                    link(nc.vector.reciprocal(rms, rms))
                    link(nc.vector.tensor_tensor(heads, heads, rms.unsqueeze(2).broadcast_to([P, 8, HD]), ALU.mult))
                    nc.vector.tensor_tensor(heads, heads, sub[:].unsqueeze(1).broadcast_to([P, 8, HD]),
                                            ALU.mult).then_inc(s["ob"], 1)
                if b >= 1 and h == 0:
                    transposed_out(b - 1)
                if b >= 1 and h in (1, 2):
                    for j in (2 * h - 2, 2 * h - 1):
                        merge(b - 1, j)
            transposed_out(3)
            for j in range(4):
                merge(3, j)

            for j in range(1, 4, 2):
                dve.wait_ge(s["mTps"], j + 1)
                nc.vector.tensor_copy(hT[:, 2 * j:2 * j + 2, :].rearrange("p k t -> p (k t)"),
                                      bank[j][:]).then_inc(s["mTD"], 1)
            for t in range(NT):
                for n in range(2):
                    dve.wait_ge(s["wo"], 2 * t + n + 1)
                    cols = slice(n * BANK, (n + 1) * BANK)
                    link(nc.vector.tensor_tensor(x[:, t, cols], x[:, t, cols], bank[4 + 2 * t + n][:], ALU.add))
                squares(t, hk[:, t].rearrange("p k q -> p (k q)"))
            for t in range(NT):
                normalise(t, NT + t + 1, s["hk2"])
            dve.wait_ge(s["wr"], 16 * 5)
            for j in range(4):
                dve.wait_ge(s["h2ps"], j + 1)
                scaled(hT[:, 2 * j:2 * j + 2, :], bank[j][:].rearrange("p (k t) -> p k t", k=2),
                       gffn[:, 2 * j:2 * j + 2], s["h2T"])

            V = nc.vector
            t4 = lambda ap: ap.unsqueeze(2).broadcast_to([P, NT, NG])
            t32 = lambda ap: ap.unsqueeze(2).broadcast_to([P, NT, NE])
            iota = lambda n: cst[:, C_IOTA:C_IOTA + n].unsqueeze(1).broadcast_to([P, NT, n])
            dve.wait_ge(s["lg_ps"], 1)
            link(V.tensor_tensor(lg[:], bank[4][:, 0:NT * (NG + NE)].rearrange("p (t n) -> p t n", t=NT),
                                 rbias[:].unsqueeze(1).broadcast_to([P, NT, NG + NE]), ALU.add))
            link(V.tensor_reduce(m[:, 0, :], lg[:, :, 0:NG], AX, ALU.max))
            V.tensor_tensor(ge[:], lg[:, :, 0:NG], t4(m[:, 0, :]), ALU.subtract).then_inc(s["eg"], 1)
            dve.wait_ge(s["eg"], 1)
            link(V.tensor_scalar(cg[:], ge[:], 0.0, -float(NE), ALU.is_equal, ALU.mult))
            link(V.tensor_tensor(cg[:], cg[:], iota(NG), ALU.add))
            link(V.tensor_reduce(m[:, 1, :], cg[:], AX, ALU.min))
            link(V.tensor_tensor(ohg[:], cg[:], t4(m[:, 1, :]), ALU.is_equal))
            dve.wait_ge(s["e2"], 1)
            link(V.tensor_reduce(m[:, 2, :], eg[:], AX, ALU.add))
            link(V.reciprocal(m[:, 2, :], m[:, 2, :]))
            link(V.tensor_scalar(ohg[:], ohg[:], -1.0, NEG, ALU.add, ALU.mult))
            for t in range(NT):
                link(V.tensor_tensor(em[:, t, :].rearrange("p (g e) -> p g e", g=NG),
                                     lg[:, t, NG:].rearrange("p (g e) -> p g e", g=NG),
                                     ohg[:, t, :].unsqueeze(2).broadcast_to([P, NG, EPG]), ALU.add))
            for k, oh in ((3, oh1), (4, oh2)):
                link(V.tensor_reduce(m[:, k, :], em[:], AX, ALU.max))
                link(V.tensor_tensor(ce[:], em[:], t32(m[:, k, :]), ALU.is_equal))
                link(V.scalar_tensor_tensor(out=ce[:], in0=ce[:], scalar=-float(NE), in1=iota(NE),
                                            op0=ALU.mult, op1=ALU.add))
                link(V.tensor_reduce(m[:, 7, :], ce[:], AX, ALU.min))
                link(V.tensor_tensor(oh[:], ce[:], t32(m[:, 7, :]), ALU.is_equal))
                if k == 3:
                    link(V.scalar_tensor_tensor(out=em[:], in0=oh[:], scalar=-NEG, in1=em[:],
                                                op0=ALU.mult, op1=ALU.add))
            V.tensor_tensor(asg[:], oh1[:], oh2[:], ALU.add).then_inc(s["asg"], 1)
            V.tensor_tensor(m[:, 5, :], m[:, 4, :], m[:, 3, :], ALU.subtract).then_inc(s["eg"], 1)
            dve.wait_ge(s["e2"], 2)
            link(V.tensor_scalar(m[:, 7, :], m[:, 6, :], 1.0, None, ALU.add))
            link(V.reciprocal(m[:, 7, :], m[:, 7, :]))
            link(V.tensor_tensor(m[:, 8, :], m[:, 7, :], m[:, 2, :], ALU.mult))
            link(V.tensor_tensor(m[:, 9, :], m[:, 8, :], m[:, 6, :], ALU.mult))
            link(V.tensor_tensor(gate[:], oh1[:], t32(m[:, 8, :]), ALU.mult))
            link(V.tensor_tensor(ce[:], oh2[:], t32(m[:, 9, :]), ALU.mult))
            link(V.tensor_tensor(gate[:], gate[:], ce[:], ALU.add))
            dve.wait_ge(s["pos"], 1)
            link(V.scalar_tensor_tensor(out=slot[:], in0=bank[5][:, 0:NT * NE].rearrange("p (t e) -> p t e", t=NT),
                                        scalar=1.0, in1=asg[:], op0=ALU.add, op1=ALU.mult))
            link(V.tensor_scalar(slot[:], slot[:], -1.0, None, ALU.add))
            link(V.tensor_reduce(most[:], bank[5][:, NT * NE:(NT + 1) * NE], AX, ALU.max))
            V.tensor_copy(flag[:], most[:]).then_inc(s["flag"], 1)

            def picks(z, p, pair, first=False):
                if not first:
                    dve.wait_ge(z["gat"], 2 * p)
                    dve.wait_ge(z["Pw"], p)
                V.tensor_tensor(pick[:].rearrange("p t (g s) -> p t g s", g=2),
                                slot[:, :, bass.ds(2 * pair, 2)].unsqueeze(3).broadcast_to([P, NT, 2, CAP]),
                                slot_no.unsqueeze(1).unsqueeze(1).broadcast_to([P, NT, 2, CAP]),
                                ALU.is_equal).then_inc(z["P"], 1)

            def weighted(z, p, pair, first=False):
                dve.wait_ge(z["P"], p + 1)
                if not first:
                    dve.wait_ge(z["STp"], p)
                V.tensor_tensor(pickw[:].rearrange("p t (g s) -> p t g s", g=2),
                                pick[:].rearrange("p t (g s) -> p t g s", g=2),
                                gate[:, :, bass.ds(2 * pair, 2)].unsqueeze(3).broadcast_to([P, NT, 2, CAP]),
                                ALU.mult).then_inc(z["Pw"], 1)

            def gathered(z, p, first=False):
                for half in range(2):
                    dve.wait_ge(z["gat"], 2 * p + half + 1)
                    if not first:
                        dve.wait_ge(z["B"], p)
                    V.tensor_tensor(xT[:, 4 * half:4 * half + 4, :],
                                    bank[6 + half][:].rearrange("p (k q) -> p k q", k=4),
                                    gffn[:, 4 * half:4 * half + 4].unsqueeze(2).broadcast_to([P, 4, P]),
                                    ALU.mult).then_inc(z["xT"], 1)

            def hidden(z, p, first=False):
                dve.wait_ge(z["sg"], p + 1)
                dve.wait_ge(z["B"], p + 1)
                if not first:
                    dve.wait_ge(z["hTp"], p)
                V.tensor_tensor(hid[:], sg[:].rearrange("p (q c) -> p c q", c=CE),
                                bank[5][:].rearrange("p (q c) -> p c q", c=CE), ALU.mult).then_inc(z["hid"], 1)

            def outputs(z, p, first=False):
                dve.wait_ge(z["STp"], p + 1)
                if not first:
                    dve.wait_ge(z["comb"], p)
                V.tensor_copy(pickT[:].rearrange("p t q -> p (t q)"), bank[5][:, 0:TOK]).then_inc(z["ST"], 1)
                dve.wait_ge(z["Y"], 2 * p + 2)
                V.tensor_copy(y[:, BANK:], bank[7][:]).then_inc(z["y1"], 1)

            def experts(p, first=False, last=False):
                weighted(main, p, p, first)
                if not last:
                    picks(main, p + 1, p + 1)
                hidden(main, p, first)
                if not last:
                    gathered(main, p + 1)
                outputs(main, p, first)

            picks(main, 0, 0, first=True)
            gathered(main, 0, first=True)
            experts(0, first=True)
            experts(1)
            with dve.Fori(0, LOOPS) as i:
                for j in range(STEP):
                    experts(i * STEP + PEEL + j)
            for p in range(PEEL + LOOPS * STEP, PAIRS):
                experts(p, last=(p == PAIRS - 1))

            dve.wait_ge(s["flag"], 1)
            crowded = dve.value_load(flag[0:1, 0:1])
            with dve.If(crowded > CAP):
                with dve.Fori(0, BLOCKS - 1) as b:
                    dve.wait_ge(over["comb"], b * PAIRS + 1)
                    V.tensor_scalar(slot[:], slot[:], -float(CAP), None, ALU.add).then_inc(s_over_slot, 1)
                    with dve.Fori(0, PAIRS) as p:
                        q = b * PAIRS + p
                        dve.wait_ge(over["comb"], q + 1)
                        dve.wait_ge(s_over_slot, b + 1)
                        picks(over, q, p, first=True)
                        weighted(over, q, p, first=True)
                        gathered(over, q, first=True)
                        hidden(over, q, first=True)
                        outputs(over, q, first=True)
                dve.wait_ge(over["comb"], (BLOCKS - 1) * PAIRS + 1)

            dve.wait_ge(main["comb"], PAIRS)
            for t in range(NT):
                for n in range(2):
                    cols = slice(n * BANK, (n + 1) * BANK)
                    link(V.tensor_tensor(x[:, t, cols], x[:, t, cols], bank[2 * t + n][:], ALU.add))
                squares(t, hk[:, t].rearrange("p k q -> p (k q)"))
            dve.wait_ge(s["late"], 16)
            for t in range(NT):
                dve.wait_ge(s["rms"], 2 * NT + t + 1)
                link(V.reciprocal(rs[:, t:t + 1], rs[:, t:t + 1]))
                V.scalar_tensor_tensor(out=x[:, t, :], in0=x[:, t, :], scalar=rs[:, t:t + 1], in1=gfin[:],
                                       op0=ALU.mult, op1=ALU.mult).then_inc(s["fx"], 1)

        @block.tensor
        def _(pe):
            mm = nc.tensor.matmul

            def transpose_rows(src, done):
                for j in range(4):
                    for kk in range(2):
                        for t in range(NT):
                            c = kk * TOK + t * P
                            last = nc.tensor.transpose(bank[j][:, c:c + P], src(t, 2 * j + kk), ident)
                    last.then_inc(done, 1)

            pe.wait_ge(s["small"], 16 * 10)
            mm(bank[7][0:12, 0:MAP], relb[:], onehot[:], start=True, stop=True).then_inc(s["tr1"], 1)
            pe.wait_ge(s["cst"], 16)
            pe.wait_ge(s["hk"], NT)
            transpose_rows(lambda t, k: hk[:, t, k, :], s["tr1"])

            pe.wait_ge(s["hk"], NT + 4)
            pe.wait_ge(s["dvec"], 1)
            for i, (u, col, kind, to, scale) in enumerate(blocks):
                arrived(pe, u)
                w = units[u][:].rearrange("p (k n) -> p k n", k=KD)
                if i >= 8:
                    pe.wait_ge((s["projA"], s["projD"])[i % 2], (i - 8) // 2 + 1)
                dst = bank[i % 8]
                for k in range(KD):
                    go = dict(start=(k == 0), stop=(k == KD - 1))
                    if kind == "T":
                        last = mm(dst[:, 0:TOK], w[:, k, col:col + P], hT[:, k, :], **go)
                    elif kind == "K":
                        for g in range(2):
                            last = mm(dst[g * HD:(g + 1) * HD, 0:TOK], w[:, k, col:col + HD], hT[:, k, :], **go)
                    elif kind == "V":
                        t = to[1]
                        last = mm(dst[:, 0:TOK], hT[:, k, t * P:(t + 1) * P], w[:, k, col:col + TOK], **go)
                if kind == "W":
                    for t in range(NT):
                        for k in range(KD):
                            last = mm(dst[:, t * P:(t + 1) * P], hT[:, k, t * P:(t + 1) * P], w[:, k, col:col + P],
                                      start=(k == 0), stop=(k == KD - 1))
                last.then_inc(s["proj"], 1)

            nb = len(blocks)
            pe.wait_ge(s["projA"], (nb + 1) // 2)
            pe.wait_ge(s["projD"], nb // 2)

            def qk_rows(b, h):
                half = slice((h % 2) * HD, (h % 2) * HD + HD)
                if b == A_:
                    return [(QK["Aq"] + h // 2, QK["Ak"] + h // 2, half)]
                if b == B_:
                    rows = slice(32 * h, 32 * h + 32)
                    return [(QK["Bq1"], QK["Bk1"], rows), (QK["Bq2"], QK["Bk2"], rows)]
                if b == C_BR:
                    return [(QK["Cq"] + h // 2, QK["Ck"] + h // 2, half)]
                return [(QK["Dq"] + h // 2, QK["Dk"] + h // 2, half)]

            def scores(st):
                b, h = divmod(st, 4)
                if st >= 1:
                    pe.wait_ge(s["sread"], st)
                maps = qk_rows(b, h)
                for i, (qb, kb, r) in enumerate(maps):
                    dst = bank[i if b == B_ else st % 2]
                    if b == C_BR:
                        mm(dst[:, 0:TOK], qk[r, kb, 0:P], qk[r, qb, :], start=True, stop=True)
                        last = mm(dst[:, TOK:MAP], qk[r, kb, P:TOK], qk[r, qb, P:TOK], start=True, stop=True)
                    else:
                        mm(dst[:, 0:P], qk[r, qb, 0:P], qk[r, kb, 0:P], start=True, stop=True)
                        last = mm(dst[:, P:MAP], qk[r, qb, P:TOK], qk[r, kb, :], start=True, stop=True)
                last.then_inc(s["scores"], 1)

            def gate_half(st, half):
                b, h = divmod(st, 4)
                n, t = divmod(h, 2)
                unit = where[("gate", b, n)]
                w = units[unit % RING1][:].rearrange("p (k n) -> p k n", k=KD)
                if half == 0:
                    arrived(pe, unit)
                    if st >= 2:
                        pe.wait_ge(s["gexp"], st - 1)
                for k in range(4 * half, 4 * half + 4):
                    last = mm(bank[4 + st % 2][:], hT[:, k, t * P:(t + 1) * P], w[:, k, :],
                              start=(k == 0), stop=(k == KD - 1))
                if half:
                    last.then_inc(s["gate"], 1)

            def middle(st):
                pe.wait_ge(s["probs"], st + 1)
                if st >= 1:
                    pe.wait_ge(s["pt"], st)
                if st // 4 == C_BR:
                    mm(bank[2][:, 0:MAP], at_or_after, prob[:, 1, :], start=True, stop=False, skip_group_check=True)
                    last = mm(bank[2][:, P:TOK], ones, prob[:, 1, TOK:MAP], start=False, stop=True,
                              skip_group_check=True)
                else:
                    for c in range(3):
                        last = nc.tensor.transpose(bank[2][:, c * P:(c + 1) * P], prob[:, 0, c * P:(c + 1) * P], ident)
                last.then_inc(s["ptps"], 1)

            def values(st):
                b, h = divmod(st, 4)
                pe.wait_ge(s["pt"], st + 1)
                if st >= 1:
                    pe.wait_ge(s["oev"], st)
                c = V_AT[b] + (h if b != D_ else h // 2) * HD
                mm(bank[3][:, 0:HD], pT[:, 0:P], vv[:, 0, c:c + HD], start=True, stop=True)
                mm(bank[3][:, HD:2 * HD], pT[:, P:TOK], vv[:, 0, c:c + HD], start=True, stop=False)
                mm(bank[3][:, HD:2 * HD], pT[:, TOK:MAP], vv[:, 1, c:c + HD], start=False, stop=True).then_inc(s["pv"], 1)

            def turn(b):
                if b == B_:
                    pe.wait_ge(s["ob"], 1)
                pe.wait_ge(s["oev"], 4 * b + 4)
                if b >= 1:
                    pe.wait_ge(s["mrg"], 4 * b)
                for c in range(2):
                    for t in range(NT):
                        last = nc.tensor.transpose(bank[7][:, c * TOK + t * P:c * TOK + (t + 1) * P],
                                                   o[:, b % 2, t, c * P:(c + 1) * P], ident)
                last.then_inc(s["oTps"], 1)

            def branch(b, j):
                t, n = divmod(j, 2)
                unit = where[("br", b, 0)]
                w = units[unit % RING1][:, 0:2 * D].rearrange("p (c n) -> p c n", c=2)
                arrived(pe, unit)
                pe.wait_ge(s["oTs"], b + 1)
                if 4 * b + j >= 2:
                    pe.wait_ge(s["mrg"], 4 * b + j - 1)
                for c in range(2):
                    last = mm(bank[6 + j % 2][:], oT[:, c, t * P:(t + 1) * P], w[:, c, n * BANK:(n + 1) * BANK],
                              start=(c == 0), stop=(c == 1))
                last.then_inc(s["br"], 1)

            for st in range(16):
                b, h = divmod(st, 4)
                scores(st)
                gate_half(st, 0)
                middle(st)
                gate_half(st, 1)
                values(st)
                if b >= 1 and h == 0:
                    turn(b - 1)
                if b >= 1 and h in (1, 2):
                    branch(b - 1, 2 * h - 2)
                    branch(b - 1, 2 * h - 1)
            turn(3)
            for j in range(4):
                branch(3, j)

            pe.wait_ge(s["mrg"], 16)
            transpose_rows(lambda t, k: merged[:, t, :].rearrange("p (q k) -> p k q", k=KD)[:, k, :], s["mTps"])
            pe.wait_ge(s["mTA"], 2)
            pe.wait_ge(s["mTD"], 2)
            pe.wait_ge(s["gexp"], 16)
            for t in range(NT):
                for n in range(2):
                    unit = where[("wo", n, 0)]
                    w = units[unit % RING1][:].rearrange("p (k n) -> p k n", k=KD)
                    arrived(pe, unit)
                    for k in range(KD):
                        last = mm(bank[4 + 2 * t + n][:], hT[:, k, t * P:(t + 1) * P], w[:, k, :],
                                  start=(k == 0), stop=(k == KD - 1))
                    last.then_inc(s["wo"], 1)

            pe.wait_ge(s["hk2"], NT)
            transpose_rows(lambda t, k: hk[:, t, k, :], s["h2ps"])
            pe.wait_ge(s["h2T"], 4)
            pe.wait_ge(s["wr"], 16 * 5)
            R = NG + NE
            for t in range(NT):
                for k in range(KD):
                    last = mm(bank[4][:, t * R:(t + 1) * R], hT[:, k, t * P:(t + 1) * P], wr[:, k, :],
                              start=(k == 0), stop=(k == KD - 1))
            last.then_inc(s["lg_ps"], 1)
            pe.wait_ge(s["asg"], 1)
            mm(bank[5][:, 0:NE], before, asg[:, 0, :], start=True, stop=True)
            mm(bank[5][:, NE:2 * NE], ones, asg[:, 0, :], start=True, stop=False)
            mm(bank[5][:, NE:2 * NE], before, asg[:, 1, :], start=False, stop=True)
            mm(bank[5][:, 2 * NE:3 * NE], ones, asg[:, 0, :], start=True, stop=False)
            mm(bank[5][:, 2 * NE:3 * NE], ones, asg[:, 1, :], start=False, stop=True).then_inc(s["pos"], 1)
            pe.wait_ge(s["flag"], 1)

            def gather(z, p, first=False):
                pe.wait_ge(z["P"], p + 1)
                if not first:
                    pe.wait_ge(z["y0"], p - 1)
                    pe.wait_ge(z["y1"], p - 1)
                for half in range(2):
                    for k in range(4 * half, 4 * half + 4):
                        c = (k % 4) * P
                        for t in range(NT):
                            last = mm(bank[6 + half][:, c:c + P], hk[:, t, k, :], pick[:, t, :],
                                      start=(t == 0), stop=(t == NT - 1))
                    last.then_inc(z["gat"], 1)

            def up(z, p, slots, here, first=False):
                pe.wait_ge(z["xT"], 2 * p + 2)
                for w in range(2):
                    if not first:
                        pe.wait_ge((z["hT"], z["ST"])[w], p)
                    for g in range(2):
                        here(2 * w + g)
                    for k in range(KD):
                        for g in range(2):
                            rhs = units[slots[2 * w + g]][:].rearrange("p (k n) -> p k n", k=KD)[:, k, :]
                            last = mm(bank[4 + w][g * CAP:(g + 1) * CAP, :], xT[:, k, g * CAP:(g + 1) * CAP], rhs,
                                      start=(k == 0), stop=(k == KD - 1))
                    last.then_inc((z["A"], z["B"])[w], 1)

            def turn_hidden(z, p):
                pe.wait_ge(z["hid"], p + 1)
                for c in range(CE):
                    last = nc.tensor.transpose(bank[4][:, c * P:(c + 1) * P], hid[:, c, :], ident)
                last.then_inc(z["hTp"], 1)
                pe.wait_ge(z["Pw"], p + 1)
                for t in range(NT):
                    last = nc.tensor.transpose(bank[5][:, t * P:(t + 1) * P], pickw[:, t, :], ident)
                last.then_inc(z["STp"], 1)

            def down(z, p, slots, here):
                pe.wait_ge(z["hT"], p + 1)
                for g in range(2):
                    here(4 + g)
                for n in range(2):
                    for c in range(CE):
                        for g in range(2):
                            rhs = units[slots[4 + g]][:].rearrange("p (c n) -> p c n", c=CE)
                            last = mm(bank[6 + n][g * CAP:(g + 1) * CAP, :], hidT[:, c, g * CAP:(g + 1) * CAP],
                                      rhs[:, c, n * BANK:(n + 1) * BANK], start=(c == 0), stop=(c == CE - 1))
                    last.then_inc(z["Y"], 1)

            def combine(z, p, start=False, stop=False):
                pe.wait_ge(z["y0"], p + 1)
                pe.wait_ge(z["y1"], p + 1)
                pe.wait_ge(z["ST"], p + 1)
                for t in range(NT):
                    for n in range(2):
                        last = mm(bank[2 * t + n][:], pickT[:, t, :], y[:, n * BANK:(n + 1) * BANK],
                                  start=start, stop=stop, skip_group_check=True)
                last.then_inc(z["comb"], 1)

            def experts(p, base, i=0, first=False, last=False, start=False):
                n0 = base * PAIR_UNITS
                slots = [slot_of(n0 + r) for r in range(PAIR_UNITS)]
                here = lambda r: pe.wait_ge(s_unit[slots[r]], unit_value(n0 + r, i))
                up(main, p, slots, here, first)
                if not last:
                    gather(main, p + 1, first=first)
                if not first:
                    combine(main, p - 1, start=start)
                turn_hidden(main, p)
                if not last:
                    pe.wait_ge(main["xT"], 2 * p + 4)
                down(main, p, slots, here)

            gather(main, 0, first=True)
            experts(0, 0, first=True)
            experts(1, 1, start=True)
            with pe.Fori(0, LOOPS) as i:
                for j in range(STEP):
                    experts(i * STEP + PEEL + j, PEEL + j, i)
            for p in range(PEEL + LOOPS * STEP, PAIRS):
                experts(p, p, last=(p == PAIRS - 1))
            combine(main, PAIRS - 1, stop=True)

            crowded = pe.value_load(flag[0:1, 0:1])
            with pe.If(crowded > CAP):
                pe.wait_ge(main["comb"], PAIRS)
                pe.nop().then_inc(over["comb"], 1)
                with pe.Fori(0, BLOCKS - 1) as b:
                    with pe.Fori(0, PAIRS) as p:
                        q = b * PAIRS + p
                        slots = list(range(PAIR_UNITS))
                        here = lambda r: pe.wait_ge(s_over_unit[r], 16 * q + 16)
                        gather(over, q, first=True)
                        up(over, q, slots, here, first=True)
                        turn_hidden(over, q)
                        down(over, q, slots, here)
                        combine(over, q)


_INS = ["x", "rel_bias", "g_mix", "w_in", "diff_lq1", "diff_lk1", "diff_lq2", "diff_lk2", "diff_subln", "swa_sinks",
        "w_gate", "w_br", "w_o", "g_ffn", "w_route_group", "b_route_group", "w_route_expert", "b_route_expert",
        "w1", "w3", "w2", "g_final"]


def _constants():
    import math
    import numpy as np

    j = np.arange(P)
    c = np.zeros((P, C_W), np.float32)
    c[:, C_ID:C_ID + P] = np.eye(P)
    c[:, C_GE:C_GE + P] = j[:, None] >= j[None, :]
    c[:, C_LT:C_LT + P] = j[:, None] < j[None, :]
    c[:, C_ONE:C_ONE + P] = 1.0
    c[:, C_SLOT:C_SLOT + CAP] = np.arange(CAP)
    c[:, C_IOTA:C_IOTA + NE] = np.arange(NE)
    diag = np.where(j[:, None] < j[None, :], 0.0, -NEG)
    c[:, C_DIAG:C_DIAG + P] = diag
    c[:, C_DIAG + 2 * P:C_DIAG + 3 * P] = diag
    c[:, C_EPS] = EPS
    c[:, C_UNIT] = 1.0
    dist = np.arange(MAP) - (P - 1)
    n = np.maximum(dist, 0)
    large = 16 + (np.log(np.maximum(n, 1) / 16) / math.log(128 / 16) * 16).astype(np.int32)
    bucket = np.where(n < 16, n, np.minimum(large, 31))
    onehot = np.zeros((32, MAP), np.float32)
    seen = (dist >= 0) & (dist < TOK)
    onehot[bucket[seen], np.nonzero(seen)[0]] = -1.0
    mask = np.zeros((12, MAP), np.float32)
    mask[:, dist < 0] = NEG
    mask[8:, dist >= 128] = NEG
    return {"constants": c, "bucket_onehot": onehot, "bias_mask": mask}


def kernel(**inputs):
    import numpy as np
    import concourse.bacc as bacc
    from concourse.bass_utils import run_bass_kernel_spmd

    nc = bacc.Bacc("TRN2", target_bir_lowering=False, num_devices=1)
    arrays, args = {}, {}
    for name, value in list(inputs.items()) + list(_constants().items()):
        v = np.ascontiguousarray(value)
        arrays[f"in_{name}"] = v
        args[name] = nc.dram_tensor(f"in_{name}", v.shape, mybir.dt.from_np(v.dtype), kind="ExternalInput").ap()
    out = nc.dram_tensor("out", (1, TOK, D), F32, kind="ExternalOutput").ap()
    hybrid_decoder_layer(nc, args, out)
    return run_bass_kernel_spmd(nc, [arrays], core_ids=[0]).results[0]["out"]
```

```python
from contextlib import ExitStack

import concourse.bass as bass
from concourse import mybir

F32 = mybir.dt.float32
I32 = mybir.dt.int32
ALU = mybir.AluOpType
ACT = mybir.ActivationFunctionType
AX = mybir.AxisListType.X

P = 128
TOK = 256
NT = TOK // P
D = 1024
KD = D // P
HD = 64
EPS = 1e-6
BANK = 512
NEG = 1.0e30

C_ID, C_GE, C_LT, C_ONE, C_SLOT, C_IOTA, C_DIAG = 0, 128, 256, 384, 512, 576, 608
C_EPS, C_UNIT, C_W = 992, 993, 994

CAP = 64
NG, EPG = 4, 8
NE = NG * EPG
DE = 512
CE = DE // P
PAIRS = NE // 2
BLOCKS = TOK // CAP

UNIT = 4096
RING, RING1 = 9, 7
PAIR_UNITS = 6
PEEL = 2
STEP = 3
LOOPS = 4

MAP = 3 * P
TILE_COLS = [(0, P), (P, MAP)]

A_, B_, C_BR, D_ = range(4)
QK = dict(Aq=0, Ak=2, Bq1=4, Bq2=5, Bk1=6, Bk2=7, Cq=8, Ck=10, Dq=12, Dk=14)
V_AT = [0, 256, 512, 768]
LAM_INIT = 0.2


def projection_blocks():
    s64, s32 = HD ** -0.5, 32 ** -0.5
    out = []
    out += [(0, 128 * i, "T", i, (-s64 if i < 2 else 1.0)) for i in range(4)]
    out += [(1, 0, "V", (A_, t), 1.0) for t in range(NT)]
    out += [(1, 256, "T", 4, -s32), (1, 384, "T", 5, -s32)]
    out += [(2, 0, "T", 6, 1.0), (2, 128, "T", 7, 1.0)]
    out += [(2, 256, "V", (B_, t), 1.0) for t in range(NT)]
    out += [(3, 128 * i, "T", 8 + i, (s64 if i < 2 else 1.0)) for i in range(4)]
    out += [(4, 0, "V", (C_BR, t), 1.0) for t in range(NT)]
    out += [(4, 256, "T", 12, -s64), (4, 384, "T", 13, -s64)]
    out += [(5, 0, "K", 14, 1.0), (5, 64, "K", 15, 1.0), (5, 128, "W", None, 1.0)]
    return out


def hybrid_decoder_layer(nc, a, out):
    blocks = projection_blocks()
    ends = [max(i for i, b in enumerate(blocks) if b[0] == u) + 1 for u in range(6)]

    stream = [("in", u, 0) for u in range(6)] + [("gate", 0, 0), ("gate", 0, 1)]
    for b in range(1, 4):
        stream += [("gate", b, 0), ("br", b - 1, 0), ("gate", b, 1)]
    stream += [("br", 3, 0), ("wo", 0, 0), ("wo", 1, 0)]
    slot_uses = [sum(u % RING1 == s for u in range(len(stream))) for s in range(RING)]
    slot_uses[7] = slot_uses[8] = 0
    where = {x: u for u, x in enumerate(stream)}
    FIRST = len(stream) % RING1

    with ExitStack() as ctx:
        at = [16512]

        def place(name, shape, dt=F32, offset=None):
            size = 4
            for n in shape[1:]:
                size *= n
            if offset is None:
                offset = at[0]
                at[0] += (size + 31) // 32 * 32
            return nc.alloc_sbuf_tensor_at(name, list(shape), dt, offset=offset)

        sem = lambda name: ctx.enter_context(nc.semaphore(name))
        bank = [ctx.enter_context(nc.psum_tensor(f"bank{i}", [P, BANK], F32)) for i in range(8)]

        cst = place("cst", [P, C_W])
        x = place("x", [P, NT, D])
        hk = place("hk", [P, NT, KD, P])
        hT = place("hT", [P, KD, TOK])
        merged = hk[:].rearrange("p t k q -> p t (k q)")
        wr = place("wr", [P, KD, NG + NE])
        rbias = place("rbias", [P, NG + NE])
        gmix = place("gmix", [P, KD])
        gffn = place("gffn", [P, KD])
        sub = place("sub", [P, HD])
        sinks = place("sinks", [P, 4])
        nsink = place("nsink", [P, 4])
        lqk = place("lqk", [P, 2, 2, 32])
        lam = place("lam", [P, 8])
        ss = place("ss", [P, 2])
        rs = place("rs", [P, 2])
        nm = place("nm", [P, 2, 2, 2])
        lsum = place("lsum", [P, 2, 2, 2])
        esink = place("esink", [P, 2, 2])
        shared = at[0]
        ring_at = 229344 - RING * UNIT * 4
        units = [place(f"unit{s}", [P, UNIT], offset=ring_at + 4 * UNIT * ((s + 2) % RING)) for s in range(RING)]

        vv = place("vv", [P, NT, 896])
        sig = place("sig", [P, NT, D])
        o = place("o", [P, NT, 256])
        oT = place("oT", [P, 2, TOK])
        pT = place("pT", [P, MAP])
        prob1 = place("prob1", [P, 2, MAP])
        assert at[0] <= ring_at, (at[0], ring_at)
        relb = place("relb", [32, 12], offset=shared + 7168)
        onehot = place("onehot", [32, MAP], offset=shared + 7168 + 64)
        bmask = place("bmask", [12, MAP], offset=shared + 7168 + 64 + 1536)
        dvec = place("dvec", [12, MAP], offset=shared + 7168 + 64 + 3072)
        at[0] = ring_at
        qk = place("qk", [P, 16, TOK])
        bias = place("bias", [P, 12, TOK])
        prob0 = place("prob0", [P, 2, MAP])
        prob = (prob0, prob1)
        assert at[0] <= ring_at + 8 * UNIT

        at[0] = shared
        xT = place("xT", [P, KD, P])
        sg = place("sg", [P, DE])
        hid = place("hid", [P, CE, P])
        hidT = place("hidT", [P, CE, P])
        y = place("y", [P, D])
        pick = place("pick", [P, NT, P])
        pickw = place("pickw", [P, NT, P])
        pickT = place("pickT", [P, NT, P])
        lg = place("lg", [P, NT, NG + NE])
        ge = place("ge", [P, NT, NG])
        eg = place("eg", [P, NT, NG])
        cg = place("cg", [P, NT, NG])
        ohg = place("ohg", [P, NT, NG])
        em = place("em", [P, NT, NE])
        ce = place("ce", [P, NT, NE])
        oh1 = place("oh1", [P, NT, NE])
        oh2 = place("oh2", [P, NT, NE])
        asg = place("asg", [P, NT, NE])
        gate = place("gate", [P, NT, NE])
        slot = place("slot", [P, NT, NE])
        m = place("m", [P, 10, NT])
        most = place("most", [P, 1])
        flag = place("flag", [P, 1], I32)
        gfin = place("gfin", [P, D])
        assert at[0] <= ring_at

        dram_vec = nc.dram_tensor("dram_vec", (12, MAP), F32, kind="Internal").ap()

        ident = cst[:, C_ID:C_ID + P]
        at_or_after = cst[:, C_GE:C_GE + P]
        before = cst[:, C_LT:C_LT + P]
        ones = cst[:, C_ONE:C_ONE + P]
        slot_no = cst[:, C_SLOT:C_SLOT + CAP]
        eps = cst[:, C_EPS:C_EPS + 1]
        unit1 = cst[:, C_UNIT:C_UNIT + 1]

        names = """cst small wr late scratch biasT hk tr1 dvec lamx lame proj projA projD scores sread norm probs maps logs
            ptps dd pt gate tanh pv oev bsq brms ob oTps oTs br mrg mTps mTA mTD wo h2ps h2T lg_ps eg sums e2 asg
            pos flag fx stored chain_a chain_d rms hk2"""
        s = {n: sem("s_" + n) for n in names.split()}
        s_x = [sem(f"s_rows{t}") for t in range(NT)]
        s_unit = [sem(f"s_unit{i}") for i in range(RING)]

        def moe_sems(tag):
            ns = "P Pw gat xT A B sg hid hTp STp hT ST Y y0 y1 comb".split()
            return {n: sem(f"s_{tag}_{n}") for n in ns}

        main, over = moe_sems("moe"), moe_sems("over")
        s_over_unit = [sem(f"s_over_unit{i}") for i in range(PAIR_UNITS)]
        s_over_slot = sem("s_over_slot")

        def arrived(eng, unit):
            eng.wait_ge(s_unit[unit % RING1], 16 * (unit // RING1 + 1))

        def slot_of(n):
            return (n + FIRST) % RING

        def unit_value(n, i=0):
            k = slot_of(n)
            first = (k - FIRST) % RING
            return i * (16 * PAIR_UNITS * STEP // RING) + 16 * (slot_uses[k] + (n - first) // RING + 1)

        def free_of(n, i=0):
            p, r = divmod(n, PAIR_UNITS)
            p = i * STEP + p
            return ((main["A"], p + 1), (main["B"], p + 1), (main["Y"], 2 * p + 2))[r // 2]

        def expert_source(r, expert):
            w = (a["w1"], a["w3"], a["w2"])[r // 2]
            e = expert + r % 2
            rows = CE if r >= 4 else KD
            return w[0, bass.ds(e, 1)].rearrange("e (p k) n -> p (e k) n", p=P, k=rows)

        def unit_view(k, r):
            return units[k][:].rearrange("p (k n) -> p k n", k=(CE if r >= 4 else KD))

        block = ctx.enter_context(nc.Block())

        @block.sync
        def _(sp):
            for t in range(NT):
                sp.dma_start(x[:, t, :], a["x"][0, t * P:(t + 1) * P, :]).then_inc(s_x[t], 16)
            sp.dma_start(cst[:], a["constants"]).then_inc(s["cst"], 16)
            sp.dma_start(gmix[:], a["g_mix"][0].rearrange("(p k) -> p k", k=KD)).then_inc(s["small"], 16)
            sp.dma_start(relb[:], a["rel_bias"]).then_inc(s["small"], 16)
            sp.dma_start(onehot[:], a["bucket_onehot"]).then_inc(s["small"], 16)
            sp.dma_start(bmask[:], a["bias_mask"]).then_inc(s["small"], 16)
            for i, n in enumerate(("diff_lq1", "diff_lk1", "diff_lq2", "diff_lk2")):
                sp.dma_start(lqk[:, i // 2, i % 2, :], a[n][0].partition_broadcast(P)).then_inc(s["small"], 16)
            sp.dma_start(sub[:], a["diff_subln"][0].partition_broadcast(P)).then_inc(s["small"], 16)
            sp.dma_start(sinks[:], a["swa_sinks"][0].partition_broadcast(P)).then_inc(s["small"], 16)

            def released(u):
                kind, i, n = stream[u]
                if kind == "in":
                    sp.wait_ge(s["proj"], ends[i])
                elif kind == "gate":
                    sp.wait_ge(s["gate"], 4 * i + 2 * n + 2)
                elif kind == "br":
                    sp.wait_ge(s["br"], 4 * i + 4)
                else:
                    sp.wait_ge(s["wo"], 3 + i)

            w_in = a["w_in"][0].rearrange("(p k) n -> p k n", k=KD)
            w_o = a["w_o"][0].rearrange("(p k) n -> p k n", k=KD)
            for u, (kind, i, n) in enumerate(stream):
                if u >= RING1:
                    released(u - RING1)
                dst = units[u % RING1]
                if kind == "in":
                    wide = min(BANK, 2816 - BANK * i)
                    src = w_in[:, :, BANK * i:BANK * i + wide]
                    dst = dst[:].rearrange("p (k n) -> p k n", k=KD)[:, :, 0:wide]
                elif kind == "gate":
                    src = a["w_gate"][0, i].rearrange("(p k) n -> p k n", k=KD)[:, :, BANK * n:BANK * (n + 1)]
                    dst = dst[:].rearrange("p (k n) -> p k n", k=KD)
                elif kind == "br":
                    src = a["w_br"][0, i].rearrange("(c p) n -> p c n", p=P)
                    dst = dst[:, 0:2 * D].rearrange("p (c n) -> p c n", c=2)
                else:
                    src = w_o[:, :, BANK * i:BANK * (i + 1)]
                    dst = dst[:].rearrange("p (k n) -> p k n", k=KD)
                sp.dma_start(dst, src).then_inc(s_unit[u % RING1], 16)

            def load_expert_unit(n, i=0, loop=False):
                if n < RING and not loop:
                    k = slot_of(n)
                    if k < RING1:
                        released(max(u for u in range(len(stream)) if u % RING1 == k))
                    else:
                        sp.wait_ge(s["pv"], 16)
                else:
                    sp.wait_ge(*free_of(n - RING, i))
                p, r = divmod(n, PAIR_UNITS)
                sp.dma_start(unit_view(slot_of(n), r), expert_source(r, (i * STEP + p) * 2)).then_inc(s_unit[slot_of(n)], 16)

            head = 2 * PAIR_UNITS
            for n in range(head):
                load_expert_unit(n)
            span = STEP * PAIR_UNITS
            with sp.Fori(0, LOOPS) as i:
                for n in range(head, head + span):
                    load_expert_unit(n, i, loop=True)
            for n in range(head + LOOPS * span, PAIRS * PAIR_UNITS):
                load_expert_unit(n)

            sp.wait_ge(s["flag"], 1)
            crowded = sp.value_load(flag[0:1, 0:1])
            with sp.If(crowded > CAP):
                sp.wait_ge(main["Y"], 2 * PAIRS)
                with sp.Fori(0, BLOCKS - 1) as b:
                    with sp.Fori(0, PAIRS) as p:
                        sp.wait_ge(over["comb"], b * PAIRS + p + 1)
                        for r in range(PAIR_UNITS):
                            sp.dma_start(unit_view(r, r), expert_source(r, p * 2)).then_inc(s_over_unit[r], 16)
                sp.wait_ge(over["comb"], (BLOCKS - 1) * PAIRS + 1)

            sp.wait_ge(main["comb"], PAIRS)
            for t in range(NT):
                sp.wait_ge(s["fx"], t + 1)
                sp.dma_start(out[0, t * P:(t + 1) * P, :], x[:, t, :]).then_inc(s["stored"], 16)
            sp.wait_ge(s["stored"], 16 * NT)

        @block.gpsimd
        def _(pool):
            pool.wait_ge(s["dvec"], 1)
            pool.dma_start(dram_vec, dvec[:]).then_inc(s["scratch"], 16)
            pool.wait_ge(s["scratch"], 16)
            pool.dma_start(bias[:], bass.AP(dram_vec.tensor, 0, [[1, P], [MAP, 12], [1, TOK]])).then_inc(s["biasT"], 16)
            pool.wait_ge(s["hk2"], NT)
            pool.dma_start(gfin[:], a["g_final"].partition_broadcast(P)).then_inc(s["late"], 16)

        @block.scalar
        def _(act):
            chain = [0]

            def link(ins):
                chain[0] += 1
                ins.then_inc(s["chain_a"], 1)
                act.wait_ge(s["chain_a"], chain[0])

            act.dma_start(gffn[:], a["g_ffn"][0].rearrange("(p k) -> p k", k=KD)).then_inc(s["wr"], 16)
            act.dma_start(wr[:, :, 0:NG], a["w_route_group"][0].rearrange("(p k) n -> p k n", k=KD)).then_inc(s["wr"], 16)
            act.dma_start(wr[:, :, NG:], a["w_route_expert"][0].rearrange("(p k) n -> p k n", k=KD)).then_inc(s["wr"], 16)
            act.dma_start(rbias[:, 0:NG], a["b_route_group"][0].partition_broadcast(P)).then_inc(s["wr"], 16)
            act.dma_start(rbias[:, NG:], a["b_route_expert"][0].partition_broadcast(P)).then_inc(s["wr"], 16)

            def root(n, src, scale, dst, done):
                act.wait_ge(s["sums"], n)
                nc.scalar.activation(dst, src, ACT.Sqrt, bias=eps, scale=scale).then_inc(done, 1)

            act.wait_ge(s["cst"], 16)
            for t in range(NT):
                root(t + 1, ss[:, t:t + 1], 1.0 / D, rs[:, t:t + 1], s["rms"])
            act.wait_ge(s["lamx"], 1)
            nc.scalar.activation(lam[:, 2:4], lam[:, 0:2], ACT.Exp).then_inc(s["lame"], 1)

            def block_out(i):
                unit, col, kind, to, scale = blocks[i]
                src = bank[i % 8][:, 0:TOK]
                if kind in "TK":
                    return qk[:, to, :], src, scale
                if kind == "V":
                    return vv[:, to[1], V_AT[to[0]]:V_AT[to[0]] + 256], src, scale
                return vv[:, :, V_AT[3]:V_AT[3] + P], src.rearrange("p (t n) -> p t n", t=NT), scale

            for i in range(0, len(blocks), 2):
                act.wait_ge(s["proj"], i + 1)
                dst, src, scale = block_out(i)
                nc.scalar.activation(dst, src, ACT.Copy, scale=scale).then_inc(s["projA"], 1)

            def exponentials(st):
                b, h = divmod(st, 4)
                par = st % 2
                pr = prob[par]
                if b == D_:
                    act.wait_ge(s["norm"], h + 1)
                    for t in range(NT):
                        nc.scalar.activation(esink[:, par, t:t + 1], sinks[:, h:h + 1], ACT.Exp,
                                             bias=nm[:, par, 0, t:t + 1])
                else:
                    act.wait_ge(s["sread"], st + 1)
                if b == C_BR:
                    link(nc.scalar.activation(pr[:, 1, :], pr[:, 0, :], ACT.Abs))
                    link(nc.scalar.activation(pr[:, 1, :], pr[:, 1, :], ACT.Exp, scale=-1.0))
                    return
                for mp in range(2 if b == B_ else 1):
                    for t, (c0, c1) in enumerate(TILE_COLS):
                        last = nc.scalar.activation(pr[:, mp, c0:c1], pr[:, mp, c0:c1], ACT.Exp, scale=-1.0,
                                                    bias=nm[:, par, mp, t:t + 1], accum_out=lsum[:, par, mp, t:t + 1])
                last.then_inc(s["maps"] if b == B_ else s["probs"], 1)

            def keys_on_rows(st):
                if st >= 1:
                    act.wait_ge(s["pv"], st)
                if st // 4 == C_BR:
                    act.wait_ge(s["dd"], st % 4 + 1)
                    nc.scalar.activation(pT[:], prob[st % 2][:, 0, :], ACT.Exp).then_inc(s["pt"], 1)
                else:
                    act.wait_ge(s["ptps"], st + 1)
                    nc.scalar.activation(pT[:], bank[2][:, 0:MAP], ACT.Copy).then_inc(s["pt"], 1)

            exponentials(0)
            for st in range(16):
                b, h = divmod(st, 4)
                ahead = st + 1 if st < 15 else None
                if b != C_BR:
                    keys_on_rows(st)
                if ahead:
                    exponentials(ahead)
                if b == C_BR:
                    keys_on_rows(st)
                if ahead and ahead // 4 == C_BR:
                    l = prob[ahead % 2][:, 1, :]
                    nc.scalar.activation(l, l, ACT.Ln, bias=unit1).then_inc(s["logs"], 1)
                n, t = divmod(h, 2)
                act.wait_ge(s["gate"], st + 1)
                if b >= 1:
                    act.wait_ge(s["mrg"], 4 * (b - 1) + h + 1)
                nc.scalar.activation(sig[:, t, n * BANK:(n + 1) * BANK], bank[4 + st % 2][:], ACT.Tanh,
                                     scale=0.5).then_inc(s["tanh"], 1)
                if st == 7:
                    act.wait_ge(s["bsq"], 1)
                    nc.scalar.activation(lsum[:].rearrange("p a b t -> p (a b t)"), lsum[:].rearrange("p a b t -> p (a b t)"),
                                         ACT.Sqrt, bias=eps, scale=1.0 / HD).then_inc(s["brms"], 1)

            for j in range(0, 4, 2):
                act.wait_ge(s["mTps"], j + 1)
                nc.scalar.activation(hT[:, 2 * j:2 * j + 2, :].rearrange("p k t -> p (k t)"), bank[j][:],
                                     ACT.Copy, scale=0.5).then_inc(s["mTA"], 1)
            for t in range(NT):
                root(NT + t + 1, ss[:, t:t + 1], 1.0 / D, rs[:, t:t + 1], s["rms"])
            act.wait_ge(s["eg"], 1)
            nc.scalar.activation(eg[:], ge[:], ACT.Exp).then_inc(s["e2"], 1)
            act.wait_ge(s["eg"], 2)
            nc.scalar.activation(m[:, 6, :], m[:, 5, :], ACT.Exp).then_inc(s["e2"], 1)

            def experts(z, p, first=False):
                act.wait_ge(z["A"], p + 1)
                if not first:
                    act.wait_ge(z["hid"], p)
                nc.scalar.activation(sg[:], bank[4][:], ACT.Silu).then_inc(z["sg"], 1)
                act.wait_ge(z["hTp"], p + 1)
                if not first:
                    act.wait_ge(z["Y"], 2 * p)
                nc.scalar.activation(hidT[:].rearrange("p c q -> p (c q)"), bank[4][:], ACT.Copy).then_inc(z["hT"], 1)
                act.wait_ge(z["Y"], 2 * p + 1)
                if not first:
                    act.wait_ge(z["comb"], p)
                nc.scalar.activation(y[:, 0:BANK], bank[6][:], ACT.Copy).then_inc(z["y0"], 1)

            experts(main, 0, first=True)
            experts(main, 1)
            with act.Fori(0, LOOPS) as i:
                for j in range(STEP):
                    experts(main, i * STEP + PEEL + j)
            for p in range(PEEL + LOOPS * STEP, PAIRS):
                experts(main, p)

            act.wait_ge(s["flag"], 1)
            crowded = act.value_load(flag[0:1, 0:1])
            with act.If(crowded > CAP):
                with act.Fori(0, BLOCKS - 1) as b:
                    with act.Fori(0, PAIRS) as p:
                        q = b * PAIRS + p
                        act.wait_ge(over["comb"], q + 1)
                        experts(over, q, first=True)
                act.wait_ge(over["comb"], (BLOCKS - 1) * PAIRS + 1)
            for t in range(NT):
                root(2 * NT + t + 1, ss[:, t:t + 1], 1.0 / D, rs[:, t:t + 1], s["rms"])

        @block.vector
        def _(dve):
            chain = [0]

            def link(ins):
                chain[0] += 1
                ins.then_inc(s["chain_d"], 1)
                dve.wait_ge(s["chain_d"], chain[0])

            def squares(t, junk):
                nc.vector.tensor_tensor_reduce(out=junk, in0=x[:, t, :], in1=x[:, t, :], scale=1.0, scalar=0.0,
                                               op0=ALU.mult, op1=ALU.add, accum_out=ss[:, t:t + 1]).then_inc(s["sums"], 1)

            def normalise(t, n, done):
                dve.wait_ge(s["rms"], n)
                link(nc.vector.reciprocal(rs[:, t:t + 1], rs[:, t:t + 1]))
                nc.vector.tensor_scalar(hk[:, t, :, :], x[:, t, :].rearrange("p (q k) -> p k q", k=KD),
                                        rs[:, t:t + 1], None, ALU.mult).then_inc(done, 1)

            def scaled(dst, src, g, done):
                nc.vector.tensor_tensor(dst, src, g.unsqueeze(2).broadcast_to([P, 2, TOK]), ALU.mult).then_inc(done, 1)

            for t in range(NT):
                dve.wait_ge(s_x[t], 16)
                squares(t, hk[:, t].rearrange("p k q -> p (k q)"))
            for t in range(NT):
                normalise(t, t + 1, s["hk"])

            dve.wait_ge(s["small"], 16 * 10)
            dve.wait_ge(s["tr1"], 1)
            nc.vector.tensor_tensor(dvec[:], bank[7][0:12, 0:MAP], bmask[:], ALU.add).then_inc(s["dvec"], 1)
            for j in range(4):
                dve.wait_ge(s["tr1"], j + 2)
                scaled(hT[:, 2 * j:2 * j + 2, :], bank[j][:].rearrange("p (k t) -> p k t", k=2),
                       gmix[:, 2 * j:2 * j + 2], s["hk"])
            link(nc.vector.tensor_tensor(lqk[:, :, 0, :], lqk[:, :, 0, :], lqk[:, :, 1, :], ALU.mult))
            nc.vector.tensor_reduce(lam[:, 0:2], lqk[:, :, 0, :], AX, ALU.add).then_inc(s["lamx"], 1)
            link(nc.vector.tensor_scalar(sub[:], sub[:], 1.0 - LAM_INIT, None, ALU.mult))
            link(nc.vector.tensor_scalar(nsink[:], sinks[:], -1.0, None, ALU.mult))
            dve.wait_ge(s["lame"], 1)
            link(nc.vector.tensor_tensor(lam[:, 4:5], lam[:, 3:4], lam[:, 2:3], ALU.subtract))
            link(nc.vector.tensor_scalar(lam[:, 5:6], lam[:, 4:5], -LAM_INIT, None, ALU.add))
            neg_lam = lam[:, 5:6]

            def block_out(i):
                unit, col, kind, to, scale = blocks[i]
                src = bank[i % 8][:, 0:TOK]
                if kind in "TK":
                    return qk[:, to, :], src, scale
                if kind == "V":
                    return vv[:, to[1], V_AT[to[0]]:V_AT[to[0]] + 256], src, scale
                return vv[:, :, V_AT[3]:V_AT[3] + P], src.rearrange("p (t n) -> p t n", t=NT), scale

            for i in range(1, len(blocks), 2):
                dve.wait_ge(s["proj"], i + 1)
                dst, src, scale = block_out(i)
                nc.vector.tensor_scalar(dst, src, scale, None, ALU.mult).then_inc(s["projD"], 1)

            dve.wait_ge(s["biasT"], 16)

            def biased(par, mp, src, table):
                for t, (c0, c1) in enumerate(TILE_COLS):
                    keys = bias[:, table, 127::-1] if t == 0 else bias[:, table, 255::-1]
                    last = nc.vector.tensor_tensor_reduce(out=prob[par][:, mp, c0:c1], in0=src[:, c0:c1], in1=keys,
                                                          scale=1.0, scalar=4.0 * NEG, op0=ALU.add, op1=ALU.min,
                                                          accum_out=nm[:, par, mp, t:t + 1])
                return last

            def front(st):
                b, h = divmod(st, 4)
                par = st % 2
                dve.wait_ge(s["scores"], st + 1)
                if st >= 2:
                    dve.wait_ge(s["pt"], st - 1)
                if b == B_:
                    biased(par, 0, bank[0], 4 + h)
                    biased(par, 1, bank[1], 4 + h).then_inc(s["sread"], 1)
                elif b == C_BR:
                    nc.vector.tensor_tensor(prob[par][:, 0, :], bank[par][:, 0:MAP], cst[:, C_DIAG:C_DIAG + MAP],
                                            ALU.add).then_inc(s["sread"], 1)
                else:
                    biased(par, 0, bank[par], h if b == A_ else 8 + h).then_inc(s["sread"], 1)
                    if b == D_:
                        dve.wait_ge(s["sread"], st + 1)
                        nc.vector.tensor_scalar(nm[:, par, 0, :], nm[:, par, 0, :], nsink[:, h:h + 1], None,
                                                ALU.min).then_inc(s["norm"], 1)

            def difference(st):
                par = st % 2
                pr = prob[par]
                dve.wait_ge(s["maps"], st % 4 + 1)
                link(nc.vector.reciprocal(lsum[:, par, :, :], lsum[:, par, :, :]))
                link(nc.vector.tensor_scalar(lsum[:, par, 1, :], lsum[:, par, 1, :], neg_lam, None, ALU.mult))
                for t, (c0, c1) in enumerate(TILE_COLS):
                    link(nc.vector.tensor_scalar(pr[:, 1, c0:c1], pr[:, 1, c0:c1], lsum[:, par, 1, t:t + 1],
                                                 None, ALU.mult))
                for t, (c0, c1) in enumerate(TILE_COLS):
                    last = nc.vector.scalar_tensor_tensor(out=pr[:, 0, c0:c1], in0=pr[:, 0, c0:c1],
                                                          scalar=lsum[:, par, 0, t:t + 1], in1=pr[:, 1, c0:c1],
                                                          op0=ALU.mult, op1=ALU.add)
                last.then_inc(s["probs"], 1)

            def softplus(st):
                pr = prob[st % 2]
                dve.wait_ge(s["logs"], st % 4 + 1)
                nc.vector.scalar_tensor_tensor(out=pr[:, 1, :], in0=pr[:, 0, :], scalar=0.0, in1=pr[:, 1, :],
                                               op0=ALU.max, op1=ALU.add).then_inc(s["probs"], 1)

            def log_weights(st):
                pr = prob[st % 2]
                dve.wait_ge(s["ptps"], st + 1)
                nc.vector.tensor_tensor(pr[:, 0, :], pr[:, 0, :], bank[2][:, 0:MAP], ALU.subtract).then_inc(s["dd"], 1)

            def head_output(st):
                b, h = divmod(st, 4)
                par = st % 2
                if b in (A_, D_):
                    dve.wait_ge(s["probs"], st + 1)
                    if b == D_:
                        link(nc.vector.tensor_tensor(lsum[:, par, 0, :], lsum[:, par, 0, :], esink[:, par, :], ALU.add))
                    link(nc.vector.reciprocal(lsum[:, par, 0, :], lsum[:, par, 0, :]))
                    dve.wait_ge(s["pv"], st + 1)
                    for t in range(NT):
                        last = nc.vector.tensor_scalar(o[:, t, h * HD:(h + 1) * HD], bank[3][:, t * HD:(t + 1) * HD],
                                                       lsum[:, par, 0, t:t + 1], None, ALU.mult)
                else:
                    dve.wait_ge(s["pv"], st + 1)
                    last = nc.vector.tensor_copy(o[:, :, h * HD:(h + 1) * HD],
                                                 bank[3][:, 0:P].rearrange("p (t d) -> p t d", t=NT))
                last.then_inc(s["oev"], 1)

            def head_norms():
                heads = o[:].rearrange("p t (h d) -> p (t h) d", d=HD)
                dve.wait_ge(s["oev"], 8)
                sq = oT[:].rearrange("p c (g d) -> p (c g) d", d=HD)
                rms = lsum[:].rearrange("p a b t -> p (a b t)")
                link(nc.vector.tensor_tensor(sq, heads, heads, ALU.mult))
                nc.vector.tensor_reduce(rms, sq, AX, ALU.add).then_inc(s["bsq"], 1)
                dve.wait_ge(s["brms"], 1)
                link(nc.vector.reciprocal(rms, rms))
                link(nc.vector.tensor_tensor(heads, heads, rms.unsqueeze(2).broadcast_to([P, 8, HD]), ALU.mult))
                nc.vector.tensor_tensor(heads, heads, sub[:].unsqueeze(1).broadcast_to([P, 8, HD]),
                                        ALU.mult).then_inc(s["ob"], 1)

            def turned(b):
                dve.wait_ge(s["oTps"], b + 1)
                if b >= 1:
                    dve.wait_ge(s["br"], 4 * b)
                nc.vector.tensor_copy(oT[:].rearrange("p c t -> p (c t)"), bank[7][:]).then_inc(s["oTs"], 1)

            def merge(b, j):
                n, t = divmod(j, 2)
                cols = slice(n * BANK, (n + 1) * BANK)
                chunk = sig[:, t, cols]
                dve.wait_ge(s["br"], 4 * b + j + 1)
                dve.wait_ge(s["tanh"], 4 * b + j + 1)
                to = merged[:, t, cols] if b == 0 else chunk
                gated = nc.vector.scalar_tensor_tensor(out=to, in0=chunk, scalar=1.0, in1=bank[6 + j % 2][:],
                                                       op0=ALU.add, op1=ALU.mult)
                if b == 0:
                    gated.then_inc(s["mrg"], 1)
                else:
                    link(gated)
                    nc.vector.tensor_tensor(merged[:, t, cols], merged[:, t, cols], chunk, ALU.add).then_inc(s["mrg"], 1)

            front(0)
            for st in range(16):
                b, h = divmod(st, 4)
                ahead = st + 1 if st < 15 else None
                if ahead:
                    front(ahead)
                if b == C_BR:
                    log_weights(st)
                if ahead and ahead // 4 == B_:
                    difference(ahead)
                if b >= 1 and h == 0:
                    turned(b - 1)
                if ahead == 8:
                    softplus(ahead)
                head_output(st)
                if b >= 1:
                    merge(b - 1, h)
                if ahead and ahead // 4 == C_BR and ahead != 8:
                    softplus(ahead)
                if st == 7:
                    head_norms()
            turned(3)
            for j in range(4):
                merge(3, j)

            for j in range(1, 4, 2):
                dve.wait_ge(s["mTps"], j + 1)
                nc.vector.tensor_scalar(hT[:, 2 * j:2 * j + 2, :].rearrange("p k t -> p (k t)"), bank[j][:], 0.5, None,
                                        ALU.mult).then_inc(s["mTD"], 1)
            for t in range(NT):
                for n in range(2):
                    dve.wait_ge(s["wo"], 2 * t + n + 1)
                    cols = slice(n * BANK, (n + 1) * BANK)
                    link(nc.vector.tensor_tensor(x[:, t, cols], x[:, t, cols], bank[4 + 2 * t + n][:], ALU.add))
                squares(t, hk[:, t].rearrange("p k q -> p (k q)"))
            for t in range(NT):
                normalise(t, NT + t + 1, s["hk2"])
            dve.wait_ge(s["wr"], 16 * 5)
            for j in range(4):
                dve.wait_ge(s["h2ps"], j + 1)
                scaled(hT[:, 2 * j:2 * j + 2, :], bank[j][:].rearrange("p (k t) -> p k t", k=2),
                       gffn[:, 2 * j:2 * j + 2], s["h2T"])

            V = nc.vector
            t4 = lambda ap: ap.unsqueeze(2).broadcast_to([P, NT, NG])
            t32 = lambda ap: ap.unsqueeze(2).broadcast_to([P, NT, NE])
            iota = lambda n: cst[:, C_IOTA:C_IOTA + n].unsqueeze(1).broadcast_to([P, NT, n])
            dve.wait_ge(s["lg_ps"], 1)
            link(V.tensor_tensor(lg[:], bank[4][:, 0:NT * (NG + NE)].rearrange("p (t n) -> p t n", t=NT),
                                 rbias[:].unsqueeze(1).broadcast_to([P, NT, NG + NE]), ALU.add))
            link(V.tensor_reduce(m[:, 0, :], lg[:, :, 0:NG], AX, ALU.max))
            V.tensor_tensor(ge[:], lg[:, :, 0:NG], t4(m[:, 0, :]), ALU.subtract).then_inc(s["eg"], 1)
            dve.wait_ge(s["eg"], 1)
            link(V.tensor_scalar(cg[:], ge[:], 0.0, -float(NE), ALU.is_equal, ALU.mult))
            link(V.tensor_tensor(cg[:], cg[:], iota(NG), ALU.add))
            link(V.tensor_reduce(m[:, 1, :], cg[:], AX, ALU.min))
            link(V.tensor_tensor(ohg[:], cg[:], t4(m[:, 1, :]), ALU.is_equal))
            dve.wait_ge(s["e2"], 1)
            link(V.tensor_reduce(m[:, 2, :], eg[:], AX, ALU.add))
            link(V.reciprocal(m[:, 2, :], m[:, 2, :]))
            link(V.tensor_scalar(ohg[:], ohg[:], -1.0, NEG, ALU.add, ALU.mult))
            for t in range(NT):
                link(V.tensor_tensor(em[:, t, :].rearrange("p (g e) -> p g e", g=NG),
                                     lg[:, t, NG:].rearrange("p (g e) -> p g e", g=NG),
                                     ohg[:, t, :].unsqueeze(2).broadcast_to([P, NG, EPG]), ALU.add))
            for k, oh in ((3, oh1), (4, oh2)):
                link(V.tensor_reduce(m[:, k, :], em[:], AX, ALU.max))
                link(V.tensor_tensor(ce[:], em[:], t32(m[:, k, :]), ALU.is_equal))
                link(V.scalar_tensor_tensor(out=ce[:], in0=ce[:], scalar=-float(NE), in1=iota(NE),
                                            op0=ALU.mult, op1=ALU.add))
                link(V.tensor_reduce(m[:, 7, :], ce[:], AX, ALU.min))
                link(V.tensor_tensor(oh[:], ce[:], t32(m[:, 7, :]), ALU.is_equal))
                if k == 3:
                    link(V.scalar_tensor_tensor(out=em[:], in0=oh[:], scalar=-NEG, in1=em[:],
                                                op0=ALU.mult, op1=ALU.add))
            V.tensor_tensor(asg[:], oh1[:], oh2[:], ALU.add).then_inc(s["asg"], 1)
            V.tensor_tensor(m[:, 5, :], m[:, 4, :], m[:, 3, :], ALU.subtract).then_inc(s["eg"], 1)
            dve.wait_ge(s["e2"], 2)
            link(V.tensor_scalar(m[:, 7, :], m[:, 6, :], 1.0, None, ALU.add))
            link(V.reciprocal(m[:, 7, :], m[:, 7, :]))
            link(V.tensor_tensor(m[:, 8, :], m[:, 7, :], m[:, 2, :], ALU.mult))
            link(V.tensor_tensor(m[:, 9, :], m[:, 8, :], m[:, 6, :], ALU.mult))
            link(V.tensor_tensor(gate[:], oh1[:], t32(m[:, 8, :]), ALU.mult))
            link(V.tensor_tensor(ce[:], oh2[:], t32(m[:, 9, :]), ALU.mult))
            link(V.tensor_tensor(gate[:], gate[:], ce[:], ALU.add))
            dve.wait_ge(s["pos"], 1)
            link(V.scalar_tensor_tensor(out=slot[:], in0=bank[5][:, 0:NT * NE].rearrange("p (t e) -> p t e", t=NT),
                                        scalar=1.0, in1=asg[:], op0=ALU.add, op1=ALU.mult))
            link(V.tensor_scalar(slot[:], slot[:], -1.0, None, ALU.add))
            link(V.tensor_reduce(most[:], bank[5][:, NT * NE:(NT + 1) * NE], AX, ALU.max))
            V.tensor_copy(flag[:], most[:]).then_inc(s["flag"], 1)

            def picks(z, p, pair, first=False):
                if not first:
                    dve.wait_ge(z["gat"], 2 * p)
                    dve.wait_ge(z["Pw"], p)
                V.tensor_tensor(pick[:].rearrange("p t (g s) -> p t g s", g=2),
                                slot[:, :, bass.ds(2 * pair, 2)].unsqueeze(3).broadcast_to([P, NT, 2, CAP]),
                                slot_no.unsqueeze(1).unsqueeze(1).broadcast_to([P, NT, 2, CAP]),
                                ALU.is_equal).then_inc(z["P"], 1)

            def weighted(z, p, pair, first=False):
                dve.wait_ge(z["P"], p + 1)
                if not first:
                    dve.wait_ge(z["STp"], p)
                V.tensor_tensor(pickw[:].rearrange("p t (g s) -> p t g s", g=2),
                                pick[:].rearrange("p t (g s) -> p t g s", g=2),
                                gate[:, :, bass.ds(2 * pair, 2)].unsqueeze(3).broadcast_to([P, NT, 2, CAP]),
                                ALU.mult).then_inc(z["Pw"], 1)

            def gathered(z, p, first=False):
                for half in range(2):
                    dve.wait_ge(z["gat"], 2 * p + half + 1)
                    if not first:
                        dve.wait_ge(z["B"], p)
                    V.tensor_tensor(xT[:, 4 * half:4 * half + 4, :],
                                    bank[6 + half][:].rearrange("p (k q) -> p k q", k=4),
                                    gffn[:, 4 * half:4 * half + 4].unsqueeze(2).broadcast_to([P, 4, P]),
                                    ALU.mult).then_inc(z["xT"], 1)

            def hidden(z, p, first=False):
                dve.wait_ge(z["sg"], p + 1)
                dve.wait_ge(z["B"], p + 1)
                if not first:
                    dve.wait_ge(z["hTp"], p)
                V.tensor_tensor(hid[:], sg[:].rearrange("p (q c) -> p c q", c=CE),
                                bank[5][:].rearrange("p (q c) -> p c q", c=CE), ALU.mult).then_inc(z["hid"], 1)

            def outputs(z, p, first=False):
                dve.wait_ge(z["STp"], p + 1)
                if not first:
                    dve.wait_ge(z["comb"], p)
                V.tensor_copy(pickT[:].rearrange("p t q -> p (t q)"), bank[5][:, 0:TOK]).then_inc(z["ST"], 1)
                dve.wait_ge(z["Y"], 2 * p + 2)
                V.tensor_copy(y[:, BANK:], bank[7][:]).then_inc(z["y1"], 1)

            def experts(p, first=False, last=False):
                weighted(main, p, p, first)
                if not last:
                    picks(main, p + 1, p + 1)
                hidden(main, p, first)
                if not last:
                    gathered(main, p + 1)
                outputs(main, p, first)

            picks(main, 0, 0, first=True)
            gathered(main, 0, first=True)
            experts(0, first=True)
            experts(1)
            with dve.Fori(0, LOOPS) as i:
                for j in range(STEP):
                    experts(i * STEP + PEEL + j)
            for p in range(PEEL + LOOPS * STEP, PAIRS):
                experts(p, last=(p == PAIRS - 1))

            dve.wait_ge(s["flag"], 1)
            crowded = dve.value_load(flag[0:1, 0:1])
            with dve.If(crowded > CAP):
                with dve.Fori(0, BLOCKS - 1) as b:
                    dve.wait_ge(over["comb"], b * PAIRS + 1)
                    V.tensor_scalar(slot[:], slot[:], -float(CAP), None, ALU.add).then_inc(s_over_slot, 1)
                    with dve.Fori(0, PAIRS) as p:
                        q = b * PAIRS + p
                        dve.wait_ge(over["comb"], q + 1)
                        dve.wait_ge(s_over_slot, b + 1)
                        picks(over, q, p, first=True)
                        weighted(over, q, p, first=True)
                        gathered(over, q, first=True)
                        hidden(over, q, first=True)
                        outputs(over, q, first=True)
                dve.wait_ge(over["comb"], (BLOCKS - 1) * PAIRS + 1)

            dve.wait_ge(main["comb"], PAIRS)
            for t in range(NT):
                for n in range(2):
                    cols = slice(n * BANK, (n + 1) * BANK)
                    link(V.tensor_tensor(x[:, t, cols], x[:, t, cols], bank[2 * t + n][:], ALU.add))
                squares(t, hk[:, t].rearrange("p k q -> p (k q)"))
            dve.wait_ge(s["late"], 16)
            for t in range(NT):
                dve.wait_ge(s["rms"], 2 * NT + t + 1)
                link(V.reciprocal(rs[:, t:t + 1], rs[:, t:t + 1]))
                V.scalar_tensor_tensor(out=x[:, t, :], in0=x[:, t, :], scalar=rs[:, t:t + 1], in1=gfin[:],
                                       op0=ALU.mult, op1=ALU.mult).then_inc(s["fx"], 1)

        @block.tensor
        def _(pe):
            mm = nc.tensor.matmul

            def transpose_rows(src, done):
                for j in range(4):
                    for kk in range(2):
                        for t in range(NT):
                            c = kk * TOK + t * P
                            last = nc.tensor.transpose(bank[j][:, c:c + P], src(t, 2 * j + kk), ident)
                    last.then_inc(done, 1)

            pe.wait_ge(s["small"], 16 * 10)
            mm(bank[7][0:12, 0:MAP], relb[:], onehot[:], start=True, stop=True).then_inc(s["tr1"], 1)
            pe.wait_ge(s["cst"], 16)
            pe.wait_ge(s["hk"], NT)
            transpose_rows(lambda t, k: hk[:, t, k, :], s["tr1"])

            pe.wait_ge(s["hk"], NT + 4)
            pe.wait_ge(s["dvec"], 1)
            for i, (u, col, kind, to, scale) in enumerate(blocks):
                arrived(pe, u)
                w = units[u][:].rearrange("p (k n) -> p k n", k=KD)
                if i >= 8:
                    pe.wait_ge((s["projA"], s["projD"])[i % 2], (i - 8) // 2 + 1)
                dst = bank[i % 8]
                for k in range(KD):
                    go = dict(start=(k == 0), stop=(k == KD - 1))
                    if kind == "T":
                        last = mm(dst[:, 0:TOK], w[:, k, col:col + P], hT[:, k, :], **go)
                    elif kind == "K":
                        for g in range(2):
                            last = mm(dst[g * HD:(g + 1) * HD, 0:TOK], w[:, k, col:col + HD], hT[:, k, :], **go)
                    elif kind == "V":
                        t = to[1]
                        last = mm(dst[:, 0:TOK], hT[:, k, t * P:(t + 1) * P], w[:, k, col:col + TOK], **go)
                if kind == "W":
                    for t in range(NT):
                        for k in range(KD):
                            last = mm(dst[:, t * P:(t + 1) * P], hT[:, k, t * P:(t + 1) * P], w[:, k, col:col + P],
                                      start=(k == 0), stop=(k == KD - 1))
                last.then_inc(s["proj"], 1)

            nb = len(blocks)
            pe.wait_ge(s["projA"], (nb + 1) // 2)
            pe.wait_ge(s["projD"], nb // 2)

            def qk_rows(b, h):
                half = slice((h % 2) * HD, (h % 2) * HD + HD)
                if b == A_:
                    return [(QK["Aq"] + h // 2, QK["Ak"] + h // 2, half)]
                if b == B_:
                    rows = slice(32 * h, 32 * h + 32)
                    return [(QK["Bq1"], QK["Bk1"], rows), (QK["Bq2"], QK["Bk2"], rows)]
                if b == C_BR:
                    return [(QK["Cq"] + h // 2, QK["Ck"] + h // 2, half)]
                return [(QK["Dq"] + h // 2, QK["Dk"] + h // 2, half)]

            def scores(st):
                b, h = divmod(st, 4)
                if st >= 1:
                    pe.wait_ge(s["sread"], st)
                maps = qk_rows(b, h)
                for i, (qb, kb, r) in enumerate(maps):
                    dst = bank[i if b == B_ else st % 2]
                    if b == C_BR:
                        mm(dst[:, 0:TOK], qk[r, kb, 0:P], qk[r, qb, :], start=True, stop=True)
                        last = mm(dst[:, TOK:MAP], qk[r, kb, P:TOK], qk[r, qb, P:TOK], start=True, stop=True)
                    else:
                        mm(dst[:, 0:P], qk[r, qb, 0:P], qk[r, kb, 0:P], start=True, stop=True)
                        last = mm(dst[:, P:MAP], qk[r, qb, P:TOK], qk[r, kb, :], start=True, stop=True)
                last.then_inc(s["scores"], 1)

            def gate_half(st, half):
                b, h = divmod(st, 4)
                n, t = divmod(h, 2)
                unit = where[("gate", b, n)]
                w = units[unit % RING1][:].rearrange("p (k n) -> p k n", k=KD)
                if half == 0:
                    arrived(pe, unit)
                    if st >= 2:
                        pe.wait_ge(s["tanh"], st - 1)
                for k in range(4 * half, 4 * half + 4):
                    last = mm(bank[4 + st % 2][:], hT[:, k, t * P:(t + 1) * P], w[:, k, :],
                              start=(k == 0), stop=(k == KD - 1))
                if half:
                    last.then_inc(s["gate"], 1)

            def middle(st):
                pe.wait_ge(s["probs"], st + 1)
                if st >= 1:
                    pe.wait_ge(s["pt"], st)
                if st // 4 == C_BR:
                    mm(bank[2][:, 0:MAP], at_or_after, prob[st % 2][:, 1, :], start=True, stop=False, skip_group_check=True)
                    last = mm(bank[2][:, P:TOK], ones, prob[st % 2][:, 1, TOK:MAP], start=False, stop=True,
                              skip_group_check=True)
                else:
                    for c in range(3):
                        last = nc.tensor.transpose(bank[2][:, c * P:(c + 1) * P], prob[st % 2][:, 0, c * P:(c + 1) * P],
                                                   ident)
                last.then_inc(s["ptps"], 1)

            def values(st):
                b, h = divmod(st, 4)
                pe.wait_ge(s["pt"], st + 1)
                if st >= 1:
                    pe.wait_ge(s["oev"], st)
                c = V_AT[b] + (h if b != D_ else h // 2) * HD
                mm(bank[3][:, 0:HD], pT[:, 0:P], vv[:, 0, c:c + HD], start=True, stop=True)
                mm(bank[3][:, HD:2 * HD], pT[:, P:TOK], vv[:, 0, c:c + HD], start=True, stop=False)
                mm(bank[3][:, HD:2 * HD], pT[:, TOK:MAP], vv[:, 1, c:c + HD], start=False, stop=True).then_inc(s["pv"], 1)

            def turn(b):
                if b == B_:
                    pe.wait_ge(s["ob"], 1)
                pe.wait_ge(s["oev"], 4 * b + 4)
                if b >= 1:
                    pe.wait_ge(s["mrg"], 4 * b)
                for c in range(2):
                    for t in range(NT):
                        last = nc.tensor.transpose(bank[7][:, c * TOK + t * P:c * TOK + (t + 1) * P],
                                                   o[:, t, c * P:(c + 1) * P], ident)
                last.then_inc(s["oTps"], 1)

            def branch(b, j):
                n, t = divmod(j, 2)
                unit = where[("br", b, 0)]
                w = units[unit % RING1][:, 0:2 * D].rearrange("p (c n) -> p c n", c=2)
                arrived(pe, unit)
                pe.wait_ge(s["oTs"], b + 1)
                if 4 * b + j >= 2:
                    pe.wait_ge(s["mrg"], 4 * b + j - 1)
                for c in range(2):
                    last = mm(bank[6 + j % 2][:], oT[:, c, t * P:(t + 1) * P], w[:, c, n * BANK:(n + 1) * BANK],
                              start=(c == 0), stop=(c == 1))
                last.then_inc(s["br"], 1)

            scores(0)
            for st in range(16):
                b, h = divmod(st, 4)
                gate_half(st, 0)
                if st < 15:
                    scores(st + 1)
                middle(st)
                if b >= 1 and h == 0:
                    turn(b - 1)
                gate_half(st, 1)
                values(st)
                if b >= 1:
                    branch(b - 1, h)
            turn(3)
            for j in range(4):
                branch(3, j)

            pe.wait_ge(s["mrg"], 16)
            transpose_rows(lambda t, k: merged[:, t, :].rearrange("p (q k) -> p k q", k=KD)[:, k, :], s["mTps"])
            pe.wait_ge(s["mTA"], 2)
            pe.wait_ge(s["mTD"], 2)
            pe.wait_ge(s["tanh"], 16)
            for t in range(NT):
                for n in range(2):
                    unit = where[("wo", n, 0)]
                    w = units[unit % RING1][:].rearrange("p (k n) -> p k n", k=KD)
                    arrived(pe, unit)
                    for k in range(KD):
                        last = mm(bank[4 + 2 * t + n][:], hT[:, k, t * P:(t + 1) * P], w[:, k, :],
                                  start=(k == 0), stop=(k == KD - 1))
                    last.then_inc(s["wo"], 1)

            pe.wait_ge(s["hk2"], NT)
            transpose_rows(lambda t, k: hk[:, t, k, :], s["h2ps"])
            pe.wait_ge(s["h2T"], 4)
            pe.wait_ge(s["wr"], 16 * 5)
            R = NG + NE
            for t in range(NT):
                for k in range(KD):
                    last = mm(bank[4][:, t * R:(t + 1) * R], hT[:, k, t * P:(t + 1) * P], wr[:, k, :],
                              start=(k == 0), stop=(k == KD - 1))
            last.then_inc(s["lg_ps"], 1)
            pe.wait_ge(s["asg"], 1)
            mm(bank[5][:, 0:NE], before, asg[:, 0, :], start=True, stop=True)
            mm(bank[5][:, NE:2 * NE], ones, asg[:, 0, :], start=True, stop=False)
            mm(bank[5][:, NE:2 * NE], before, asg[:, 1, :], start=False, stop=True)
            mm(bank[5][:, 2 * NE:3 * NE], ones, asg[:, 0, :], start=True, stop=False)
            mm(bank[5][:, 2 * NE:3 * NE], ones, asg[:, 1, :], start=False, stop=True).then_inc(s["pos"], 1)
            pe.wait_ge(s["flag"], 1)

            def gather(z, p, first=False):
                pe.wait_ge(z["P"], p + 1)
                if not first:
                    pe.wait_ge(z["y0"], p - 1)
                    pe.wait_ge(z["y1"], p - 1)
                for half in range(2):
                    for k in range(4 * half, 4 * half + 4):
                        c = (k % 4) * P
                        for t in range(NT):
                            last = mm(bank[6 + half][:, c:c + P], hk[:, t, k, :], pick[:, t, :],
                                      start=(t == 0), stop=(t == NT - 1))
                    last.then_inc(z["gat"], 1)

            def up(z, p, slots, here, first=False):
                pe.wait_ge(z["xT"], 2 * p + 2)
                for w in range(2):
                    if not first:
                        pe.wait_ge((z["hT"], z["ST"])[w], p)
                    for g in range(2):
                        here(2 * w + g)
                    for k in range(KD):
                        for g in range(2):
                            rhs = units[slots[2 * w + g]][:].rearrange("p (k n) -> p k n", k=KD)[:, k, :]
                            last = mm(bank[4 + w][g * CAP:(g + 1) * CAP, :], xT[:, k, g * CAP:(g + 1) * CAP], rhs,
                                      start=(k == 0), stop=(k == KD - 1))
                    last.then_inc((z["A"], z["B"])[w], 1)

            def turn_hidden(z, p):
                pe.wait_ge(z["hid"], p + 1)
                for c in range(CE):
                    last = nc.tensor.transpose(bank[4][:, c * P:(c + 1) * P], hid[:, c, :], ident)
                last.then_inc(z["hTp"], 1)
                pe.wait_ge(z["Pw"], p + 1)
                for t in range(NT):
                    last = nc.tensor.transpose(bank[5][:, t * P:(t + 1) * P], pickw[:, t, :], ident)
                last.then_inc(z["STp"], 1)

            def down(z, p, slots, here):
                pe.wait_ge(z["hT"], p + 1)
                for g in range(2):
                    here(4 + g)
                for n in range(2):
                    for c in range(CE):
                        for g in range(2):
                            rhs = units[slots[4 + g]][:].rearrange("p (c n) -> p c n", c=CE)
                            last = mm(bank[6 + n][g * CAP:(g + 1) * CAP, :], hidT[:, c, g * CAP:(g + 1) * CAP],
                                      rhs[:, c, n * BANK:(n + 1) * BANK], start=(c == 0), stop=(c == CE - 1))
                    last.then_inc(z["Y"], 1)

            def combine(z, p, start=False, stop=False):
                pe.wait_ge(z["y0"], p + 1)
                pe.wait_ge(z["y1"], p + 1)
                pe.wait_ge(z["ST"], p + 1)
                for t in range(NT):
                    for n in range(2):
                        last = mm(bank[2 * t + n][:], pickT[:, t, :], y[:, n * BANK:(n + 1) * BANK],
                                  start=start, stop=stop, skip_group_check=True)
                last.then_inc(z["comb"], 1)

            def experts(p, base, i=0, first=False, last=False, start=False):
                n0 = base * PAIR_UNITS
                slots = [slot_of(n0 + r) for r in range(PAIR_UNITS)]
                here = lambda r: pe.wait_ge(s_unit[slots[r]], unit_value(n0 + r, i))
                up(main, p, slots, here, first)
                if not last:
                    gather(main, p + 1, first=first)
                if not first:
                    combine(main, p - 1, start=start)
                turn_hidden(main, p)
                if not last:
                    pe.wait_ge(main["xT"], 2 * p + 4)
                down(main, p, slots, here)

            gather(main, 0, first=True)
            experts(0, 0, first=True)
            experts(1, 1, start=True)
            with pe.Fori(0, LOOPS) as i:
                for j in range(STEP):
                    experts(i * STEP + PEEL + j, PEEL + j, i)
            for p in range(PEEL + LOOPS * STEP, PAIRS):
                experts(p, p, last=(p == PAIRS - 1))
            combine(main, PAIRS - 1, stop=True)

            crowded = pe.value_load(flag[0:1, 0:1])
            with pe.If(crowded > CAP):
                pe.wait_ge(main["comb"], PAIRS)
                pe.nop().then_inc(over["comb"], 1)
                with pe.Fori(0, BLOCKS - 1) as b:
                    with pe.Fori(0, PAIRS) as p:
                        q = b * PAIRS + p
                        slots = list(range(PAIR_UNITS))
                        here = lambda r: pe.wait_ge(s_over_unit[r], 16 * q + 16)
                        gather(over, q, first=True)
                        up(over, q, slots, here, first=True)
                        turn_hidden(over, q)
                        down(over, q, slots, here)
                        combine(over, q)


_INS = ["x", "rel_bias", "g_mix", "w_in", "diff_lq1", "diff_lk1", "diff_lq2", "diff_lk2", "diff_subln", "swa_sinks",
        "w_gate", "w_br", "w_o", "g_ffn", "w_route_group", "b_route_group", "w_route_expert", "b_route_expert",
        "w1", "w3", "w2", "g_final"]


def _constants():
    import math
    import numpy as np

    j = np.arange(P)
    c = np.zeros((P, C_W), np.float32)
    c[:, C_ID:C_ID + P] = np.eye(P)
    c[:, C_GE:C_GE + P] = j[:, None] >= j[None, :]
    c[:, C_LT:C_LT + P] = j[:, None] < j[None, :]
    c[:, C_ONE:C_ONE + P] = 1.0
    c[:, C_SLOT:C_SLOT + CAP] = np.arange(CAP)
    c[:, C_IOTA:C_IOTA + NE] = np.arange(NE)
    diag = np.where(j[:, None] < j[None, :], 0.0, -NEG)
    c[:, C_DIAG:C_DIAG + P] = diag
    c[:, C_DIAG + 2 * P:C_DIAG + 3 * P] = diag
    c[:, C_EPS] = EPS
    c[:, C_UNIT] = 1.0
    dist = np.arange(MAP) - (P - 1)
    n = np.maximum(dist, 0)
    large = 16 + (np.log(np.maximum(n, 1) / 16) / math.log(128 / 16) * 16).astype(np.int32)
    bucket = np.where(n < 16, n, np.minimum(large, 31))
    onehot = np.zeros((32, MAP), np.float32)
    seen = (dist >= 0) & (dist < TOK)
    onehot[bucket[seen], np.nonzero(seen)[0]] = -1.0
    mask = np.zeros((12, MAP), np.float32)
    mask[:, dist < 0] = NEG
    mask[8:, dist >= 128] = NEG
    return {"constants": c, "bucket_onehot": onehot, "bias_mask": mask}


def kernel(**inputs):
    import numpy as np
    import concourse.bacc as bacc
    from concourse.bass_utils import run_bass_kernel_spmd

    nc = bacc.Bacc("TRN2", target_bir_lowering=False, num_devices=1)
    arrays, args = {}, {}
    for name, value in list(inputs.items()) + list(_constants().items()):
        v = np.ascontiguousarray(value)
        arrays[f"in_{name}"] = v
        args[name] = nc.dram_tensor(f"in_{name}", v.shape, mybir.dt.from_np(v.dtype), kind="ExternalInput").ap()
    out = nc.dram_tensor("out", (1, TOK, D), F32, kind="ExternalOutput").ap()
    hybrid_decoder_layer(nc, args, out)
    return run_bass_kernel_spmd(nc, [arrays], core_ids=[0]).results[0]["out"]
```

```python
from contextlib import ExitStack

import concourse.bass as bass
from concourse import mybir

F32 = mybir.dt.float32
F32R = mybir.dt.float32r
BF16 = mybir.dt.bfloat16
I32 = mybir.dt.int32
ALU = mybir.AluOpType
ACT = mybir.ActivationFunctionType
AX = mybir.AxisListType.X

P = 128
TOK = 256
NT = TOK // P
D = 1024
KD = D // P
HD = 64
EPS = 1e-6
BANK = 512
NEG = 1.0e30

C_ID, C_SLOT, C_IOTA = 0, 128, 192
C_GE, C_ONE, C_DIAG, C_W = 232, 360, 488, 872

CAP = 64
NG, EPG = 4, 8
NE = NG * EPG
DE = 512
CE = DE // P
PAIRS = NE // 2
BLOCKS = TOK // CAP

UNIT = 4096
RING, RING1 = 10, 5
EXPERT_SLOTS = (0, 8, 9, 1, 2, 3, 5, 4, 6, 7)
PAIR_UNITS = 6
PEEL = 2
STEP = 5
LOOPS = 2
LAST_PIECES = ((0, 0, 0, 4), (0, 0, 4, 8), (2, 0, 0, 4), (2, 0, 4, 6), (2, 0, 6, 8),
               (4, 0, 0, 4), (4, 1, 0, 2), (4, 1, 2, 4))

MAP = 3 * P
TILE_COLS = [(0, P), (P, MAP)]

A_, B_, C_BR, D_ = range(4)
QK = dict(Aq=0, Ak=2, Bq1=4, Bq2=5, Bk1=6, Bk2=7, Cq=8, Ck=10, Dq=12, Dk=14)
V_AT = [0, 256, 512, 768]
LAM_INIT = 0.2
LAST_ORDER = (0, 2, 1, 3)


def projection_blocks():
    s64, s32 = HD ** -0.5, 32 ** -0.5
    out = []
    out += [(0, 128 * i, "T", i, (-s64 if i < 2 else 1.0)) for i in range(4)]
    out += [(1, 0, "V", (A_, t), 1.0) for t in range(NT)]
    out += [(1, 256, "T", 4, -s32), (1, 384, "T", 5, -s32)]
    out += [(2, 0, "T", 6, 1.0), (2, 128, "T", 7, 1.0)]
    out += [(2, 256, "V", (B_, t), 1.0) for t in range(NT)]
    out += [(3, 128 * i, "T", 8 + i, (s64 if i < 2 else 1.0)) for i in range(4)]
    out += [(4, 0, "V", (C_BR, t), 1.0) for t in range(NT)]
    out += [(4, 256, "T", 12, -s64), (4, 384, "T", 13, -s64)]
    out += [(5, 256, "T", 14, 1.0), (5, 384, "W", None, 1.0)]
    return out


def hybrid_decoder_layer(nc, a, out):
    blocks = projection_blocks()
    ends = [max(i for i, b in enumerate(blocks) if b[0] == u) + 1 for u in range(6)]

    stream = [("in", u, 0) for u in range(6)] + [("gate", 0, 0), ("gate", 0, 1)]
    for b in range(1, 4):
        stream += [("gate", b, 0), ("br", b - 1, 0), ("gate", b, 1)]
    stream += [("br", 3, 0), ("wo", 0, 0), ("wo", 1, 0)]
    slot_uses = [sum(u % RING1 == s for u in range(len(stream))) for s in range(RING)]
    slot_uses = [n if k < RING1 else 0 for k, n in enumerate(slot_uses)]
    where = {x: u for u, x in enumerate(stream)}
    split = [x for x in stream if x[0] != "br"]

    with ExitStack() as ctx:
        at = [16512]

        def place(name, shape, dt=F32, offset=None):
            size = 2 if dt == BF16 else 4
            for n in shape[1:]:
                size *= n
            if offset is None:
                offset = at[0]
                at[0] += (size + 31) // 32 * 32
            return nc.alloc_sbuf_tensor_at(name, list(shape), dt, offset=offset)

        sem = lambda name: ctx.enter_context(nc.semaphore(name))
        bank = [ctx.enter_context(nc.psum_tensor(f"bank{i}", [P, BANK], F32)) for i in range(8)]

        cst_at = at[0]
        cst = place("cst", [P, C_W])
        pad = at[0]
        at[0] = cst_at + 4 * (C_GE + D)
        gfin = place("gfin", [P, D], offset=cst_at + 4 * C_GE)
        after_pad, at[0] = at[0], pad
        lqk = place("lqk", [P, 2, 2, 32])
        sub = place("sub", [P, HD])
        before_bf = place("before_bf", [P, P], BF16)
        ones_bf = place("ones_bf", [P, P], BF16)
        rbias = place("rbias", [P, NG + NE])
        sinks = place("sinks", [P, 4])
        nsink = place("nsink", [P, 4])
        assert at[0] <= after_pad, (at[0], after_pad)
        at[0] = after_pad
        x = place("x", [P, NT, D])
        hk_at = at[0]
        hk = place("hk", [P, NT, KD, P])
        hk_1 = place("hk_1", [P, NT, KD, P], BF16, offset=hk_at)
        hk_2 = place("hk_2", [P, NT, KD, P], BF16, offset=hk_at + 2 * NT * D)
        hT_at = at[0]
        hT_hi = place("hT_hi", [P, KD, TOK], F32R)
        h2T = place("h2T", [P, KD, TOK], offset=hT_at)
        xT = place("xT", [P, KD, P], offset=hT_at)
        hid = place("hid", [P, CE, P], offset=hT_at + 4 * D)
        hidT = place("hidT", [P, CE, P], offset=hT_at + 4 * D + 4 * DE)
        merged = hk[:].rearrange("p t k q -> p t (k q)")
        wr = place("wr", [P, KD, NG + NE])
        gmix = place("gmix", [P, KD])
        gffn = place("gffn", [P, KD])
        lam = place("lam", [P, 8])
        ss = place("ss", [P, 2])
        ss4 = place("ss4", [P, 2, 2])
        rs = place("rs", [P, 2])
        scalars = place("scalars", [P, 3])
        eps, unit1 = scalars[:, 0:1], scalars[:, 1:2]
        warm = scalars[:, 2:3]
        nm = place("nm", [P, 2, 2, 2])
        lsum = place("lsum", [P, 2, 2, 2])
        esink = place("esink", [P, 2, 2])
        shared = at[0]
        ring_at = 229344 - RING * UNIT * 4
        units = [place(f"unit{s}", [P, UNIT], offset=ring_at + 4 * UNIT * ((s + 3) % RING)) for s in range(RING)]

        low = [place(f"low{s}", [P, KD, BANK], F32R, offset=ring_at + 4 * UNIT * (s + 3)) for s in range(RING1)]
        slot_at = lambda s: ring_at + 4 * UNIT * (s + 3)
        br_low = [place(f"br_low{s}", [P, 2, D], F32R, offset=slot_at(s)) for s in range(RING1)]
        br_high = [place(f"br_high{s}", [P, 2, D], F32R, offset=slot_at(s) + 2 * UNIT) for s in range(RING1)]
        high = [place(f"high{i}", [P, KD, BANK], F32R, offset=ring_at + 4 * UNIT * (RING1 + i + 3)) for i in range(2)]
        xg = place("xg", [P, NT, D], offset=ring_at + 4 * UNIT * 9)

        vv = place("vv", [P, NT, 896])
        sig = place("sig", [P, NT, D])
        o = place("o", [P, NT, 256])
        oT_at = at[0]
        oT_hi = place("oT_hi", [P, 2, TOK], F32R)
        oT_lo = place("oT_lo", [P, 2, TOK], F32R)
        head_squares = place("head_squares", [P, 2, TOK], offset=oT_at)
        pT = place("pT", [P, MAP])
        prob1 = place("prob1", [P, 2, MAP])
        hT_lo = place("hT_lo", [P, KD, TOK], F32R)
        assert at[0] <= ring_at + 4 * UNIT, (at[0], ring_at)
        relb = place("relb", [32, 12], offset=shared + 7168)
        onehot = place("onehot", [32, MAP], offset=shared + 7168 + 64)
        bmask = place("bmask", [12, MAP], offset=shared + 7168 + 64 + 1536)
        dvec = place("dvec", [12, MAP], offset=shared + 7168 + 64 + 3072)
        at[0] = ring_at + 4 * UNIT
        qk = place("qk", [P, 15, TOK])
        bias = place("bias", [P, 12, TOK])
        prob0 = place("prob0", [P, 2, MAP])
        prob = (prob0, prob1)
        assert at[0] <= ring_at + 3 * 4 * UNIT

        at[0] = shared
        sg = place("sg", [P, DE])
        y = place("y", [P, D])
        hk_3 = place("hk_3", [P, NT, KD, P], BF16)
        pick = place("pick", [P, NT, P], BF16)
        pickw = place("pickw", [P, NT, P])
        pickT = place("pickT", [P, NT, P])
        lg = place("lg", [P, NT, NG + NE])
        ge = place("ge", [P, NT, NG])
        eg = place("eg", [P, NT, NG])
        cg = place("cg", [P, NT, NG])
        ohg = place("ohg", [P, NT, NG])
        em = place("em", [P, NT, NE])
        ce = place("ce", [P, NT, NE])
        oh1 = place("oh1", [P, NT, NE])
        oh2 = place("oh2", [P, NT, NE])
        asg = place("asg", [P, NT, NE], BF16)
        gate = place("gate", [P, NT, NE])
        slot = place("slot", [P, NT, NE])
        m = place("m", [P, 10, NT])
        most = place("most", [P, 1])
        flag = place("flag", [P, 1], I32)
        assert at[0] <= ring_at

        rest = place("rest", [P, NT, KD, P], offset=ring_at)

        dram_vec = nc.dram_tensor("dram_vec", (12, MAP), F32, kind="Internal").ap()

        ident = cst[:, C_ID:C_ID + P]
        at_or_after = cst[:, C_GE:C_GE + P]
        ones = cst[:, C_ONE:C_ONE + P]
        slot_no = cst[:, C_SLOT:C_SLOT + CAP]

        names = """cst small wr late scratch biasT hk tr1 dvec lamx lame proj projA projD scores sread norm probs
            maps logs ptps dd pt gate tanh pv oev bsq brms ob oTps oTs br mrg first_half bf x1 x2 squared
            scaledD scaledA rs h2T hkh hkl total mTps mTh mTl hTh hTl high low wo h2ps lg_ps eg sums e2 asg
            pos flag stored warm table tri oTh brh brl xg half_up early queries chain_a chain_d rms"""
        s = {n: sem("s_" + n) for n in names.split()}
        s_x = [sem(f"s_rows{t}") for t in range(NT)]
        s_unit = [sem(f"s_unit{i}") for i in range(RING)]
        s_last = [sem(f"s_last{i}") for i in range(len(LAST_PIECES))]

        def split_count(xi, k):
            return 4 + 2 * (xi - 1) + k // 4 + 1 if xi else k // 2 + 1

        def parts(xi, piece):
            u = where[split[xi]]
            size = 4 if xi else 2
            ks = slice(size * piece, size * piece + size)
            cols = slice(BANK - TOK, BANK) if split[xi] == ("in", 5, 0) else slice(0, BANK)
            w = units[u % RING1][:].rearrange("p (k n) -> p k n", k=KD)
            return w[:, ks, cols], high[xi % 2][:, ks, cols], low[u % RING1][:, ks, cols]

        def part_free(eng, xi):
            if xi >= 2:
                kind, i, n = split[xi - 2]
                if kind == "in":
                    eng.wait_ge(s["proj"], ends[i])
                else:
                    eng.wait_ge(s["gate"], 4 * i + 2 * n + 2)

        def high_part(act, xi, piece):
            if xi == 0 and piece < 2:
                act.wait_ge(s["first_half"], 16)
            else:
                arrived(act, where[split[xi]])
            if split[xi] == ("in", 4, 0):
                act.wait_ge(s["queries"], 16 * 4)
            part_free(act, xi)
            w, hi, lo = parts(xi, piece)
            nc.scalar.activation(hi, w, ACT.Copy).then_inc(s["high"], 1)

        def low_part(eng, ops, xi, piece):
            eng.wait_ge(s["high"], split_count(xi, (4 if xi else 2) * piece))
            w, hi, lo = parts(xi, piece)
            ops.tensor_tensor(lo, w, hi.bitcast(F32), ALU.subtract).then_inc(s["low"], 1)

        def branch_parts(b):
            u = where[("br", b, 0)]
            k = u % RING1
            return u, units[k][:, 0:2 * D].rearrange("p (c n) -> p c n", c=2), br_high[k][:], br_low[k][:]

        def moe_sems(tag):
            ns = "P Pw gat xT A B sg hid hTp STp hT ST Y y0 y1 comb".split()
            return {n: sem(f"s_{tag}_{n}") for n in ns}

        main, over = moe_sems("moe"), moe_sems("over")
        s_over_unit = [sem(f"s_over_unit{i}") for i in range(PAIR_UNITS)]
        s_over_slot = sem("s_over_slot")

        def arrived(eng, unit):
            eng.wait_ge(s_unit[unit % RING1], 16 * (unit // RING1 + 1))

        def slot_of(n):
            return EXPERT_SLOTS[n % RING]

        def unit_value(n, i=0):
            k = slot_of(n)
            first = EXPERT_SLOTS.index(k)
            return i * (16 * PAIR_UNITS * STEP // RING) + 16 * (slot_uses[k] + (n - first) // RING + 1)

        def free_of(n, i=0):
            p, r = divmod(n, PAIR_UNITS)
            p = i * STEP + p
            return ((main["A"], p + 1), (main["B"], p + 1), (main["Y"], 2 * p + 2))[r // 2]

        def expert_source(r, expert):
            w = (a["w1"], a["w3"], a["w2"])[r // 2]
            e = expert + r % 2
            rows = CE if r >= 4 else KD
            return w[0, bass.ds(e, 1)].rearrange("e (p k) n -> p (e k) n", p=P, k=rows)

        def unit_view(k, r):
            return units[k][:].rearrange("p (k n) -> p k n", k=(CE if r >= 4 else KD))

        def turned_part(b, c):
            return bank[c][:, 0:TOK] if b == D_ else bank[7][:, c * TOK:(c + 1) * TOK]

        def halves_turned(b, c):
            return b + 1 + (c if b == D_ else 0)

        def branch_bank(b, j):
            return bank[(6, 7, 2, 3)[j] if b == D_ else 6 + j % 2]

        block = ctx.enter_context(nc.Block())

        @block.sync
        def _(sp):
            sp.dma_start(x[:, 0, :], a["x"][0, 0:P, :]).then_inc(s_x[0], 16)
            sp.dma_start(cst[:, 0:C_GE], a["constants"][:, 0:C_GE]).then_inc(s["cst"], 16)
            sp.dma_start(x[:, 1, :], a["x"][0, P:TOK, :]).then_inc(s_x[1], 16)
            sp.dma_start(gmix[:], a["g_mix"][0].rearrange("(p k) -> p k", k=KD)).then_inc(s["cst"], 16)

            def small_loads():
                sp.dma_start(cst[:, C_GE:], a["constants"][:, C_GE:]).then_inc(s["tri"], 16)
                sp.dma_start(gffn[:], a["g_ffn"][0].rearrange("(p k) -> p k", k=KD)).then_inc(s["wr"], 16)
                sp.dma_start(wr[:, :, 0:NG], a["w_route_group"][0].rearrange("(p k) n -> p k n", k=KD)).then_inc(s["wr"], 16)
                sp.dma_start(wr[:, :, NG:], a["w_route_expert"][0].rearrange("(p k) n -> p k n", k=KD)).then_inc(s["wr"], 16)
                sp.dma_start(rbias[:, 0:NG], a["b_route_group"][0].partition_broadcast(P)).then_inc(s["wr"], 16)
                sp.dma_start(rbias[:, NG:], a["b_route_expert"][0].partition_broadcast(P)).then_inc(s["wr"], 16)
                sp.dma_start(relb[:], a["rel_bias"]).then_inc(s["small"], 16)
                sp.dma_start(onehot[:], a["bucket_onehot"]).then_inc(s["small"], 16)
                sp.dma_start(bmask[:], a["bias_mask"]).then_inc(s["small"], 16)
                for i, n in enumerate(("diff_lq1", "diff_lk1", "diff_lq2", "diff_lk2")):
                    sp.dma_start(lqk[:, i // 2, i % 2, :], a[n][0].partition_broadcast(P)).then_inc(s["small"], 16)
                sp.dma_start(sub[:], a["diff_subln"][0].partition_broadcast(P)).then_inc(s["small"], 16)
                sp.dma_start(sinks[:], a["swa_sinks"][0].partition_broadcast(P)).then_inc(s["small"], 16)

            def released(u):
                kind, i, n = stream[u]
                if kind == "in":
                    sp.wait_ge(s["proj"], ends[i])
                elif kind == "gate":
                    sp.wait_ge(s["gate"], 4 * i + 2 * n + 2)
                elif kind == "br":
                    sp.wait_ge(s["br"], 4 * i + 4)
                else:
                    sp.wait_ge(s["wo"], 2 + 2 * i)

            w_in = a["w_in"][0].rearrange("(p k) n -> p k n", k=KD)
            w_o = a["w_o"][0].rearrange("(p k) n -> p k n", k=KD)
            for u, (kind, i, n) in enumerate(stream):
                if u >= RING1:
                    released(u - RING1)
                dst = units[u % RING1]
                if kind == "in":
                    wide = min(BANK, 2816 - BANK * i)
                    src = w_in[:, :, BANK * i:BANK * i + wide]
                    dst = dst[:].rearrange("p (k n) -> p k n", k=KD)[:, :, BANK - wide:]
                    if i == 4:
                        for place_of, head in enumerate((0, 2, 1, 3)):
                            to = dst[:, :, TOK + place_of * HD:TOK + (place_of + 1) * HD]
                            head_cols = src[:, :, TOK + head * HD:TOK + (head + 1) * HD]
                            sp.dma_start(to, head_cols).then_inc(s["queries"], 16)
                        src, dst = src[:, :, 0:TOK], dst[:, :, 0:TOK]
                elif kind == "gate":
                    src = a["w_gate"][0, i].rearrange("(p k) n -> p k n", k=KD)[:, :, BANK * n:BANK * (n + 1)]
                    dst = dst[:].rearrange("p (k n) -> p k n", k=KD)
                elif kind == "br":
                    src = a["w_br"][0, i].rearrange("(c p) n -> p c n", p=P)
                    dst = dst[:, 0:2 * D].rearrange("p (c n) -> p c n", c=2)
                else:
                    src = w_o[:, :, BANK * i:BANK * (i + 1)]
                    dst = dst[:].rearrange("p (k n) -> p k n", k=KD)
                if u == 0:
                    sp.dma_start(dst[:, 0:4, :], src[:, 0:4, :]).then_inc(s["first_half"], 16)
                    dst, src = dst[:, 4:, :], src[:, 4:, :]
                sp.dma_start(dst, src).then_inc(s_unit[u % RING1], 16)
                if u == 1:
                    small_loads()

            def load_expert_unit(n, i=0, loop=False):
                if n < RING and not loop:
                    k = slot_of(n)
                    if k < RING1:
                        released(max(u for u in range(len(stream)) if u % RING1 == k))
                    elif k < RING1 + 2:
                        sp.wait_ge(s["wo"], 2 + 2 * (k - RING1))
                    elif k == RING1 + 2:
                        sp.wait_ge(s["hkl"], 2 * NT)
                    else:
                        sp.wait_ge(s["pv"], 16)
                else:
                    sp.wait_ge(*free_of(n - RING, i))
                p, r = divmod(n, PAIR_UNITS)
                sp.dma_start(unit_view(slot_of(n), r), expert_source(r, (i * STEP + p) * 2)).then_inc(s_unit[slot_of(n)], 16)

            head = 2 * PAIR_UNITS
            for n in range(RING):
                load_expert_unit(n)
            for half in range(2):
                for n in (RING, RING + 1):
                    if half == 0:
                        sp.wait_ge(s["half_up"], 1)
                    else:
                        sp.wait_ge(*free_of(n - RING))
                    part = (slice(None), slice(2 * half, 2 * half + 2), slice(None))
                    r = n % PAIR_UNITS
                    dst, src = unit_view(slot_of(n), r)[part], expert_source(r, 2)[part]
                    sp.dma_start(dst, src).then_inc(s_unit[slot_of(n)] if half else s["early"], 16)
            assert head == RING + 2
            span = STEP * PAIR_UNITS
            with sp.Fori(0, LOOPS) as i:
                for n in range(head, head + span):
                    load_expert_unit(n, i, loop=True)
            count = PAIRS * PAIR_UNITS
            for n in range(head + LOOPS * span, count - PAIR_UNITS):
                load_expert_unit(n)
            for i, (r, n_half, k0, k1) in enumerate(LAST_PIECES):
                cols = slice(n_half * BANK, (n_half + 1) * BANK)
                for n in (count - PAIR_UNITS + r, count - PAIR_UNITS + r + 1):
                    sp.wait_ge(*free_of(n - RING))
                    dst, src = unit_view(slot_of(n), r), expert_source(r, PAIRS * 2 - 2 + n % 2)
                    sp.dma_start(dst[:, k0:k1, cols], src[:, k0:k1, cols]).then_inc(s_last[i], 16)

            sp.wait_ge(s["pos"], 1)
            sp.dma_start(gfin[:], a["g_final"].partition_broadcast(P)).then_inc(s["late"], 16)

            sp.wait_ge(s["flag"], 1)
            crowded = sp.value_load(flag[0:1, 0:1])
            with sp.If(crowded > CAP):
                sp.wait_ge(main["Y"], 2 * PAIRS)
                with sp.Fori(0, BLOCKS - 1) as b:
                    with sp.Fori(0, PAIRS) as p:
                        sp.wait_ge(over["comb"], b * PAIRS + p + 1)
                        for r in range(PAIR_UNITS):
                            sp.dma_start(unit_view(r, r), expert_source(r, p * 2)).then_inc(s_over_unit[r], 16)
                sp.wait_ge(over["comb"], (BLOCKS - 1) * PAIRS + 1)

            for t in range(NT):
                sp.wait_ge((s["scaledD"], s["scaledA"])[t], 1)
                sp.dma_start(out[0, t * P:(t + 1) * P, :], xg[:, t, :]).then_inc(s["stored"], 16)
            sp.wait_ge(s["stored"], 16 * NT)

        @block.gpsimd
        def _(pool):
            pool.wait_ge(s["dvec"], 1)
            pool.dma_start(dram_vec, dvec[:]).then_inc(s["scratch"], 16)
            pool.wait_ge(s["scratch"], 16)
            pool.dma_start(bias[:], bass.AP(dram_vec.tensor, 0, [[1, P], [MAP, 12], [1, TOK]])).then_inc(s["biasT"], 16)
            for b in range(4):
                u, w, hi, lo = branch_parts(b)
                pool.wait_ge(s["brh"], b + 1)
                nc.gpsimd.tensor_tensor(lo, w, hi.bitcast(F32), ALU.subtract).then_inc(s["brl"], 1)
            pool.wait_ge(s["low"], split_count(14, KD - 1))
            for half in range(2):
                low_part(pool, nc.gpsimd, 15, half)
            for t in range(NT):
                for n in range(2):
                    pool.wait_ge(s["hkh"], 2 * t + n + 1)
                    to = (rest, hk_3)[n][:, t, :, :]
                    nc.gpsimd.tensor_tensor(to, rest[:, t, :, :], (hk_1, hk_2)[n][:, t, :, :],
                                            ALU.subtract).then_inc(s["hkl"], 1)
            pool.wait_ge(s["late"], 16)
            for t in range(NT):
                pool.wait_ge(s["x2"], t + 1)
                nc.gpsimd.tensor_tensor(xg[:, t, 0:BANK], x[:, t, 0:BANK], gfin[:, 0:BANK], ALU.mult).then_inc(s["xg"], 1)

        @block.scalar
        def _(act):
            chain = [0]

            def link(ins):
                chain[0] += 1
                ins.then_inc(s["chain_a"], 1)
                act.wait_ge(s["chain_a"], chain[0])

            def root(n, src, scale, dst, done):
                act.wait_ge(s["sums"], n)
                nc.scalar.activation(dst, src, ACT.Sqrt, bias=eps, scale=scale).then_inc(done, 1)

            act.wait_ge(s["warm"], 3)
            link(nc.scalar.activation(warm, warm, ACT.Sqrt))
            root(1, ss[:, 0:1], 1.0 / D, rs[:, 0:1], s["rms"])
            act.wait_ge(s_x[1], 16)
            link(nc.scalar.activation(merged[:, 1, :], x[:, 1, :], ACT.Square, accum_out=ss[:, 1:2]))
            nc.scalar.activation(rs[:, 1:2], ss[:, 1:2], ACT.Sqrt, bias=eps, scale=1.0 / D).then_inc(s["rms"], 1)
            act.wait_ge(s["cst"], 32)
            def block_out(i):
                unit, col, kind, to, scale = blocks[i]
                src = bank[i % 8][:, 0:TOK]
                if kind in "TK":
                    return qk[:, to, :], src, scale
                if kind == "V":
                    return vv[:, to[1], V_AT[to[0]]:V_AT[to[0]] + 256], src, scale
                return vv[:, :, V_AT[3]:V_AT[3] + P], src.rearrange("p (t n) -> p t n", t=NT), scale

            high_part(act, 0, 0)
            for j in range(4):
                act.wait_ge(s["tr1"], j + 1)
                for k in (2 * j, 2 * j + 1):
                    last = nc.scalar.activation(hT_hi[:, k, :], bank[4 + j][:, (k % 2) * TOK:(k % 2 + 1) * TOK], ACT.Copy,
                                                scale=gmix[:, k:k + 1])
                last.then_inc(s["hTh"], 1)
                if j < 3:
                    high_part(act, 0, j + 1)
            for half in range(2):
                high_part(act, 1, half)
            act.wait_ge(s["lamx"], 1)
            nc.scalar.activation(lam[:, 2:4], lam[:, 0:2], ACT.Exp).then_inc(s["lame"], 1)
            for u in range(6):
                for i in range(ends[u - 1] if u else 0, ends[u]):
                    if i % 2 == 0:
                        act.wait_ge(s["proj"], i + 1)
                        dst, src, scale = block_out(i)
                        nc.scalar.activation(dst, src, ACT.Copy, scale=scale).then_inc(s["projA"], 1)
                for half in range(2 if u < 5 else 0):
                    high_part(act, u + 2, half)

            def exponentials(st):
                b, h = divmod(st, 4)
                par = st % 2
                pr = prob[par]
                if b == D_:
                    act.wait_ge(s["norm"], h + 1)
                    for t in range(NT):
                        nc.scalar.activation(esink[:, par, t:t + 1], sinks[:, h:h + 1], ACT.Exp,
                                             bias=nm[:, par, 0, t:t + 1])
                else:
                    act.wait_ge(s["sread"], st + 1)
                if b == C_BR:
                    link(nc.scalar.activation(pr[:, 1, :], pr[:, 0, :], ACT.Abs))
                    link(nc.scalar.activation(pr[:, 1, :], pr[:, 1, :], ACT.Exp, scale=-1.0))
                    return
                for mp in range(2 if b == B_ else 1):
                    for t, (c0, c1) in enumerate(TILE_COLS):
                        last = nc.scalar.activation(pr[:, mp, c0:c1], pr[:, mp, c0:c1], ACT.Exp, scale=-1.0,
                                                    bias=nm[:, par, mp, t:t + 1], accum_out=lsum[:, par, mp, t:t + 1])
                last.then_inc(s["maps"] if b == B_ else s["probs"], 1)

            def keys_on_rows(st):
                if st >= 1:
                    act.wait_ge(s["pv"], st)
                if st // 4 == C_BR:
                    act.wait_ge(s["dd"], st % 4 + 1)
                    nc.scalar.activation(pT[:], prob[st % 2][:, 0, :], ACT.Exp).then_inc(s["pt"], 1)
                else:
                    act.wait_ge(s["ptps"], st + 1)
                    nc.scalar.activation(pT[:], bank[2][:, 0:MAP], ACT.Copy).then_inc(s["pt"], 1)

            def turned_high(b, c=1):
                act.wait_ge(s["oTps"], halves_turned(b, c))
                if b >= 1:
                    act.wait_ge(s["br"], 4 * b)
                if b == D_:
                    nc.scalar.activation(oT_hi[:, c, :], turned_part(b, c), ACT.Copy).then_inc(s["oTh"], 1)
                else:
                    nc.scalar.activation(oT_hi[:].rearrange("p c t -> p (c t)"), bank[7][:], ACT.Copy).then_inc(s["oTh"], 1)

            exponentials(0)
            for st in range(16):
                b, h = divmod(st, 4)
                ahead = st + 1 if st < 15 else None
                keys_on_rows(st)
                if b == C_BR and h == 0:
                    turned_high(1)
                if ahead:
                    exponentials(ahead)
                if b in (B_, D_) and h == 0:
                    turned_high(b - 1)
                if ahead and ahead // 4 == C_BR:
                    l = prob[ahead % 2][:, 1, :]
                    nc.scalar.activation(l, l, ACT.Ln, bias=unit1).then_inc(s["logs"], 1)
                if st < 15:
                    high_part(act, 7 + st // 2, st % 2)
                if st == 14:
                    high_part(act, 14, 1)
                if st in (3, 7, 11, 13):
                    u, w, hi, lo = branch_parts(st // 4)
                    arrived(act, u)
                    nc.scalar.activation(hi, w, ACT.Copy).then_inc(s["brh"], 1)
                if st == 15:
                    turned_high(D_, 0)
                n, t = divmod(h, 2)
                act.wait_ge(s["gate"], st + 1)
                if b >= 1:
                    act.wait_ge(s["mrg"], 4 * (b - 1) + h + 1)
                nc.scalar.activation(sig[:, t, n * BANK:(n + 1) * BANK], bank[4 + st % 2][:], ACT.Tanh,
                                     scale=0.5).then_inc(s["tanh"], 1)
                if st == 7:
                    act.wait_ge(s["bsq"], 1)
                    nc.scalar.activation(lsum[:].rearrange("p a b t -> p (a b t)"), lsum[:].rearrange("p a b t -> p (a b t)"),
                                         ACT.Sqrt, bias=eps, scale=1.0 / HD).then_inc(s["brms"], 1)
                    link(nc.scalar.activation(warm, unit1, ACT.Exp))
            turned_high(D_, 1)

            for half in range(2):
                high_part(act, 15, half)
            for j in range(4):
                t, i = divmod(j, 2)
                act.wait_ge(s["mTps"], j + 1)
                nc.scalar.activation(hT_hi[:, 4 * i:4 * i + 4, t * P:(t + 1) * P],
                                     bank[j][:].rearrange("p (k t) -> p k t", k=4), ACT.Copy, scale=0.5).then_inc(s["mTh"], 1)
            link(nc.scalar.activation(warm, unit1, ACT.Sqrt))

            def second_part(t):
                act.wait_ge(s["hkl"], 2 * t + 1)
                nc.scalar.activation(hk_2[:, t, :, :], rest[:, t, :, :], ACT.Copy).then_inc(s["hkh"], 1)

            for t in range(NT):
                act.wait_ge(s["x1"], t + 1)
                link(nc.scalar.activation(y[:], x[:, t, :], ACT.Square, accum_out=ss[:, t:t + 1]))
                nc.scalar.activation(rs[:, t:t + 1], ss[:, t:t + 1], ACT.Sqrt, bias=eps, scale=1.0 / D).then_inc(s["rms"], 1)
                if t == 1:
                    second_part(0)
                act.wait_ge(s["rs"], t + 1)
                link(nc.scalar.activation(rest[:, t, :, :], x[:, t, :].rearrange("p (q k) -> p k q", k=KD), ACT.Copy,
                                          scale=rs[:, t:t + 1]))
                nc.scalar.activation(hk_1[:, t, :, :], rest[:, t, :, :], ACT.Copy).then_inc(s["hkh"], 1)
            act.wait_ge(s["eg"], 1)
            nc.scalar.activation(eg[:], ge[:], ACT.Exp).then_inc(s["e2"], 1)
            second_part(1)
            act.wait_ge(s["eg"], 2)
            nc.scalar.activation(m[:, 6, :], m[:, 5, :], ACT.Exp).then_inc(s["e2"], 1)

            def experts(z, p, first=False):
                act.wait_ge(z["A"], p + 1)
                if not first:
                    act.wait_ge(z["hid"], p)
                nc.scalar.activation(sg[:], bank[4][:], ACT.Silu).then_inc(z["sg"], 1)
                act.wait_ge(z["hTp"], p + 1)
                if not first:
                    act.wait_ge(z["Y"], 2 * p)
                nc.scalar.activation(hidT[:].rearrange("p c q -> p (c q)"), bank[4][:], ACT.Copy).then_inc(z["hT"], 1)
                act.wait_ge(z["Y"], 2 * p + 1)
                if not first:
                    act.wait_ge(z["comb"], p)
                nc.scalar.activation(y[:, 0:BANK], bank[6][:], ACT.Copy).then_inc(z["y0"], 1)

            experts(main, 0, first=True)
            experts(main, 1)
            with act.Fori(0, LOOPS) as i:
                for j in range(STEP):
                    experts(main, i * STEP + PEEL + j)
            for p in range(PEEL + LOOPS * STEP, PAIRS):
                experts(main, p)

            act.wait_ge(s["flag"], 1)
            crowded = act.value_load(flag[0:1, 0:1])
            with act.If(crowded > CAP):
                with act.Fori(0, BLOCKS - 1) as b:
                    with act.Fori(0, PAIRS) as p:
                        q = b * PAIRS + p
                        act.wait_ge(over["comb"], q + 1)
                        experts(over, q, first=True)
                act.wait_ge(over["comb"], (BLOCKS - 1) * PAIRS + 1)
            link(nc.scalar.activation(warm, warm, ACT.Sqrt))
            for n in range(2):
                for t in range(NT):
                    act.wait_ge(s["x2"], 2 * n + t + 1)
                    cols = slice(n * BANK, (n + 1) * BANK)
                    nc.scalar.activation(merged[:, t, cols], x[:, t, cols], ACT.Square,
                                         accum_out=ss4[:, t, n:n + 1]).then_inc(s["squared"], 1)
            root(NT, ss[:], 1.0 / D, rs[:], s["rms"])
            act.wait_ge(s["rs"], NT + 1)
            nc.scalar.activation(xg[:, 1, :], xg[:, 1, :], ACT.Copy, scale=rs[:, 1:2]).then_inc(s["scaledA"], 1)

        @block.vector
        def _(dve):
            chain = [0]

            def link(ins):
                chain[0] += 1
                ins.then_inc(s["chain_d"], 1)
                dve.wait_ge(s["chain_d"], chain[0])

            def squares(t, junk):
                nc.vector.tensor_tensor_reduce(out=junk, in0=x[:, t, :], in1=x[:, t, :], scale=1.0, scalar=0.0,
                                               op0=ALU.mult, op1=ALU.add, accum_out=ss[:, t:t + 1]).then_inc(s["sums"], 1)

            def normalise(t, n, done):
                dve.wait_ge(s["rms"], n)
                link(nc.vector.reciprocal(rs[:, t:t + 1], rs[:, t:t + 1]))
                nc.vector.tensor_scalar(hk[:, t, :, :], x[:, t, :].rearrange("p (q k) -> p k q", k=KD),
                                        rs[:, t:t + 1], None, ALU.mult).then_inc(done, 1)

            for tile, value in ((eps, EPS), (unit1, 1.0), (warm, 1.0)):
                nc.vector.memset(tile, value).then_inc(s["warm"], 1)
            dve.wait_ge(s_x[0], 16)
            squares(0, hk[:, 0].rearrange("p k q -> p (k q)"))
            for t in range(NT):
                normalise(t, t + 1, s["hk"])

            for j in range(4):
                low_part(dve, nc.vector, 0, j)
                dve.wait_ge(s["hTh"], j + 1)
                for k in (2 * j, 2 * j + 1):
                    last = nc.vector.scalar_tensor_tensor(out=hT_lo[:, k, :], in0=bank[4 + j][:, (k % 2) * TOK:(k % 2 + 1) * TOK],
                                                          scalar=gmix[:, k:k + 1], in1=hT_hi[:, k, :].bitcast(F32),
                                                          op0=ALU.mult, op1=ALU.subtract)
                last.then_inc(s["hTl"], 1)
            for half in range(2):
                low_part(dve, nc.vector, 1, half)
            dve.wait_ge(s["small"], 16 * 9)
            dve.wait_ge(s["table"], 1)
            nc.vector.tensor_tensor(dvec[:], bank[7][0:12, 0:MAP], bmask[:], ALU.add).then_inc(s["dvec"], 1)
            dve.wait_ge(s["tri"], 16)
            nc.vector.tensor_scalar(before_bf[:], at_or_after, -1.0, 1.0, ALU.mult, ALU.add).then_inc(s["bf"], 1)
            nc.vector.memset(ones_bf[:], 1.0).then_inc(s["bf"], 1)
            link(nc.vector.tensor_tensor(lqk[:, :, 0, :], lqk[:, :, 0, :], lqk[:, :, 1, :], ALU.mult))
            nc.vector.tensor_reduce(lam[:, 0:2], lqk[:, :, 0, :], AX, ALU.add).then_inc(s["lamx"], 1)
            link(nc.vector.tensor_scalar(sub[:], sub[:], 1.0 - LAM_INIT, None, ALU.mult))
            link(nc.vector.tensor_scalar(nsink[:], sinks[:], -1.0, None, ALU.mult))
            dve.wait_ge(s["lame"], 1)
            link(nc.vector.tensor_tensor(lam[:, 4:5], lam[:, 3:4], lam[:, 2:3], ALU.subtract))
            link(nc.vector.tensor_scalar(lam[:, 5:6], lam[:, 4:5], -LAM_INIT, None, ALU.add))
            neg_lam = lam[:, 5:6]

            def block_out(i):
                unit, col, kind, to, scale = blocks[i]
                src = bank[i % 8][:, 0:TOK]
                if kind in "TK":
                    return qk[:, to, :], src, scale
                if kind == "V":
                    return vv[:, to[1], V_AT[to[0]]:V_AT[to[0]] + 256], src, scale
                return vv[:, :, V_AT[3]:V_AT[3] + P], src.rearrange("p (t n) -> p t n", t=NT), scale

            for u in range(6):
                for i in range(ends[u - 1] if u else 0, ends[u]):
                    if i % 2:
                        dve.wait_ge(s["proj"], i + 1)
                        dst, src, scale = block_out(i)
                        nc.vector.tensor_scalar(dst, src, scale, None, ALU.mult).then_inc(s["projD"], 1)
                for half in range(2 if u < 5 else 0):
                    low_part(dve, nc.vector, u + 2, half)

            dve.wait_ge(s["biasT"], 16)

            def biased(par, mp, src, table):
                for t, (c0, c1) in enumerate(TILE_COLS):
                    keys = bias[:, table, 127::-1] if t == 0 else bias[:, table, 255::-1]
                    last = nc.vector.tensor_tensor_reduce(out=prob[par][:, mp, c0:c1], in0=src[:, c0:c1], in1=keys,
                                                          scale=1.0, scalar=4.0 * NEG, op0=ALU.add, op1=ALU.min,
                                                          accum_out=nm[:, par, mp, t:t + 1])
                return last

            def front(st):
                b, h = divmod(st, 4)
                par = st % 2
                dve.wait_ge(s["scores"], st + 1)
                if st >= 2:
                    dve.wait_ge(s["pt"], st - 1)
                if b == B_:
                    biased(par, 0, bank[0], 4 + h)
                    biased(par, 1, bank[1], 4 + h).then_inc(s["sread"], 1)
                elif b == C_BR:
                    nc.vector.tensor_tensor(prob[par][:, 0, :], bank[par][:, 0:MAP], cst[:, C_DIAG:C_DIAG + MAP],
                                            ALU.add).then_inc(s["sread"], 1)
                else:
                    biased(par, 0, bank[par], h if b == A_ else 8 + h).then_inc(s["sread"], 1)
                    if b == D_:
                        dve.wait_ge(s["sread"], st + 1)
                        nc.vector.tensor_scalar(nm[:, par, 0, :], nm[:, par, 0, :], nsink[:, h:h + 1], None,
                                                ALU.min).then_inc(s["norm"], 1)

            def difference(st):
                par = st % 2
                pr = prob[par]
                dve.wait_ge(s["maps"], st % 4 + 1)
                link(nc.vector.reciprocal(lsum[:, par, :, :], lsum[:, par, :, :]))
                link(nc.vector.tensor_scalar(lsum[:, par, 1, :], lsum[:, par, 1, :], neg_lam, None, ALU.mult))
                for t, (c0, c1) in enumerate(TILE_COLS):
                    link(nc.vector.tensor_scalar(pr[:, 1, c0:c1], pr[:, 1, c0:c1], lsum[:, par, 1, t:t + 1],
                                                 None, ALU.mult))
                for t, (c0, c1) in enumerate(TILE_COLS):
                    last = nc.vector.scalar_tensor_tensor(out=pr[:, 0, c0:c1], in0=pr[:, 0, c0:c1],
                                                          scalar=lsum[:, par, 0, t:t + 1], in1=pr[:, 1, c0:c1],
                                                          op0=ALU.mult, op1=ALU.add)
                last.then_inc(s["probs"], 1)

            def softplus(st):
                pr = prob[st % 2]
                dve.wait_ge(s["logs"], st % 4 + 1)
                nc.vector.scalar_tensor_tensor(out=pr[:, 1, :], in0=pr[:, 0, :], scalar=0.0, in1=pr[:, 1, :],
                                               op0=ALU.max, op1=ALU.add).then_inc(s["probs"], 1)

            def log_weights(st):
                pr = prob[st % 2]
                dve.wait_ge(s["ptps"], st + 1)
                nc.vector.tensor_tensor(pr[:, 0, :], pr[:, 0, :], bank[2][:, 0:MAP], ALU.subtract).then_inc(s["dd"], 1)

            def head_output(st):
                b, h = divmod(st, 4)
                par = st % 2
                if b in (A_, D_):
                    dve.wait_ge(s["probs"], st + 1)
                    if b == D_:
                        link(nc.vector.tensor_tensor(lsum[:, par, 0, :], lsum[:, par, 0, :], esink[:, par, :], ALU.add))
                    link(nc.vector.reciprocal(lsum[:, par, 0, :], lsum[:, par, 0, :]))
                    dve.wait_ge(s["pv"], st + 1)
                    for t in range(NT):
                        last = nc.vector.tensor_scalar(o[:, t, h * HD:(h + 1) * HD], bank[3][:, t * HD:(t + 1) * HD],
                                                       lsum[:, par, 0, t:t + 1], None, ALU.mult)
                else:
                    dve.wait_ge(s["pv"], st + 1)
                    last = nc.vector.tensor_copy(o[:, :, h * HD:(h + 1) * HD],
                                                 bank[3][:, 0:P].rearrange("p (t d) -> p t d", t=NT))
                last.then_inc(s["oev"], 1)

            heads = o[:].rearrange("p t (h d) -> p (t h) d", d=HD)
            rms = lsum[:].rearrange("p a b t -> p (a b t)")

            def head_squares_summed():
                dve.wait_ge(s["oev"], 8)
                sq = head_squares[:].rearrange("p c (g d) -> p (c g) d", d=HD)
                link(nc.vector.tensor_tensor(sq, heads, heads, ALU.mult))
                nc.vector.tensor_reduce(rms, sq, AX, ALU.add).then_inc(s["bsq"], 1)

            def head_norms_end():
                dve.wait_ge(s["brms"], 1)
                link(nc.vector.reciprocal(rms, rms))
                link(nc.vector.tensor_tensor(heads, heads, rms.unsqueeze(2).broadcast_to([P, 8, HD]), ALU.mult))
                nc.vector.tensor_tensor(heads, heads, sub[:].unsqueeze(1).broadcast_to([P, 8, HD]),
                                        ALU.mult).then_inc(s["ob"], 1)

            def turned(b, c=1):
                dve.wait_ge(s["oTh"], halves_turned(b, c))
                if b == D_:
                    nc.vector.tensor_tensor(oT_lo[:, c, :], turned_part(b, c), oT_hi[:, c, :].bitcast(F32),
                                            ALU.subtract).then_inc(s["oTs"], 1)
                else:
                    nc.vector.tensor_tensor(oT_lo[:].rearrange("p c t -> p (c t)"), bank[7][:],
                                            oT_hi[:].bitcast(F32).rearrange("p c t -> p (c t)"),
                                            ALU.subtract).then_inc(s["oTs"], 1)

            def merge(b, j):
                n, t = divmod(LAST_ORDER[j] if b == D_ else j, 2)
                cols = slice(n * BANK, (n + 1) * BANK)
                chunk = sig[:, t, cols]
                dve.wait_ge(s["br"], 4 * b + j + 1)
                dve.wait_ge(s["tanh"], 16 if b == D_ else 4 * b + j + 1)
                to = merged[:, t, cols] if b == 0 else chunk
                gated = nc.vector.scalar_tensor_tensor(out=to, in0=chunk, scalar=1.0, in1=branch_bank(b, j)[:],
                                                       op0=ALU.add, op1=ALU.mult)
                if b == 0:
                    gated.then_inc(s["mrg"], 1)
                else:
                    link(gated)
                    nc.vector.tensor_tensor(merged[:, t, cols], merged[:, t, cols], chunk, ALU.add).then_inc(s["mrg"], 1)

            front(0)
            for st in range(16):
                b, h = divmod(st, 4)
                ahead = st + 1 if st < 15 else None
                if ahead:
                    front(ahead)
                if b == C_BR:
                    log_weights(st)
                if b >= 1 and h == 0:
                    turned(b - 1)
                if ahead and ahead // 4 == B_:
                    difference(ahead)
                if ahead == 8:
                    softplus(ahead)
                if st == 15:
                    low_part(dve, nc.vector, 14, 1)
                    turned(D_, 0)
                    merge(b - 1, h)
                head_output(st)
                if b >= 1 and st < 15:
                    merge(b - 1, h)
                if ahead and ahead // 4 == C_BR and ahead != 8:
                    softplus(ahead)
                if st == 7:
                    head_squares_summed()
                if st == 7:
                    low_part(dve, nc.vector, 10, 1)
                    head_norms_end()
                elif st < 15:
                    low_part(dve, nc.vector, 7 + st // 2, st % 2)

            def merged_low(t):
                for i in range(2):
                    dve.wait_ge(s["mTh"], 2 * t + i + 1)
                    ks, rows = slice(4 * i, 4 * i + 4), slice(t * P, (t + 1) * P)
                    nc.vector.scalar_tensor_tensor(out=hT_lo[:, ks, rows], in0=bank[2 * t + i][:].rearrange("p (k t) -> p k t", k=4),
                                                   scalar=0.5, in1=hT_hi[:, ks, rows].bitcast(F32),
                                                   op0=ALU.mult, op1=ALU.subtract).then_inc(s["mTl"], 1)

            turned(D_, 1)
            for nth in range(3):
                merge(3, nth)
            merged_low(0)
            merge(3, 3)
            merged_low(1)
            dve.wait_ge(s["wr"], 16 * 5)
            def add_product(t, n):
                dve.wait_ge(s["wo"], 2 * n + t + 1)
                cols = slice(n * BANK, (n + 1) * BANK)
                return nc.vector.tensor_tensor(x[:, t, cols], x[:, t, cols], bank[4 + 2 * t + n][:], ALU.add)

            for t in range(NT):
                link(add_product(t, 0))
            for t in range(NT):
                add_product(t, 1).then_inc(s["x1"], 1)
                for i in range(2):
                    if i == t:
                        dve.wait_ge(s["rms"], NT + t + 1)
                        nc.vector.reciprocal(rs[:, t:t + 1], rs[:, t:t + 1]).then_inc(s["rs"], 1)
                    dve.wait_ge(s["h2ps"], 2 * t + i + 1)
                    ks = slice(4 * i, 4 * i + 4)
                    nc.vector.tensor_tensor(h2T[:, ks, t * P:(t + 1) * P], bank[2 * t + i][:].rearrange("p (k t) -> p k t", k=4),
                                            gffn[:, ks].unsqueeze(2).broadcast_to([P, 4, P]), ALU.mult).then_inc(s["h2T"], 1)

            V = nc.vector
            t4 = lambda ap: ap.unsqueeze(2).broadcast_to([P, NT, NG])
            t32 = lambda ap: ap.unsqueeze(2).broadcast_to([P, NT, NE])
            from_end = lambda n: cst[:, C_IOTA:C_IOTA + n].unsqueeze(1).broadcast_to([P, NT, n])
            R = NG + NE
            for t in range(NT):
                dve.wait_ge(s["lg_ps"], t + 1)
                dve.wait_ge(s["rs"], t + 1)
                link(V.scalar_tensor_tensor(out=lg[:, t, :], in0=bank[4 + t][:, 0:R], scalar=rs[:, t:t + 1],
                                            in1=rbias[:], op0=ALU.mult, op1=ALU.add))
            link(V.tensor_reduce(m[:, 0, :], lg[:, :, 0:NG], AX, ALU.max))
            V.tensor_tensor(ge[:], lg[:, :, 0:NG], t4(m[:, 0, :]), ALU.subtract).then_inc(s["eg"], 1)
            dve.wait_ge(s["eg"], 1)
            link(V.scalar_tensor_tensor(out=cg[:], in0=ge[:], scalar=0.0, in1=from_end(NG), op0=ALU.is_equal, op1=ALU.mult))
            link(V.tensor_reduce(m[:, 1, :], cg[:], AX, ALU.max))
            link(V.tensor_tensor(ohg[:], cg[:], t4(m[:, 1, :]), ALU.is_equal))
            link(V.tensor_scalar(ohg[:], ohg[:], -1.0, NEG, ALU.add, ALU.mult))
            for t in range(NT):
                last = V.tensor_tensor(em[:, t, :].rearrange("p (g e) -> p g e", g=NG),
                                       lg[:, t, NG:].rearrange("p (g e) -> p g e", g=NG),
                                       ohg[:, t, :].unsqueeze(2).broadcast_to([P, NG, EPG]), ALU.add)
            link(last)
            for k, oh in ((3, oh1), (4, oh2)):
                link(V.tensor_reduce(m[:, k, :], em[:], AX, ALU.max))
                for t in range(NT):
                    last = V.scalar_tensor_tensor(out=ce[:, t, :], in0=em[:, t, :], scalar=m[:, k, t:t + 1],
                                                  in1=cst[:, C_IOTA:C_IOTA + NE], op0=ALU.is_equal, op1=ALU.mult)
                link(last)
                link(V.tensor_reduce(m[:, 7, :], ce[:], AX, ALU.max))
                link(V.tensor_tensor(oh[:], ce[:], t32(m[:, 7, :]), ALU.is_equal))
                if k == 3:
                    link(V.scalar_tensor_tensor(out=em[:], in0=oh[:], scalar=-NEG, in1=em[:],
                                                op0=ALU.mult, op1=ALU.add))
            V.tensor_tensor(asg[:], oh1[:], oh2[:], ALU.add).then_inc(s["asg"], 1)
            V.tensor_tensor(m[:, 5, :], m[:, 4, :], m[:, 3, :], ALU.subtract).then_inc(s["eg"], 1)
            dve.wait_ge(s["pos"], 1)
            link(V.scalar_tensor_tensor(out=slot[:], in0=bank[5][:, 0:NT * NE].rearrange("p (t e) -> p t e", t=NT),
                                        scalar=1.0, in1=asg[:], op0=ALU.add, op1=ALU.mult))
            link(V.tensor_scalar(slot[:], slot[:], -1.0, None, ALU.add))

            def picks(z, p, pair, first=False):
                if not first:
                    dve.wait_ge(z["gat"], 2 * p)
                    dve.wait_ge(z["Pw"], p)
                V.tensor_tensor(pick[:].rearrange("p t (g s) -> p t g s", g=2),
                                slot[:, :, bass.ds(2 * pair, 2)].unsqueeze(3).broadcast_to([P, NT, 2, CAP]),
                                slot_no.unsqueeze(1).unsqueeze(1).broadcast_to([P, NT, 2, CAP]),
                                ALU.is_equal).then_inc(z["P"], 1)

            def weighted(z, p, pair, first=False):
                dve.wait_ge(z["P"], p + 1)
                if not first:
                    dve.wait_ge(z["STp"], p)
                V.tensor_tensor(pickw[:].rearrange("p t (g s) -> p t g s", g=2),
                                pick[:].rearrange("p t (g s) -> p t g s", g=2),
                                gate[:, :, bass.ds(2 * pair, 2)].unsqueeze(3).broadcast_to([P, NT, 2, CAP]),
                                ALU.mult).then_inc(z["Pw"], 1)

            def gathered(z, p, first=False):
                for half in range(2):
                    dve.wait_ge(z["gat"], 2 * p + half + 1)
                    if not first:
                        dve.wait_ge(z["B"], p)
                    V.tensor_tensor(xT[:, 4 * half:4 * half + 4, :],
                                    bank[6 + half][:].rearrange("p (k q) -> p k q", k=4),
                                    gffn[:, 4 * half:4 * half + 4].unsqueeze(2).broadcast_to([P, 4, P]),
                                    ALU.mult).then_inc(z["xT"], 1)

            def hidden(z, p, first=False):
                dve.wait_ge(z["sg"], p + 1)
                dve.wait_ge(z["B"], p + 1)
                if not first:
                    dve.wait_ge(z["hTp"], p)
                V.tensor_tensor(hid[:], sg[:].rearrange("p (q c) -> p c q", c=CE),
                                bank[5][:].rearrange("p (q c) -> p c q", c=CE), ALU.mult).then_inc(z["hid"], 1)

            def outputs(z, p, first=False):
                dve.wait_ge(z["STp"], p + 1)
                if not first:
                    dve.wait_ge(z["comb"], p)
                V.tensor_copy(pickT[:].rearrange("p t q -> p (t q)"), bank[5][:, 0:TOK]).then_inc(z["ST"], 1)
                dve.wait_ge(z["Y"], 2 * p + 2)
                V.tensor_copy(y[:, BANK:], bank[7][:]).then_inc(z["y1"], 1)

            def experts(p, first=False, last=False):
                weighted(main, p, p, first)
                if not last:
                    picks(main, p + 1, p + 1)
                hidden(main, p, first)
                if not last:
                    gathered(main, p + 1)
                outputs(main, p, first)

            picks(main, 0, 0, first=True)
            link(V.tensor_reduce(most[:], bank[5][:, NT * NE:(NT + 1) * NE], AX, ALU.max))
            V.tensor_copy(flag[:], most[:]).then_inc(s["flag"], 1)
            dve.wait_ge(s["e2"], 2)
            link(V.tensor_reduce(m[:, 2, :], eg[:], AX, ALU.add))
            link(V.reciprocal(m[:, 2, :], m[:, 2, :]))
            link(V.tensor_scalar(m[:, 7, :], m[:, 6, :], 1.0, None, ALU.add))
            link(V.reciprocal(m[:, 7, :], m[:, 7, :]))
            link(V.tensor_tensor(m[:, 8, :], m[:, 7, :], m[:, 2, :], ALU.mult))
            link(V.tensor_tensor(m[:, 9, :], m[:, 8, :], m[:, 6, :], ALU.mult))
            link(V.tensor_tensor(gate[:], oh1[:], t32(m[:, 8, :]), ALU.mult))
            link(V.tensor_tensor(ce[:], oh2[:], t32(m[:, 9, :]), ALU.mult))
            link(V.tensor_tensor(gate[:], gate[:], ce[:], ALU.add))
            gathered(main, 0, first=True)
            experts(0, first=True)
            experts(1)
            with dve.Fori(0, LOOPS) as i:
                for j in range(STEP):
                    experts(i * STEP + PEEL + j)
            for p in range(PEEL + LOOPS * STEP, PAIRS):
                experts(p, last=(p == PAIRS - 1))

            dve.wait_ge(s["flag"], 1)
            crowded = dve.value_load(flag[0:1, 0:1])
            with dve.If(crowded > CAP):
                with dve.Fori(0, BLOCKS - 1) as b:
                    dve.wait_ge(over["comb"], b * PAIRS + 1)
                    V.tensor_scalar(slot[:], slot[:], -float(CAP), None, ALU.add).then_inc(s_over_slot, 1)
                    with dve.Fori(0, PAIRS) as p:
                        q = b * PAIRS + p
                        dve.wait_ge(over["comb"], q + 1)
                        dve.wait_ge(s_over_slot, b + 1)
                        picks(over, q, p, first=True)
                        weighted(over, q, p, first=True)
                        gathered(over, q, first=True)
                        hidden(over, q, first=True)
                        outputs(over, q, first=True)
                dve.wait_ge(over["comb"], (BLOCKS - 1) * PAIRS + 1)

            dve.wait_ge(s["late"], 16)
            for n in range(2):
                cols = slice(n * BANK, (n + 1) * BANK)
                for t in range(NT):
                    dve.wait_ge(s["total"], 2 * n + t + 1)
                    V.tensor_tensor(x[:, t, cols], x[:, t, cols], bank[2 * t + n][:], ALU.add).then_inc(s["x2"], 1)
            dve.wait_ge(s["x2"], 2 * NT)
            link(V.tensor_tensor(xg[:, 0, BANK:], x[:, 0, BANK:], gfin[:, BANK:], ALU.mult))
            dve.wait_ge(s["squared"], 4)
            V.tensor_tensor(ss[:], ss4[:, :, 0], ss4[:, :, 1], ALU.add).then_inc(s["sums"], 1)
            V.tensor_tensor(xg[:, 1, BANK:], x[:, 1, BANK:], gfin[:, BANK:], ALU.mult).then_inc(s["xg"], 1)
            dve.wait_ge(s["xg"], NT + 1)
            dve.wait_ge(s["rms"], 2 * NT + 1)
            V.reciprocal(rs[:], rs[:]).then_inc(s["rs"], 1)
            dve.wait_ge(s["rs"], NT + 1)
            V.tensor_scalar(xg[:, 0, :], xg[:, 0, :], rs[:, 0:1], None, ALU.mult).then_inc(s["scaledD"], 1)

        @block.tensor
        def _(pe):
            mm = nc.tensor.matmul

            pe.wait_ge(s["cst"], 32)
            for t in range(NT):
                pe.wait_ge(s["hk"], t + 1)
                for k in range(KD):
                    c = (k % 2) * TOK + t * P
                    last = nc.tensor.transpose(bank[4 + k // 2][:, c:c + P], hk[:, t, k, :], ident)
                    if t == NT - 1 and k % 2:
                        last.then_inc(s["tr1"], 1)

            def three(dst, a_hi, a_lo, b_hi, b_lo, first, last):
                mm(dst, a_hi, b_hi, start=first, stop=False)
                mm(dst, a_hi, b_lo, start=False, stop=False)
                return mm(dst, a_lo, b_hi, start=False, stop=last)


            def project(i, t, ks):
                u, col, kind, to, scale = blocks[i]
                hi, lo = high[u % 2], low[u % RING1]
                dst = bank[i % 8]
                for k in ks:
                    pe.wait_ge(s["hTl"], k // 2 + 1)
                    pe.wait_ge(s["low"], split_count(u, k))
                    go = (k == 0, k == KD - 1)
                    if kind == "T":
                        c = slice(col, col + P)
                        last = three(dst[:, 0:TOK], hi[:, k, c], lo[:, k, c], hT_hi[:, k, :], hT_lo[:, k, :], *go)
                    else:
                        rows = slice(t * P, (t + 1) * P)
                        to_cols = rows if kind == "W" else slice(0, TOK)
                        c = slice(col, col + (P if kind == "W" else TOK))
                        last = three(dst[:, to_cols], hT_hi[:, k, rows], hT_lo[:, k, rows], hi[:, k, c], lo[:, k, c], *go)
                return last

            for quarter in range(4):
                for i in range(ends[0]):
                    last = project(i, None, range(2 * quarter, 2 * quarter + 2))
                    if quarter == 3:
                        last.then_inc(s["proj"], 1)
            pe.wait_ge(s["small"], 16 * 9)
            mm(bank[7][0:12, 0:MAP], relb[:], onehot[:], start=True, stop=True).then_inc(s["table"], 1)
            for i in range(ends[0], len(blocks)):
                kind, to = blocks[i][2:4]
                if i == 7:
                    pe.wait_ge(s["dvec"], 1)
                if i >= 8:
                    pe.wait_ge((s["projA"], s["projD"])[i % 2], (i - 8) // 2 + 1)
                for t in range(NT) if kind == "W" else [to[1] if kind == "V" else None]:
                    last = project(i, t, range(KD))
                last.then_inc(s["proj"], 1)

            nb = len(blocks)
            for b in (0, 4):
                i = max(i for i in range(nb) if i % 8 == b)
                pe.wait_ge((s["projA"], s["projD"])[i % 2], i // 2 + 1)

            def qk_rows(b, h):
                half = slice((h % 2) * HD, (h % 2) * HD + HD)
                if b == A_:
                    return [(QK["Aq"] + h // 2, QK["Ak"] + h // 2, half)]
                if b == B_:
                    rows = slice(32 * h, 32 * h + 32)
                    return [(QK["Bq1"], QK["Bk1"], rows), (QK["Bq2"], QK["Bk2"], rows)]
                if b == C_BR:
                    return [(QK["Cq"] + h // 2, QK["Ck"] + h // 2, half)]
                return [(QK["Dq"] + h % 2, QK["Dk"], slice((h // 2) * HD, (h // 2) * HD + HD))]

            def scores(st):
                b, h = divmod(st, 4)
                if st >= 1:
                    pe.wait_ge(s["sread"], st)
                maps = qk_rows(b, h)
                for i, (qb, kb, r) in enumerate(maps):
                    dst = bank[i if b == B_ else st % 2]
                    if b == C_BR:
                        mm(dst[:, 0:TOK], qk[r, kb, 0:P], qk[r, qb, :], start=True, stop=True)
                        last = mm(dst[:, TOK:MAP], qk[r, kb, P:TOK], qk[r, qb, P:TOK], start=True, stop=True)
                    else:
                        mm(dst[:, 0:P], qk[r, qb, 0:P], qk[r, kb, 0:P], start=True, stop=True)
                        last = mm(dst[:, P:MAP], qk[r, qb, P:TOK], qk[r, kb, :], start=True, stop=True)
                last.then_inc(s["scores"], 1)

            def gate_half(st, half):
                b, h = divmod(st, 4)
                n, t = divmod(h, 2)
                xi = split.index(("gate", b, n))
                hi, lo = high[xi % 2], low[where[split[xi]] % RING1]
                pe.wait_ge(s["low"], split_count(xi, 4 * half))
                if half == 0 and st >= 2:
                    pe.wait_ge(s["tanh"], st - 1)
                rows = slice(t * P, (t + 1) * P)
                for k in range(4 * half, 4 * half + 4):
                    last = three(bank[4 + st % 2][:], hT_hi[:, k, rows], hT_lo[:, k, rows], hi[:, k, :], lo[:, k, :],
                                 k == 0, k == KD - 1)
                if half:
                    last.then_inc(s["gate"], 1)

            def middle(st):
                pe.wait_ge(s["probs"], st + 1)
                if st >= 1:
                    pe.wait_ge(s["pt"], st)
                if st // 4 == C_BR:
                    mm(bank[2][:, 0:MAP], at_or_after, prob[st % 2][:, 1, :], start=True, stop=False, skip_group_check=True)
                    last = mm(bank[2][:, P:TOK], ones, prob[st % 2][:, 1, TOK:MAP], start=False, stop=True,
                              skip_group_check=True)
                else:
                    for c in range(3):
                        last = nc.tensor.transpose(bank[2][:, c * P:(c + 1) * P], prob[st % 2][:, 0, c * P:(c + 1) * P],
                                                   ident)
                last.then_inc(s["ptps"], 1)

            def values(st):
                b, h = divmod(st, 4)
                pe.wait_ge(s["pt"], st + 1)
                if st >= 1:
                    pe.wait_ge(s["oev"], st)
                c = V_AT[b] + (h if b != D_ else h // 2) * HD
                mm(bank[3][:, 0:HD], pT[:, 0:P], vv[:, 0, c:c + HD], start=True, stop=True)
                mm(bank[3][:, HD:2 * HD], pT[:, P:TOK], vv[:, 0, c:c + HD], start=True, stop=False)
                mm(bank[3][:, HD:2 * HD], pT[:, TOK:MAP], vv[:, 1, c:c + HD], start=False, stop=True).then_inc(s["pv"], 1)

            def turn(b, halves=range(2)):
                if b == B_:
                    pe.wait_ge(s["ob"], 1)
                pe.wait_ge(s["oev"], 4 * b + 2 * halves[-1] + 2)
                if b == D_:
                    pe.wait_ge(s["sread"], 16)
                elif b >= 1:
                    pe.wait_ge(s["mrg"], 4 * b)
                for c in halves:
                    for t in range(NT):
                        last = nc.tensor.transpose(turned_part(b, c)[:, t * P:(t + 1) * P], o[:, t, c * P:(c + 1) * P], ident)
                last.then_inc(s["oTps"], 1)

            def branch(b, j, halves=range(2)):
                n, t = divmod(LAST_ORDER[j] if b == D_ else j, 2)
                u, w, hi, lo = branch_parts(b)
                pe.wait_ge(s["brl"], b + 1)
                pe.wait_ge(s["oTs"], halves_turned(b, halves[-1]))
                if b == D_ and j >= 2:
                    pe.wait_ge((s["pt"], s["oev"])[j % 2], 16)
                elif 4 * b + j >= 2:
                    pe.wait_ge(s["mrg"], 4 * b + j - 1)
                rows, cols = slice(t * P, (t + 1) * P), slice(n * BANK, (n + 1) * BANK)
                for c in halves:
                    last = three(branch_bank(b, j)[:], oT_hi[:, c, rows], oT_lo[:, c, rows], hi[:, c, cols], lo[:, c, cols],
                                 c == 0, c == 1)
                if c == 1:
                    last.then_inc(s["br"], 1)

            scores(0)
            for st in range(16):
                b, h = divmod(st, 4)
                gate_half(st, 0)
                if st < 15:
                    scores(st + 1)
                else:
                    turn(D_, [0])
                if st == 0:
                    pe.wait_ge(s["projA"], (nb + 1) // 2)
                    pe.wait_ge(s["projD"], nb // 2)
                middle(st)
                if b in (B_, D_) and h == 0:
                    turn(b - 1)
                gate_half(st, 1)
                if b == C_BR and h == 0:
                    turn(1)
                values(st)
                if b >= 1 and st < 15:
                    branch(b - 1, h)
                if st == 14:
                    branch(b - 1, 3)
            branch(D_, 0, [0])
            turn(D_, [1])
            branch(D_, 1, [0])

            def turn_tile(t, rows, done):
                for i in range(2):
                    for kk in range(4):
                        k_th = rows[:, t, :].rearrange("p (q k) -> p k q", k=KD)[:, 4 * i + kk, :]
                        last = nc.tensor.transpose(bank[2 * t + i][:, kk * P:(kk + 1) * P], k_th, ident)
                    last.then_inc(done, 1)

            def out_product(t, n, ks=range(KD)):
                xi = split.index(("wo", n, 0))
                hi, lo = high[xi % 2], low[where[split[xi]] % RING1]
                rows = slice(t * P, (t + 1) * P)
                for k in ks:
                    pe.wait_ge(s["mTl"], 2 * t + k // 4 + 1)
                    pe.wait_ge(s["low"], split_count(xi, k))
                    last = three(bank[4 + 2 * t + n][:], hT_hi[:, k, rows], hT_lo[:, k, rows], hi[:, k, :], lo[:, k, :],
                                 k == 0, k == KD - 1)
                if ks[-1] == KD - 1:
                    last.then_inc(s["wo"], 1)

            def route(t, ks=range(KD)):
                for k in ks:
                    pe.wait_ge(s["h2T"], 2 * t + k // 4 + 1)
                    last = mm(bank[4 + t][:, 0:NG + NE], h2T[:, k, t * P:(t + 1) * P], wr[:, k, :],
                              start=(k == 0), stop=(k == KD - 1))
                if ks[-1] == KD - 1:
                    last.then_inc(s["lg_ps"], 1)

            branch(D_, 0, [1])
            branch(D_, 1, [1])
            branch(D_, 2)
            pe.wait_ge(s["mrg"], 14)
            turn_tile(0, merged, s["mTps"])
            branch(3, 3)
            pe.wait_ge(s["tanh"], 16)
            out_product(0, 0)
            pe.wait_ge(s["mrg"], 16)
            turn_tile(1, merged, s["mTps"])
            out_product(1, 0)
            out_product(0, 1)
            out_product(1, 1, range(4))
            pe.wait_ge(s["x1"], 1)
            turn_tile(0, x, s["h2ps"])
            out_product(1, 1, range(4, KD))
            route(0, range(4))
            pe.wait_ge(s["x1"], 2)
            turn_tile(1, x, s["h2ps"])
            route(0, range(4, KD))
            route(1)
            pe.wait_ge(s["asg"], 1)
            pe.wait_ge(s["bf"], 2)
            mm(bank[5][:, 0:NE], before_bf[:], asg[:, 0, :], start=True, stop=True)
            mm(bank[5][:, NE:2 * NE], ones_bf[:], asg[:, 0, :], start=True, stop=False)
            mm(bank[5][:, NE:2 * NE], before_bf[:], asg[:, 1, :], start=False, stop=True)
            mm(bank[5][:, 2 * NE:3 * NE], ones_bf[:], asg[:, 0, :], start=True, stop=False)
            mm(bank[5][:, 2 * NE:3 * NE], ones_bf[:], asg[:, 1, :], start=False, stop=True).then_inc(s["pos"], 1)
            pe.wait_ge(s["hkl"], 2 * NT)

            def gather(z, p, first=False):
                pe.wait_ge(z["P"], p + 1)
                if not first:
                    pe.wait_ge(z["y0"], p - 1)
                    pe.wait_ge(z["y1"], p - 1)
                for half in range(2):
                    for k in range(4 * half, 4 * half + 4):
                        c = (k % 4) * P
                        for t in range(NT):
                            for i, part in enumerate((hk_1, hk_2, hk_3)):
                                last = mm(bank[6 + half][:, c:c + P], part[:, t, k, :], pick[:, t, :],
                                          start=(t == 0 and i == 0), stop=(t == NT - 1 and i == 2))
                    last.then_inc(z["gat"], 1)

            def up(w, z, p, slots, here, first=False):
                if not first:
                    pe.wait_ge((z["hT"], z["ST"])[w], p)
                for k in range(KD):
                    if k % 4 == 0:
                        pe.wait_ge(z["xT"], 2 * p + 1 + k // 4)
                    here(2 * w, k)
                    for g in range(2):
                        rhs = units[slots[2 * w + g]][:].rearrange("p (k n) -> p k n", k=KD)[:, k, :]
                        last = mm(bank[4 + w][g * CAP:(g + 1) * CAP, :], xT[:, k, g * CAP:(g + 1) * CAP], rhs,
                                  start=(k == 0), stop=(k == KD - 1))
                    if k == 3 and w == 0 and z is main and first:
                        last.then_inc(s["half_up"], 1)
                last.then_inc((z["A"], z["B"])[w], 1)

            def turn_hidden(z, p):
                pe.wait_ge(z["hid"], p + 1)
                for c in range(CE):
                    last = nc.tensor.transpose(bank[4][:, c * P:(c + 1) * P], hid[:, c, :], ident)
                last.then_inc(z["hTp"], 1)

            def turn_picks(z, p):
                pe.wait_ge(z["Pw"], p + 1)
                for t in range(NT):
                    last = nc.tensor.transpose(bank[5][:, t * P:(t + 1) * P], pickw[:, t, :], ident)
                last.then_inc(z["STp"], 1)

            def down(z, p, slots, here):
                pe.wait_ge(z["hT"], p + 1)
                for n in range(2):
                    for c in range(CE):
                        here(4, CE * n + c)
                        for g in range(2):
                            rhs = units[slots[4 + g]][:].rearrange("p (c n) -> p c n", c=CE)
                            last = mm(bank[6 + n][g * CAP:(g + 1) * CAP, :], hidT[:, c, g * CAP:(g + 1) * CAP],
                                      rhs[:, c, n * BANK:(n + 1) * BANK], start=(c == 0), stop=(c == CE - 1))
                    last.then_inc(z["Y"], 1)

            def combine(z, p, start=False, stop=False, halves=range(2)):
                pe.wait_ge(z["ST"], p + 1)
                for n in halves:
                    pe.wait_ge((z["y0"], z["y1"])[n], p + 1)
                    for t in range(NT):
                        last = mm(bank[2 * t + n][:], pickT[:, t, :], y[:, n * BANK:(n + 1) * BANK],
                                  start=start, stop=stop, skip_group_check=True)
                        if stop:
                            last.then_inc(s["total"], 1)
                if not stop and n == 1:
                    last.then_inc(z["comb"], 1)

            def experts(p, base, i=0, first=False, last=False, start=False):
                n0 = base * PAIR_UNITS
                slots = [slot_of(n0 + r) for r in range(PAIR_UNITS)]

                def here(r, step):
                    if last:
                        for piece, (matrix, n_half, k0, k1) in enumerate(LAST_PIECES):
                            if r == matrix and step == CE * n_half + k0:
                                pe.wait_ge(s_last[piece], 32)
                    elif step == 0:
                        for q in (r, r + 1):
                            pe.wait_ge(s_unit[slots[q]], unit_value(n0 + q, i))
                        if n0 + r == RING:
                            pe.wait_ge(s["early"], 32)

                up(0, main, p, slots, here, first)
                if not first:
                    combine(main, p - 1, start=start, halves=range(1 if last else 2))
                up(1, main, p, slots, here, first)
                if not last:
                    gather(main, p + 1, first=first)
                turn_hidden(main, p)
                if last:
                    combine(main, p - 1, halves=[1])
                turn_picks(main, p)
                if not last:
                    pe.wait_ge(main["xT"], 2 * p + 4)
                down(main, p, slots, here)

            gather(main, 0, first=True)
            pe.wait_ge(s["flag"], 1)
            experts(0, 0, first=True)
            experts(1, 1, start=True)
            with pe.Fori(0, LOOPS) as i:
                for j in range(STEP):
                    experts(i * STEP + PEEL + j, PEEL + j, i)
            for p in range(PEEL + LOOPS * STEP, PAIRS):
                experts(p, p, last=(p == PAIRS - 1))
            combine(main, PAIRS - 1, stop=True)

            crowded = pe.value_load(flag[0:1, 0:1])
            with pe.If(crowded > CAP):
                pe.wait_ge(s["total"], 4)
                pe.nop().then_inc(over["comb"], 1)
                with pe.Fori(0, BLOCKS - 1) as b:
                    with pe.Fori(0, PAIRS) as p:
                        q = b * PAIRS + p
                        slots = list(range(PAIR_UNITS))

                        def here(r, step):
                            for w in (r, r + 1) if step == 0 else ():
                                pe.wait_ge(s_over_unit[w], 16 * q + 16)

                        gather(over, q, first=True)
                        for w in range(2):
                            up(w, over, q, slots, here, first=True)
                        turn_hidden(over, q)
                        turn_picks(over, q)
                        down(over, q, slots, here)
                        combine(over, q)


_INS = ["x", "rel_bias", "g_mix", "w_in", "diff_lq1", "diff_lk1", "diff_lq2", "diff_lk2", "diff_subln", "swa_sinks",
        "w_gate", "w_br", "w_o", "g_ffn", "w_route_group", "b_route_group", "w_route_expert", "b_route_expert",
        "w1", "w3", "w2", "g_final"]


def _constants():
    import math
    import numpy as np

    j = np.arange(P)
    c = np.zeros((P, C_W), np.float32)
    c[:, C_ID:C_ID + P] = np.eye(P)
    c[:, C_GE:C_GE + P] = j[:, None] >= j[None, :]
    c[:, C_ONE:C_ONE + P] = 1.0
    c[:, C_SLOT:C_SLOT + CAP] = np.arange(CAP)
    c[:, C_IOTA:C_IOTA + NE] = NE - np.arange(NE)
    diag = np.where(j[:, None] < j[None, :], 0.0, -NEG)
    c[:, C_DIAG:C_DIAG + P] = diag
    c[:, C_DIAG + 2 * P:C_DIAG + 3 * P] = diag
    dist = np.arange(MAP) - (P - 1)
    n = np.maximum(dist, 0)
    large = 16 + (np.log(np.maximum(n, 1) / 16) / math.log(128 / 16) * 16).astype(np.int32)
    bucket = np.where(n < 16, n, np.minimum(large, 31))
    onehot = np.zeros((32, MAP), np.float32)
    seen = (dist >= 0) & (dist < TOK)
    onehot[bucket[seen], np.nonzero(seen)[0]] = -1.0
    mask = np.zeros((12, MAP), np.float32)
    mask[:, dist < 0] = NEG
    mask[8:, dist >= 128] = NEG
    return {"constants": c, "bucket_onehot": onehot, "bias_mask": mask}


def kernel(**inputs):
    import numpy as np
    import concourse.bacc as bacc
    from concourse.bass_utils import run_bass_kernel_spmd

    nc = bacc.Bacc("TRN2", target_bir_lowering=False, num_devices=1)
    arrays, args = {}, {}
    for name, value in list(inputs.items()) + list(_constants().items()):
        v = np.ascontiguousarray(value)
        arrays[f"in_{name}"] = v
        args[name] = nc.dram_tensor(f"in_{name}", v.shape, mybir.dt.from_np(v.dtype), kind="ExternalInput").ap()
    out = nc.dram_tensor("out", (1, TOK, D), F32, kind="ExternalOutput").ap()
    hybrid_decoder_layer(nc, args, out)
    return run_bass_kernel_spmd(nc, [arrays], core_ids=[0]).results[0]["out"]
```
